# Optimizing a Trainium2 kernel written in Bass

```python
import jax, jax.numpy as jnp
from jax import lax
import numpy as np
import math

D_MODEL = 1024
BATCH = 1
SEQ = 512
DEPTH = 1

MIX_W = 1024
CONV_K = 3
CONV_GROUPS = 8
N_HEADS = 16
HEAD_DIM = 64
N_KV = 4
HPG = N_HEADS // N_KV
KV_W = N_KV * HEAD_DIM
L_CMP = 32
STRIDE_CMP = 16
CMP_HIDDEN = 128
L_SEL = 64
N_SEL_BLOCKS = 16
WINDOW = 512
Q_BLOCK = 16
CHUNK = 128
GM_GROUPS = 8
GM_GW = MIX_W // GM_GROUPS
N_BRANCH = 3
EPS = 1e-6
NEG = -1e30

A_OFF = 0
A_COLS = 4 * MIX_W
B_OFF = A_OFF + A_COLS
B_COLS = 2 * MIX_W + 6 * KV_W + 3 * N_HEADS
C_OFF = B_OFF + B_COLS
C_COLS = 3 * MIX_W
G_OFF = C_OFF + C_COLS
G_COLS = N_BRANCH * D_MODEL
IN_COLS = G_OFF + G_COLS


def rmsnorm(x, g):
    x32 = x.astype(jnp.float32)
    y = x32 * lax.rsqrt(jnp.mean(x32 * x32, axis=-1, keepdims=True) + EPS)
    return y.astype(x.dtype) * g

def layernorm(x, g, b):
    x32 = x.astype(jnp.float32)
    mu = jnp.mean(x32, axis=-1, keepdims=True)
    xc = x32 - mu
    y = xc * lax.rsqrt(jnp.mean(xc * xc, axis=-1, keepdims=True) + EPS)
    return y.astype(x.dtype) * g + b

def masked_softmax(s, mask):
    p = jax.nn.softmax(jnp.where(mask, s, NEG), axis=-1)
    return jnp.where(mask, p, 0.0)

def alibi_slopes():
    i = jnp.arange(1, N_HEADS + 1, dtype=jnp.float32)
    return (2.0 ** (-8.0 * i / N_HEADS)).reshape(N_KV, HPG)

def short_conv_mixer(h, w_in_a, conv_w, conv_b):
    S = h.shape[1]
    b, cg, xin, z = jnp.split(h @ w_in_a, 4, axis=-1)
    y = cg * xin
    yp = jnp.pad(y, ((0, 0), (CONV_K - 1, 0), (0, 0)))
    conv = conv_b + sum(conv_w[k] * yp[:, k:k + S] for k in range(CONV_K))
    return b * conv * jax.nn.silu(z)

def nsa_mixer(h, w_in_b, pos_ck, w_ck1, w_ck2, pos_cv, w_cv1, w_cv2):
    Bsz, S, _ = h.shape
    sizes = [MIX_W] + [KV_W] * 6 + [MIX_W]
    q, kc, vc, ks, vs, kw, vw, z, gl = jnp.split(h @ w_in_b, np.cumsum(sizes).tolist(), axis=-1)

    def heads_kv(t):
        return t.reshape(Bsz, S, N_KV, HEAD_DIM).transpose(0, 2, 1, 3)

    n_cmp = (S - L_CMP) // STRIDE_CMP + 1
    cmp_start = jnp.arange(n_cmp) * STRIDE_CMP
    cmp_end = cmp_start + (L_CMP - 1)
    cmp_idx = cmp_start[:, None] + jnp.arange(L_CMP)[None, :]

    def compress(t, pos, w1, w2):
        blocks = heads_kv(t)[:, :, cmp_idx] + pos
        flat = blocks.reshape(Bsz, N_KV, n_cmp, L_CMP * HEAD_DIM)
        return jax.nn.silu(flat @ w1) @ w2

    k_cmp = compress(kc, pos_ck, w_ck1, w_ck2)
    v_cmp = compress(vc, pos_cv, w_cv1, w_cv2)

    n_sel = S // L_SEL
    k_top = min(N_SEL_BLOCKS, n_sel)
    k_blk = heads_kv(ks).reshape(Bsz, N_KV, n_sel, L_SEL, HEAD_DIM)
    v_blk = heads_kv(vs).reshape(Bsz, N_KV, n_sel, L_SEL, HEAD_DIM)
    sel_ids = jnp.arange(n_sel)
    overlap = ((cmp_start[:, None] <= (sel_ids[None, :] + 1) * L_SEL - 1)
               & (cmp_end[:, None] >= sel_ids[None, :] * L_SEL)).astype(jnp.float32)

    pad = ((0, 0), (0, 0), (WINDOW - 1, 0), (0, 0))
    k_win = jnp.pad(heads_kv(kw), pad)
    v_win = jnp.pad(heads_kv(vw), pad)
    span = Q_BLOCK + WINDOW - 1

    nq = S // Q_BLOCK
    qh = q.reshape(Bsz, nq, Q_BLOCK, N_KV, HPG, HEAD_DIM).transpose(1, 0, 3, 4, 2, 5)
    gh = gl.reshape(Bsz, nq, Q_BLOCK, N_KV, HPG, 3).transpose(1, 0, 3, 4, 2, 5)
    slopes = alibi_slopes()
    scale = HEAD_DIM ** -0.5
    bi = jnp.arange(Bsz)[:, None, None, None]
    gi = jnp.arange(N_KV)[None, :, None, None]

    def block_fn(args):
        ci, qb, gb = args
        t0 = ci * Q_BLOCK
        tq = t0 + jnp.arange(Q_BLOCK)
        d_c = tq[:, None] - cmp_end[None, :]
        s = jnp.einsum('bgnqd,bgkd->bgnqk', qb, k_cmp).astype(jnp.float32) * scale \
            - slopes[:, :, None, None] * d_c.astype(jnp.float32)
        p_cmp = masked_softmax(s, d_c >= 0)
        o_cmp = jnp.einsum('bgnqk,bgkd->bgnqd', p_cmp.astype(v_cmp.dtype), v_cmp)
        imp = jnp.einsum('bgnqk,ks->bgqs', p_cmp, overlap)
        cur = tq // L_SEL
        valid = sel_ids[None, :] * L_SEL <= tq[:, None]
        forced = (sel_ids[None, :] == 0) | (sel_ids[None, :] == cur[:, None]) | (sel_ids[None, :] == cur[:, None] - 1)
        score = jnp.where(forced, jnp.inf, jnp.where(valid, imp, -jnp.inf))
        _, sel = lax.top_k(score, k_top)
        kg = k_blk[bi, gi, sel]
        vg = v_blk[bi, gi, sel]
        spos = sel[..., None] * L_SEL + jnp.arange(L_SEL)
        d_s = (tq[None, None, :, None, None] - spos)[:, :, None]
        s = jnp.einsum('bgnqd,bgqkld->bgnqkl', qb, kg).astype(jnp.float32) * scale \
            - slopes[:, :, None, None, None] * d_s.astype(jnp.float32)
        m = jnp.broadcast_to(d_s >= 0, s.shape)
        flat_shape = (Bsz, N_KV, HPG, Q_BLOCK, k_top * L_SEL)
        p = masked_softmax(s.reshape(flat_shape), m.reshape(flat_shape))
        o_slc = jnp.einsum('bgnqm,bgqmd->bgnqd', p.astype(vg.dtype),
                           vg.reshape(Bsz, N_KV, Q_BLOCK, k_top * L_SEL, HEAD_DIM))
        kwb = lax.dynamic_slice_in_dim(k_win, t0, span, axis=2)
        vwb = lax.dynamic_slice_in_dim(v_win, t0, span, axis=2)
        kpos = t0 - (WINDOW - 1) + jnp.arange(span)
        d_w = tq[:, None] - kpos[None, :]
        m_w = (d_w >= 0) & (d_w < WINDOW) & (kpos[None, :] >= 0)
        s = jnp.einsum('bgnqd,bgkd->bgnqk', qb, kwb).astype(jnp.float32) * scale \
            - slopes[:, :, None, None] * d_w.astype(jnp.float32)
        p = masked_softmax(s, m_w)
        o_win = jnp.einsum('bgnqk,bgkd->bgnqd', p.astype(vwb.dtype), vwb)
        g = jax.nn.sigmoid(gb)
        return g[..., 0:1] * o_cmp + g[..., 1:2] * o_slc + g[..., 2:3] * o_win

    o = lax.map(block_fn, (jnp.arange(nq), qh, gh))
    o = o.transpose(1, 0, 4, 2, 3, 5).reshape(Bsz, S, MIX_W)
    return o * jax.nn.silu(z)

def gmlp_mixer(h, w_in_c, ln_g, ln_b, w_s, b_s):
    Bsz, S, _ = h.shape
    u, v, z = jnp.split(h @ w_in_c, 3, axis=-1)
    u = jax.nn.gelu(u)
    v = layernorm(jax.nn.gelu(v), ln_g, ln_b)
    vr = v.reshape(Bsz, S // CHUNK, CHUNK, GM_GROUPS, GM_GW)
    tril = jnp.tril(jnp.ones((CHUNK, CHUNK), dtype=bool))
    wm = jnp.where(tril, w_s, 0.0)
    sp = jnp.einsum('gij,bnjgc->bnigc', wm, vr) + b_s.T[:, :, None]
    return u * sp.reshape(Bsz, S, MIX_W) * jax.nn.silu(z)

def hybrid_layer(x, c, g_pre, g_post, w_ada, b_ada, w_in, conv_w, conv_b, pos_ck, w_ck1, w_ck2,
                 pos_cv, w_cv1, w_cv2, ln_g, ln_b, w_s, b_s, w_br, w_out):
    shift, scl, gate = jnp.split(jax.nn.silu(c) @ w_ada + b_ada, 3, axis=-1)
    h = rmsnorm(x, g_pre) * (1.0 + scl[:, None]) + shift[:, None]
    ys = (
        short_conv_mixer(h, w_in[:, A_OFF:A_OFF + A_COLS], conv_w, conv_b),
        nsa_mixer(h, w_in[:, B_OFF:B_OFF + B_COLS], pos_ck, w_ck1, w_ck2, pos_cv, w_cv1, w_cv2),
        gmlp_mixer(h, w_in[:, C_OFF:C_OFF + C_COLS], ln_g, ln_b, w_s, b_s),
    )
    merged = None
    for i in range(N_BRANCH):
        g_i = jax.nn.sigmoid(h @ w_in[:, G_OFF + i * D_MODEL:G_OFF + (i + 1) * D_MODEL])
        term = g_i * (ys[i] @ w_br[i])
        merged = term if merged is None else merged + term
    out = rmsnorm(merged @ w_out, g_post)
    return x + gate[:, None] * out

def first_inputs(seed: int = 0) -> dict:
    key = jax.random.key(seed)
    k = jax.random.split(key, 24)
    nrm = jax.random.normal
    f = jnp.float32
    return {
        "x": nrm(k[0], (BATCH, SEQ, D_MODEL), f),
        "c": nrm(k[1], (BATCH, D_MODEL), f),
        "g_pre": 1.0 + 0.02 * nrm(k[2], (DEPTH, D_MODEL), f),
        "g_post": 1.0 + 0.02 * nrm(k[3], (DEPTH, D_MODEL), f),
        "w_ada": 0.5 * D_MODEL ** -0.5 * nrm(k[4], (DEPTH, D_MODEL, 3 * D_MODEL), f),
        "b_ada": 0.02 * nrm(k[5], (DEPTH, 3 * D_MODEL), f),
        "w_in": D_MODEL ** -0.5 * nrm(k[6], (DEPTH, D_MODEL, IN_COLS), f),
        "conv_w": CONV_K ** -0.5 * nrm(k[7], (DEPTH, CONV_K, MIX_W), f),
        "conv_b": 0.02 * nrm(k[8], (DEPTH, MIX_W), f),
        "pos_ck": 0.02 * nrm(k[9], (DEPTH, L_CMP, HEAD_DIM), f),
        "w_ck1": (L_CMP * HEAD_DIM) ** -0.5 * nrm(k[10], (DEPTH, L_CMP * HEAD_DIM, CMP_HIDDEN), f),
        "w_ck2": CMP_HIDDEN ** -0.5 * nrm(k[11], (DEPTH, CMP_HIDDEN, HEAD_DIM), f),
        "pos_cv": 0.02 * nrm(k[12], (DEPTH, L_CMP, HEAD_DIM), f),
        "w_cv1": (L_CMP * HEAD_DIM) ** -0.5 * nrm(k[13], (DEPTH, L_CMP * HEAD_DIM, CMP_HIDDEN), f),
        "w_cv2": CMP_HIDDEN ** -0.5 * nrm(k[14], (DEPTH, CMP_HIDDEN, HEAD_DIM), f),
        "ln_g": 1.0 + 0.02 * nrm(k[15], (DEPTH, MIX_W), f),
        "ln_b": 0.02 * nrm(k[16], (DEPTH, MIX_W), f),
        "w_s": CHUNK ** -0.5 * nrm(k[17], (DEPTH, GM_GROUPS, CHUNK, CHUNK), f),
        "b_s": 1.0 + 0.02 * nrm(k[18], (DEPTH, GM_GROUPS, CHUNK), f),
        "w_br": MIX_W ** -0.5 * nrm(k[19], (DEPTH, N_BRANCH, MIX_W, D_MODEL), f),
        "w_out": D_MODEL ** -0.5 * nrm(k[20], (DEPTH, D_MODEL, D_MODEL), f),
    }

def first_block(x, c, g_pre, g_post, w_ada, b_ada, w_in, conv_w, conv_b, pos_ck, w_ck1, w_ck2,
              pos_cv, w_cv1, w_cv2, ln_g, ln_b, w_s, b_s, w_br, w_out):
    for l in range(DEPTH):
        x = hybrid_layer(x, c, g_pre[l], g_post[l], w_ada[l], b_ada[l], w_in[l], conv_w[l], conv_b[l],
                         pos_ck[l], w_ck1[l], w_ck2[l], pos_cv[l], w_cv1[l], w_cv2[l],
                         ln_g[l], ln_b[l], w_s[l], b_s[l], w_br[l], w_out[l])
    return x


_first_inputs = first_inputs


def first_inputs(seed=0):
    import zlib

    import numpy as np

    out = dict(_first_inputs(seed))
    spreads = {}
    factors = {'g_pre': 5.22,
     'g_post': 24.252,
     'conv_b': 64.0,
     'pos_ck': 64.0,
     'w_ck1': 28.755,
     'w_ck2': 27.98,
     'pos_cv': 64.0,
     'ln_g': 64.0,
     'ln_b': 64.0,
     'b_s': 64.0,
     'w_cv1': 4.757,
     'w_cv2': 4.267}
    for name, (base, spread) in spreads.items():
        noise = np.random.default_rng([zlib.crc32(name.encode()), seed]).standard_normal(out[name].shape)
        drawn = base * np.exp(spread * noise) if base else spread * noise
        out[name] = __import__('jax').numpy.asarray(drawn.astype(out[name].dtype))
    for name, factor in factors.items():
        out[name] = (out[name] * factor).astype(out[name].dtype)
    return out


_narrow_inputs = first_inputs


def first_inputs(seed=0):

    out = dict(_narrow_inputs(seed))
    wider = {'g_post': 3.18, 'conv_b': 3.31, 'ln_g': 6.88, 'ln_b': 6.47, 'b_s': 4.7}
    for name, times in wider.items():
        mean = out[name].mean()
        out[name] = (mean + times * (out[name] - mean)).astype(out[name].dtype)
    return out


N_META = 16
BLOCK_Q = 128
SB_HEADS = 4
SP_HEADS = 4
IDX_HEADS = 8
IDX_DIM = 32
TOPK_MAX = 256
DF_HEADS = 4
N_BUCKETS = 32
MAX_DISTANCE = 128
N_BIAS_HEADS = SP_HEADS + DF_HEADS
D_FF = 2816
CONV_WIDTH = 3
NEG_INF = -1e30

SB_W = SB_HEADS * HEAD_DIM
SP_W = SP_HEADS * HEAD_DIM
DF_W = DF_HEADS * 2 * HEAD_DIM
SPLITS = (SB_W, SB_W, SB_W,
          SP_W, SP_W, SP_W,
          IDX_HEADS * IDX_DIM, IDX_DIM, IDX_HEADS,
          DF_W, DF_W, DF_W,
          D_MODEL, D_MODEL, D_MODEL)
D_IN = sum(SPLITS)


def _rmsnorm(a, gain):
    af = a.astype(jnp.float32)
    af = af * lax.rsqrt(jnp.mean(af * af, axis=-1, keepdims=True) + EPS)
    return (af * gain.astype(jnp.float32)).astype(a.dtype)

def _split_cols(z):
    out, off = [], 0
    for w in SPLITS:
        out.append(z[..., off:off + w])
        off += w
    return out

def _to_blocks(a):
    b, tp = a.shape[:2]
    return jnp.moveaxis(a.reshape((b, tp // BLOCK_Q, BLOCK_Q) + a.shape[2:]), 1, 0)

def _from_blocks(a):
    nb, b = a.shape[:2]
    return jnp.moveaxis(a, 0, 1).reshape((b, nb * BLOCK_Q) + a.shape[3:])

def _t5_bucket(rel):
    n = jnp.maximum(rel, 0)
    max_exact = N_BUCKETS // 2
    nf = jnp.maximum(n, 1).astype(jnp.float32)
    large = max_exact + (jnp.log(nf / max_exact) / math.log(MAX_DISTANCE / max_exact)
                         * (N_BUCKETS - max_exact)).astype(jnp.int32)
    return jnp.where(n < max_exact, n, jnp.minimum(large, N_BUCKETS - 1))

def _stick_breaking(q, k, v):
    tp, dh = q.shape[1], q.shape[-1]
    scale = dh ** -0.5
    kf, vf = k.astype(jnp.float32), v.astype(jnp.float32)
    key_pos = jnp.arange(tp)

    def block(args):
        qb, start = args
        qpos = start + jnp.arange(BLOCK_Q)
        z = jnp.einsum('bqhd,bkhd->bhqk', qb.astype(jnp.float32), kf) * scale
        mask = key_pos[None, :] < qpos[:, None]
        log_1m_beta = jnp.where(mask, jax.nn.log_sigmoid(-z), 0.0)
        between = lax.cumsum(log_1m_beta, axis=3, reverse=True) - log_1m_beta
        w = jnp.where(mask, jnp.exp(jax.nn.log_sigmoid(z) + between), 0.0)
        return jnp.einsum('bhqk,bkhd->bqhd', w, vf)

    nb = tp // BLOCK_Q
    out = lax.map(block, (_to_blocks(q), jnp.arange(nb) * BLOCK_Q))
    return _from_blocks(out).astype(v.dtype)

def _indexed_sparse_attention(q, k, v, q_ix, k_ix, w_ix, bias_table, top_k):
    tp, h, dh = q.shape[1], q.shape[2], q.shape[3]
    scale = dh ** -0.5
    k_ixf = k_ix.astype(jnp.float32)
    key_pos = jnp.arange(tp)
    table = bias_table.astype(jnp.float32)

    def block(args):
        qb, qib, wb, start = args
        qpos = start + jnp.arange(BLOCK_Q)
        dots = jnp.einsum('bqjd,bkd->bqjk', qib.astype(jnp.float32), k_ixf)
        score = jnp.einsum('bqj,bqjk->bqk', wb.astype(jnp.float32), jax.nn.relu(dots))
        score = jnp.where((key_pos[None, :] <= qpos[:, None])[None], score, NEG_INF)
        _, sel = lax.top_k(score, top_k)
        rel = qpos[None, :, None] - sel
        valid = rel >= 0
        k_sel = jax.vmap(lambda kk, ii: kk[ii])(k, sel)
        v_sel = jax.vmap(lambda vv, ii: vv[ii])(v, sel)
        s = jnp.einsum('bqhd,bqkhd->bhqk', qb.astype(jnp.float32),
                       k_sel.astype(jnp.float32)) * scale
        s = s + jnp.moveaxis(table[_t5_bucket(rel)], -1, 1)
        s = jnp.where(valid[:, None], s, NEG_INF)
        p = jax.nn.softmax(s, axis=-1)
        return jnp.einsum('bhqk,bqkhd->bqhd', p, v_sel.astype(jnp.float32))

    nb = tp // BLOCK_Q
    out = lax.map(block, (_to_blocks(q), _to_blocks(q_ix), _to_blocks(w_ix),
                          jnp.arange(nb) * BLOCK_Q))
    return _from_blocks(out).astype(v.dtype)

def _differential_attention(q1, q2, k1, k2, v, lam, bias_table):
    tp, dh = q1.shape[1], q1.shape[-1]
    scale = dh ** -0.5
    k1f, k2f, vf = k1.astype(jnp.float32), k2.astype(jnp.float32), v.astype(jnp.float32)
    key_pos = jnp.arange(tp)
    table = bias_table.astype(jnp.float32)

    def block(args):
        q1b, q2b, start = args
        qpos = start + jnp.arange(BLOCK_Q)
        mask = key_pos[None, :] <= qpos[:, None]
        bias = jnp.moveaxis(table[_t5_bucket(qpos[:, None] - key_pos[None, :])], -1, 0)

        def attn_map(qb, kf):
            s = jnp.einsum('bqhd,bkhd->bhqk', qb.astype(jnp.float32), kf) * scale + bias
            return jax.nn.softmax(jnp.where(mask, s, NEG_INF), axis=-1)

        p = attn_map(q1b, k1f) - lam * attn_map(q2b, k2f)
        return jnp.einsum('bhqk,bkhd->bqhd', p, vf)

    nb = tp // BLOCK_Q
    out = lax.map(block, (_to_blocks(q1), _to_blocks(q2), jnp.arange(nb) * BLOCK_Q))
    return _from_blocks(out).astype(v.dtype)

def _mixer(u, layer, w_in, b_gate, q_norm_sp, k_norm_sp, q_norm_df, k_norm_df,
           lam_q1, lam_k1, lam_q2, lam_k2, subln_df, w_br_sb, w_br_sp, w_br_df, w_out,
           rel_bias, top_k):
    b, tp, _ = u.shape
    (q_sb, k_sb, v_sb, q_sp, k_sp, v_sp, q_ix, k_ix, w_ix,
     q_df, k_df, v_df, g_sb, g_sp, g_df) = _split_cols(u @ w_in)

    def hd(a, n):
        return a.reshape(b, tp, n, -1)

    y_sb = _stick_breaking(hd(q_sb, SB_HEADS), hd(k_sb, SB_HEADS), hd(v_sb, SB_HEADS))
    y_sp = _indexed_sparse_attention(_rmsnorm(hd(q_sp, SP_HEADS), q_norm_sp),
                                     _rmsnorm(hd(k_sp, SP_HEADS), k_norm_sp),
                                     hd(v_sp, SP_HEADS), hd(q_ix, IDX_HEADS), k_ix, w_ix,
                                     rel_bias[:, :SP_HEADS], top_k)
    q_df = _rmsnorm(q_df.reshape(b, tp, DF_HEADS, 2, HEAD_DIM), q_norm_df)
    k_df = _rmsnorm(k_df.reshape(b, tp, DF_HEADS, 2, HEAD_DIM), k_norm_df)
    lam_init = 0.8 - 0.6 * math.exp(-0.3 * layer)
    lam = (jnp.exp(jnp.sum(lam_q1.astype(jnp.float32) * lam_k1.astype(jnp.float32)))
           - jnp.exp(jnp.sum(lam_q2.astype(jnp.float32) * lam_k2.astype(jnp.float32)))
           + lam_init)
    y_df = _differential_attention(q_df[..., 0, :], q_df[..., 1, :], k_df[..., 0, :],
                                   k_df[..., 1, :], hd(v_df, DF_HEADS), lam,
                                   rel_bias[:, SP_HEADS:])
    y_df = _rmsnorm(y_df, subln_df) * (1.0 - lam_init)

    merged = (jax.nn.sigmoid(g_sb + b_gate[:D_MODEL]) * (y_sb.reshape(b, tp, -1) @ w_br_sb)
              + jax.nn.sigmoid(g_sp + b_gate[D_MODEL:2 * D_MODEL]) * (y_sp.reshape(b, tp, -1) @ w_br_sp)
              + jax.nn.sigmoid(g_df + b_gate[2 * D_MODEL:]) * (y_df.reshape(b, tp, -1) @ w_br_df))
    return merged @ w_out

def _conv_ffn(u, w_up, conv_w, conv_b, w_down):
    tp = u.shape[1]
    z = u @ w_up
    gate, val = z[..., :D_FF], z[..., D_FF:]
    gp = jnp.pad(gate, ((0, 0), (CONV_WIDTH - 1, 0), (0, 0)))
    conv = conv_b + sum(gp[:, i:i + tp] * conv_w[i] for i in range(CONV_WIDTH))
    return (jax.nn.silu(conv) * val) @ w_down

def second_inputs(seed: int = 0) -> dict:
    key = jax.random.key(seed)
    ks = jax.random.split(key, 24)

    def n(k, shape, s):
        return jax.random.normal(k, shape, jnp.float32) * s

    return {
        'x': n(ks[0], (BATCH, SEQ, D_MODEL), 1.0),
        'meta_tokens': n(ks[1], (N_META, D_MODEL), 1.0),
        'rel_bias': n(ks[2], (N_BUCKETS, N_BIAS_HEADS), 0.5),
        'attn_norm': 1.0 + n(ks[3], (DEPTH, D_MODEL), 0.01),
        'w_in': n(ks[4], (DEPTH, D_MODEL, D_IN), D_MODEL ** -0.5),
        'b_gate': n(ks[5], (DEPTH, 3 * D_MODEL), 0.02),
        'q_norm_sp': 1.0 + n(ks[6], (DEPTH, HEAD_DIM), 0.01),
        'k_norm_sp': 1.0 + n(ks[7], (DEPTH, HEAD_DIM), 0.01),
        'q_norm_df': 1.0 + n(ks[8], (DEPTH, HEAD_DIM), 0.01),
        'k_norm_df': 1.0 + n(ks[9], (DEPTH, HEAD_DIM), 0.01),
        'lam_q1': n(ks[10], (DEPTH, HEAD_DIM), 0.1),
        'lam_k1': n(ks[11], (DEPTH, HEAD_DIM), 0.1),
        'lam_q2': n(ks[12], (DEPTH, HEAD_DIM), 0.1),
        'lam_k2': n(ks[13], (DEPTH, HEAD_DIM), 0.1),
        'subln_df': 1.0 + n(ks[14], (DEPTH, 2 * HEAD_DIM), 0.01),
        'w_br_sb': n(ks[15], (DEPTH, SB_W, D_MODEL), SB_W ** -0.5),
        'w_br_sp': n(ks[16], (DEPTH, SP_W, D_MODEL), SP_W ** -0.5),
        'w_br_df': n(ks[17], (DEPTH, DF_W, D_MODEL), DF_W ** -0.5),
        'w_out': n(ks[18], (DEPTH, D_MODEL, D_MODEL), D_MODEL ** -0.5),
        'ffn_norm': 1.0 + n(ks[19], (DEPTH, D_MODEL), 0.01),
        'w_up': n(ks[20], (DEPTH, D_MODEL, 2 * D_FF), D_MODEL ** -0.5),
        'conv_w': n(ks[21], (DEPTH, CONV_WIDTH, D_FF), CONV_WIDTH ** -0.5),
        'conv_b': n(ks[22], (DEPTH, D_FF), 0.02),
        'w_down': n(ks[23], (DEPTH, D_FF, D_MODEL), D_FF ** -0.5),
    }

def second_block(x, meta_tokens, rel_bias, attn_norm, w_in, b_gate, q_norm_sp, k_norm_sp,
              q_norm_df, k_norm_df, lam_q1, lam_k1, lam_q2, lam_k2, subln_df, w_br_sb,
              w_br_sp, w_br_df, w_out, ffn_norm, w_up, conv_w, conv_b, w_down):
    b, s, d = x.shape
    t = N_META + s
    tp = -(-t // BLOCK_Q) * BLOCK_Q
    top_k = min(TOPK_MAX, t // 4)
    meta = jnp.broadcast_to(meta_tokens[None].astype(x.dtype), (b, N_META, d))
    h = jnp.concatenate([meta, x, jnp.zeros((b, tp - t, d), x.dtype)], axis=1)
    for l in range(DEPTH):
        h = h + _mixer(_rmsnorm(h, attn_norm[l]), l, w_in[l], b_gate[l], q_norm_sp[l],
                       k_norm_sp[l], q_norm_df[l], k_norm_df[l], lam_q1[l], lam_k1[l],
                       lam_q2[l], lam_k2[l], subln_df[l], w_br_sb[l], w_br_sp[l],
                       w_br_df[l], w_out[l], rel_bias, top_k)
        h = h + _conv_ffn(_rmsnorm(h, ffn_norm[l]), w_up[l], conv_w[l], conv_b[l], w_down[l])
    return h[:, N_META:t]


_first_inputs_2 = second_inputs


def second_inputs(seed=0):
    import zlib

    import numpy as np

    out = dict(_first_inputs_2(seed))
    spreads = {}
    factors = {'attn_norm': 4.909,
     'b_gate': 8.0,
     'q_norm_sp': 8.0,
     'k_norm_sp': 8.0,
     'q_norm_df': 8.0,
     'k_norm_df': 8.0,
     'lam_q1': 8.0,
     'subln_df': 8.0,
     'ffn_norm': 8.0,
     'conv_b': 6.173}
    for name, (base, spread) in spreads.items():
        noise = np.random.default_rng([zlib.crc32(name.encode()), seed]).standard_normal(out[name].shape)
        drawn = base * np.exp(spread * noise) if base else spread * noise
        out[name] = __import__('jax').numpy.asarray(drawn.astype(out[name].dtype))
    for name, factor in factors.items():
        out[name] = (out[name] * factor).astype(out[name].dtype)
    return out


_narrow_inputs_2 = second_inputs


def second_inputs(seed=0):

    out = dict(_narrow_inputs_2(seed))
    wider = {'lam_q2': 4.72, 'subln_df': 6.65, 'ffn_norm': 4.52, 'conv_b': 4.2}
    for name, times in wider.items():
        mean = out[name].mean()
        out[name] = (mean + times * (out[name] - mean)).astype(out[name].dtype)
    return out


CHUNK_3 = 64
Q_BLOCK_3 = 128
FOX_HEADS = 6
FOX_HEAD_DIM = 64
FOX_WIDTH = FOX_HEADS * FOX_HEAD_DIM
FOX_FORGET_BIAS_MEAN = 3.0
HGRN_HEADS = 4
HGRN_KEY_DIM = 128
HGRN_VAL_DIM = 96
HGRN_KEY_WIDTH = HGRN_HEADS * HGRN_KEY_DIM
HGRN_VAL_WIDTH = HGRN_HEADS * HGRN_VAL_DIM
CONV_CH = 256
CONV_WIDTH_3 = 31
BRANCH_WIDTH = FOX_WIDTH + HGRN_VAL_WIDTH + CONV_CH
FFN_CONV_WIDTH = 3

IN_SIZES = (FOX_WIDTH, FOX_WIDTH, FOX_WIDTH, FOX_HEADS,
            HGRN_KEY_WIDTH, HGRN_KEY_WIDTH, HGRN_VAL_WIDTH, HGRN_VAL_WIDTH,
            CONV_CH, CONV_CH, N_BRANCH * D_MODEL)
IN_WIDTH = sum(IN_SIZES)
IN_SPLITS = tuple(int(v) for v in np.cumsum(IN_SIZES)[:-1])


def rmsnorm_3(x, g):
    x32 = x.astype(jnp.float32)
    y = x32 * lax.rsqrt(jnp.mean(x32 * x32, axis=-1, keepdims=True) + EPS)
    return (y * g.astype(jnp.float32)).astype(x.dtype)

def layernorm_3(x, g, b):
    x32 = x.astype(jnp.float32)
    mu = jnp.mean(x32, axis=-1, keepdims=True)
    xc = x32 - mu
    y = xc * lax.rsqrt(jnp.mean(xc * xc, axis=-1, keepdims=True) + EPS)
    return (y * g.astype(jnp.float32) + b.astype(jnp.float32)).astype(x.dtype)

def causal_dwconv(u, w, b):
    k = w.shape[0]
    y = lax.conv_general_dilated(
        u, w[:, None, :].astype(u.dtype), window_strides=(1,), padding=[(k - 1, 0)],
        dimension_numbers=("NWC", "WIO", "NWC"), feature_group_count=u.shape[-1])
    return y + b.astype(u.dtype)

def split_heads(t, n_heads):
    b, s, w = t.shape
    return t.reshape(b, s, n_heads, w // n_heads).transpose(0, 2, 1, 3)

def fox_attention(q, k, v, logf):
    s_len = q.shape[2]
    scale = q.shape[-1] ** -0.5
    c = jnp.cumsum(logf, axis=-1)
    outs = []
    for start in range(0, s_len, Q_BLOCK_3):
        end = start + Q_BLOCK_3
        qb = q[:, :, start:end]
        kb = k[:, :, :end]
        vb = v[:, :, :end]
        logits = jnp.einsum("bhqd,bhkd->bhqk", qb, kb).astype(jnp.float32) * scale
        logits = logits + (c[:, :, start:end, None] - c[:, :, None, :end])
        mask = (start + jnp.arange(Q_BLOCK_3))[:, None] >= jnp.arange(end)[None, :]
        logits = jnp.where(mask, logits, -jnp.inf)
        p = jax.nn.softmax(logits, axis=-1)
        outs.append(jnp.einsum("bhqk,bhkd->bhqd", p.astype(v.dtype), vb))
    return jnp.concatenate(outs, axis=2)

def hgrn2_chunkwise(q, k, v, logf):
    b, h, s_len, kd = q.shape
    vd = v.shape[-1]
    n = s_len // CHUNK_3
    def to_chunks(t):
        t = t.astype(jnp.float32).reshape(b, h, n, CHUNK_3, t.shape[-1])
        return jnp.moveaxis(t, 2, 0)
    qc, kc, vc, lc = to_chunks(q), to_chunks(k), to_chunks(v), to_chunks(logf)
    bc = jnp.cumsum(lc, axis=-2)
    tri = jnp.tril(jnp.ones((CHUNK_3, CHUNK_3), dtype=bool))

    def step(state, inp):
        qx, kx, vx, bx = inp
        diff = bx[:, :, :, None, :] - bx[:, :, None, :, :]
        decay = jnp.exp(jnp.where(tri[:, :, None], diff, -jnp.inf))
        attn = jnp.einsum("bhtk,bhsk,bhtsk->bhts", qx, kx, decay)
        o = (jnp.einsum("bhts,bhsv->bhtv", attn, vx)
             + jnp.einsum("bhtk,bhkv->bhtv", qx * jnp.exp(bx), state))
        b_last = bx[:, :, -1:, :]
        new_state = (jnp.exp(b_last[:, :, 0, :])[..., None] * state
                     + jnp.einsum("bhsk,bhsv->bhkv", kx * jnp.exp(b_last - bx), vx))
        return new_state, o

    state0 = jnp.zeros((b, h, kd, vd), jnp.float32)
    _, ys = lax.scan(step, state0, (qc, kc, vc, bc))
    ys = jnp.moveaxis(ys, 0, 2).reshape(b, h, s_len, vd)
    return ys.astype(v.dtype)

def third_inputs(seed: int = 0) -> dict:
    key = jax.random.key(seed)
    ks = jax.random.split(key, 21)
    L, D = DEPTH, D_MODEL
    def nrm(k, shape, scale):
        return jax.random.normal(k, shape, jnp.float32) * scale
    return {
        "x": nrm(ks[0], (BATCH, SEQ, D), 1.0),
        "norm_mix_g": 1.0 + nrm(ks[1], (L, D), 0.02),
        "w_in": nrm(ks[2], (L, D, IN_WIDTH), D ** -0.5),
        "fox_forget_b": FOX_FORGET_BIAS_MEAN + nrm(ks[3], (L, FOX_HEADS), 0.1),
        "fox_q_norm_g": 1.0 + nrm(ks[4], (L, FOX_HEAD_DIM), 0.02),
        "fox_k_norm_g": 1.0 + nrm(ks[5], (L, FOX_HEAD_DIM), 0.02),
        "hgrn_lb_logits": nrm(ks[6], (L, HGRN_KEY_WIDTH), 0.5),
        "hgrn_out_norm_g": 1.0 + nrm(ks[7], (L, HGRN_VAL_DIM), 0.02),
        "conv_dw_w": nrm(ks[8], (L, CONV_WIDTH_3, CONV_CH), CONV_WIDTH_3 ** -0.5),
        "conv_dw_b": nrm(ks[9], (L, CONV_CH), 0.02),
        "conv_norm_g": 1.0 + nrm(ks[10], (L, CONV_CH), 0.02),
        "conv_norm_b": nrm(ks[11], (L, CONV_CH), 0.02),
        "gate_b": nrm(ks[12], (L, N_BRANCH * D), 0.1),
        "w_branch": nrm(ks[13], (L, BRANCH_WIDTH, D), FOX_WIDTH ** -0.5),
        "w_out": nrm(ks[14], (L, D, D), D ** -0.5),
        "norm_ffn_g": 1.0 + nrm(ks[15], (L, D), 0.02),
        "w_up": nrm(ks[16], (L, D, 2 * D_FF), D ** -0.5),
        "ffn_dw_w": nrm(ks[17], (L, FFN_CONV_WIDTH, D_FF), FFN_CONV_WIDTH ** -0.5),
        "ffn_dw_b": nrm(ks[18], (L, D_FF), 0.02),
        "w_down": nrm(ks[19], (L, D_FF, D), D_FF ** -0.5),
    }

def third_block(x, norm_mix_g, w_in, fox_forget_b, fox_q_norm_g, fox_k_norm_g,
              hgrn_lb_logits, hgrn_out_norm_g, conv_dw_w, conv_dw_b, conv_norm_g,
              conv_norm_b, gate_b, w_branch, w_out, norm_ffn_g, w_up, ffn_dw_w,
              ffn_dw_b, w_down):
    b, s_len, d = x.shape
    lb_all = jnp.cumsum(jax.nn.softmax(hgrn_lb_logits.astype(jnp.float32), axis=0), axis=0)
    lb_all = jnp.maximum(lb_all - lb_all[0:1], 0.0)
    o_a = FOX_WIDTH
    o_b = FOX_WIDTH + HGRN_VAL_WIDTH
    for l in range(DEPTH):
        h = rmsnorm_3(x, norm_mix_g[l])
        z = h @ w_in[l]
        (fq, fk, fv, ff, hq, hf, hi, hg, ca, cb, gl) = jnp.split(z, IN_SPLITS, axis=-1)

        qa = rmsnorm_3(split_heads(fq, FOX_HEADS), fox_q_norm_g[l])
        ka = rmsnorm_3(split_heads(fk, FOX_HEADS), fox_k_norm_g[l])
        va = split_heads(fv, FOX_HEADS)
        logf_a = jax.nn.log_sigmoid(ff.astype(jnp.float32) + fox_forget_b[l]).transpose(0, 2, 1)
        ya = fox_attention(qa, ka, va, logf_a)
        ya = ya.transpose(0, 2, 1, 3).reshape(b, s_len, FOX_WIDTH)

        lb = lb_all[l]
        logf_b = jnp.logaddexp(jnp.log(lb), jnp.log1p(-lb) + jax.nn.log_sigmoid(hf.astype(jnp.float32)))
        kb_in = -jnp.expm1(logf_b)
        yb = hgrn2_chunkwise(split_heads(hq, HGRN_HEADS),
                             split_heads(kb_in.astype(x.dtype), HGRN_HEADS),
                             split_heads(hi, HGRN_HEADS),
                             split_heads(logf_b, HGRN_HEADS))
        yb = rmsnorm_3(yb.transpose(0, 2, 1, 3), hgrn_out_norm_g[l])
        yb = yb * jax.nn.silu(hg.reshape(b, s_len, HGRN_HEADS, HGRN_VAL_DIM))
        yb = yb.reshape(b, s_len, HGRN_VAL_WIDTH)

        yc = ca * jax.nn.sigmoid(cb)
        yc = causal_dwconv(yc, conv_dw_w[l], conv_dw_b[l])
        yc = jax.nn.silu(layernorm_3(yc, conv_norm_g[l], conv_norm_b[l]))

        gates = jax.nn.sigmoid((gl + gate_b[l]).astype(jnp.float32)).astype(x.dtype)
        gates = gates.reshape(b, s_len, N_BRANCH, d)
        wb = w_branch[l]
        merged = (gates[:, :, 0] * (ya @ wb[:o_a])
                  + gates[:, :, 1] * (yb @ wb[o_a:o_b])
                  + gates[:, :, 2] * (yc @ wb[o_b:]))
        x = x + merged @ w_out[l]

        h2 = rmsnorm_3(x, norm_ffn_g[l])
        gate_in, value_in = jnp.split(h2 @ w_up[l], 2, axis=-1)
        gate_in = causal_dwconv(gate_in, ffn_dw_w[l], ffn_dw_b[l])
        x = x + (jax.nn.silu(gate_in) * value_in) @ w_down[l]
    return x


_first_inputs_3 = third_inputs


def third_inputs(seed=0):
    import zlib

    import numpy as np

    out = dict(_first_inputs_3(seed))
    spreads = {}
    factors = {'norm_mix_g': 2.937,
     'fox_forget_b': 38.24,
     'fox_q_norm_g': 8.0,
     'fox_k_norm_g': 8.0,
     'hgrn_out_norm_g': 8.0,
     'conv_dw_b': 13.641,
     'conv_norm_g': 62.712,
     'conv_norm_b': 64.0,
     'gate_b': 3.203,
     'norm_ffn_g': 11.139,
     'ffn_dw_b': 5.894}
    for name, (base, spread) in spreads.items():
        noise = np.random.default_rng([zlib.crc32(name.encode()), seed]).standard_normal(out[name].shape)
        drawn = base * np.exp(spread * noise) if base else spread * noise
        out[name] = __import__('jax').numpy.asarray(drawn.astype(out[name].dtype))
    for name, factor in factors.items():
        out[name] = (out[name] * factor).astype(out[name].dtype)
    return out


_narrow_inputs_3 = third_inputs


def third_inputs(seed=0):

    out = dict(_narrow_inputs_3(seed))
    wider = {'fox_q_norm_g': 4.94, 'fox_k_norm_g': 4.22, 'hgrn_out_norm_g': 6.27, 'ffn_dw_b': 6.16}
    for name, times in wider.items():
        mean = out[name].mean()
        out[name] = (mean + times * (out[name] - mean)).astype(out[name].dtype)
    return out


def setup_inputs(seed=0):
    out = dict(first_inputs(seed))
    for name, value in second_inputs(seed + 1).items():
        if name != "x":
            out[name + "_2"] = value
    for name, value in third_inputs(seed + 2).items():
        if name != "x":
            out[name + "_3"] = value
    return out


def reference(
    x, c, g_pre, g_post, w_ada, b_ada, w_in, conv_w, conv_b, pos_ck, w_ck1, w_ck2, pos_cv,
    w_cv1, w_cv2, ln_g, ln_b, w_s, b_s, w_br, w_out, meta_tokens_2, rel_bias_2, attn_norm_2,
    w_in_2, b_gate_2, q_norm_sp_2, k_norm_sp_2, q_norm_df_2, k_norm_df_2, lam_q1_2, lam_k1_2,
    lam_q2_2, lam_k2_2, subln_df_2, w_br_sb_2, w_br_sp_2, w_br_df_2, w_out_2, ffn_norm_2,
    w_up_2, conv_w_2, conv_b_2, w_down_2, norm_mix_g_3, w_in_3, fox_forget_b_3, fox_q_norm_g_3,
    fox_k_norm_g_3, hgrn_lb_logits_3, hgrn_out_norm_g_3, conv_dw_w_3, conv_dw_b_3,
    conv_norm_g_3, conv_norm_b_3, gate_b_3, w_branch_3, w_out_3, norm_ffn_g_3, w_up_3,
    ffn_dw_w_3, ffn_dw_b_3, w_down_3,
):
    x = first_block(
        x, c, g_pre, g_post, w_ada, b_ada, w_in, conv_w, conv_b, pos_ck, w_ck1, w_ck2, pos_cv,
        w_cv1, w_cv2, ln_g, ln_b, w_s, b_s, w_br, w_out,
    )
    x = second_block(
        x, meta_tokens_2, rel_bias_2, attn_norm_2, w_in_2, b_gate_2, q_norm_sp_2, k_norm_sp_2,
        q_norm_df_2, k_norm_df_2, lam_q1_2, lam_k1_2, lam_q2_2, lam_k2_2, subln_df_2, w_br_sb_2,
        w_br_sp_2, w_br_df_2, w_out_2, ffn_norm_2, w_up_2, conv_w_2, conv_b_2, w_down_2,
    )
    return third_block(
        x, norm_mix_g_3, w_in_3, fox_forget_b_3, fox_q_norm_g_3, fox_k_norm_g_3,
        hgrn_lb_logits_3, hgrn_out_norm_g_3, conv_dw_w_3, conv_dw_b_3, conv_norm_g_3,
        conv_norm_b_3, gate_b_3, w_branch_3, w_out_3, norm_ffn_g_3, w_up_3, ffn_dw_w_3,
        ffn_dw_b_3, w_down_3,
    )


_drawn_inputs = setup_inputs


def setup_inputs(seed=0):
    import zlib

    import numpy as np

    out = dict(_drawn_inputs(seed))
    spreads = {}
    factors = {'lam_k1_2': 4.607,
     'norm_mix_g_3': 2.684,
     'fox_q_norm_g_3': 2.842,
     'fox_k_norm_g_3': 10.315,
     'conv_norm_g_3': 4.849,
     'conv_norm_b_3': 12.338,
     'norm_ffn_g_3': 3.605,
     'ffn_dw_b_3': 2.993}
    for name, (base, spread) in spreads.items():
        noise = np.random.default_rng([zlib.crc32(name.encode()), seed]).standard_normal(out[name].shape)
        drawn = base * np.exp(spread * noise) if base else spread * noise
        out[name] = __import__('jax').numpy.asarray(drawn.astype(out[name].dtype))
    for name, factor in factors.items():
        out[name] = (out[name] * factor).astype(out[name].dtype)
    return out
```

```python
import math
from contextlib import ExitStack, contextmanager

import numpy as np

import concourse.bass as bass
from concourse import mybir

F32 = mybir.dt.float32
ALU = mybir.AluOpType
ACT = mybir.ActivationFunctionType
AX_X = mybir.AxisListType.X

P = 128
D = 1024
KT = D // P
S = 512
META = 16
T2 = META + S
HD = 64
EPS = 1e-6
BIG = 1e30
FAR = 1e33
Q_SCALE = -(HD ** -0.5)

MIX = 1024
NH, NKV = 16, 4
N_CMP = (S - 32) // 16 + 1
TOP_K = min(256, T2 // 4)
D_FF = 2816
FFT = D_FF // P
LAM_INIT = 0.8 - 0.6 * math.exp(-0.3 * 0)
FOX = 6
HG = 4
HG_V = 96
CH = 64
CONV_W = 31

OFF = 512
TAB = OFF + P


class Chain:

    def __init__(self, eng, done, base=0):
        self.eng, self.done, self.base, self.n = eng, done, base, 0

    def link(self, ins):
        self.n += 1
        ins.then_inc(self.done, 1)
        self.eng.wait_ge(self.done, self.base + self.n)


@contextmanager
def stage(nc, *names):
    sems = [nc.alloc_semaphore(f"{n}_{nc.next_id()}") for n in names]
    with ExitStack() as ctx:
        def sbuf(name, shape, dtype=F32):
            return ctx.enter_context(nc.sbuf_tensor(f"{name}_{nc.next_id()}", shape, dtype))

        def psum(name, shape):
            return ctx.enter_context(nc.psum_tensor(f"{name}_{nc.next_id()}", shape, F32))

        with ExitStack() as inner:
            def begin():
                return inner.enter_context(nc.Block())
            yield sems, sbuf, psum, begin
    nc.clear_and_free_semaphores(sems)
    nc.all_engine_barrier()


def rounds(eng, steps, unroll, body):
    full = steps // unroll
    if full:
        body(0, unroll, True)
    if full > 2:
        with eng.Fori(1, full) as r:
            body(r, unroll, False)
    elif full == 2:
        body(1, unroll, False)
    if steps % unroll:
        body(full, steps % unroll, full == 0)


def project(nc, weights, steps, tiles, n, w, act_step=None, dve_step=None, unroll=2,
            act_links=0, dve_links=0, scratch=()):
    nk = sum(t[1] for t in tiles)
    names = ["products_done", "act_done", "step_done", "act_link", "dve_link"] + [f"weights_in{u}" for u in range(unroll)]
    with stage(nc, *names) as (sems, sbuf, psum, begin):
        products_done, act_done, step_done, act_link, dve_link = sems[:5]
        weights_in = sems[5:]
        ring = sbuf("weight_ring", [P, unroll, nk, P])
        tmp = {name: sbuf(name, [P, unroll] + shape) for name, shape in scratch}
        acc = psum("acc", [P, unroll, len(tiles) * n, 512])
        block = begin()

        def out_of(u, j):
            return acc[:, u, j * n:(j + 1) * n, 0:w]

        @block.sync
        def _(sp):
            def load(r, count, first):
                for u in range(count):
                    if not first:
                        sp.wait_ge(products_done, (r - 1) * unroll + u + 1)
                    sp.dma_start(ring[:, u, :, :], weights[bass.ds(r * unroll + u, 1)].rearrange("a p k m -> p (a k) m")
                                 ).then_inc(weights_in[u], 16)
            rounds(sp, steps, unroll, load)

        @block.tensor
        def _(pe):
            def multiply(r, count, first):
                for u in range(count):
                    pe.wait_ge(weights_in[u], r * 16 + 16)
                    if not first:
                        pe.wait_ge(step_done, (r - 1) * unroll + u + 1)
                    k0 = 0
                    for j, (source, ks, rows) in enumerate(tiles):
                        for half in range(n):
                            for k in range(ks):
                                last = pe.matmul(acc[:, u, j * n + half, 0:w], ring[0:rows, u, k0 + k, :],
                                                 source(k)[:, half * w:(half + 1) * w], start=k == 0, stop=k == ks - 1)
                        k0 += ks
                    last.then_inc(products_done, 1)
            rounds(pe, steps, unroll, multiply)

        if act_step is not None:
            @block.scalar
            def _(act):
                def finish(r, count, first):
                    for u in range(count):
                        i = r * unroll + u
                        act.wait_ge(products_done, i + 1)
                        chain = Chain(act, act_link, i * act_links)
                        last = act_step(act, chain, i, lambda j: out_of(u, j), {k: v[:, u] for k, v in tmp.items()})
                        last.then_inc(step_done if dve_step is None else act_done, 1)
                        assert chain.n == act_links
                rounds(act, steps, unroll, finish)

        if dve_step is not None:
            @block.vector
            def _(dve):
                def finish(r, count, first):
                    for u in range(count):
                        i = r * unroll + u
                        if act_step is not None:
                            dve.wait_ge(act_done, i + 1)
                        else:
                            dve.wait_ge(products_done, i + 1)
                        chain = Chain(dve, dve_link, i * dve_links)
                        last = dve_step(dve, chain, i, lambda j: out_of(u, j), {k: v[:, u] for k, v in tmp.items()})
                        last.then_inc(step_done, 1)
                        assert chain.n == dve_links, (chain.n, dve_links)
                rounds(dve, steps, unroll, finish)


def project_tokens(nc, weights, cols, source, tok, epilogue, act_links=0, dve_links=0, consts=()):
    nt = (tok + P - 1) // P
    chunks = [(c, min(512, cols - c)) for c in range(0, cols, 512)]
    nb = len(chunks)
    with stage(nc, "weights_in", "products_done", "taken", "dve_link") as (sems, sbuf, psum, begin):
        weights_in, products_done, taken, dve_link = sems
        w_sb = sbuf("w_tok", [P, KT, cols])
        acc = psum("acc", [P, 2, nb, 512])
        block = begin()

        @block.sync
        def _(sp):
            sp.dma_start(w_sb[:, :, :], weights).then_inc(weights_in, 16)

        @block.tensor
        def _(pe):
            pe.wait_ge(weights_in, 16)
            for t in range(nt):
                rows = min(P, tok - t * P)
                if t >= 2:
                    pe.wait_ge(taken, t - 1)
                for b, (c, width) in enumerate(chunks):
                    for k in range(KT):
                        last = pe.matmul(acc[0:rows, t % 2, b, 0:width], source(k)[:, t * P:t * P + rows],
                                         w_sb[:, k, c:c + width], start=k == 0, stop=k == KT - 1)
                last.then_inc(products_done, 1)

        @block.scalar
        def _(act):
            for t in range(nt):
                rows = min(P, tok - t * P)
                act.wait_ge(products_done, t + 1)
                for b, (c, width) in enumerate(chunks):
                    last = epilogue(act, t, rows, c, width, acc[0:rows, t % 2, b, 0:width])
                last.then_inc(taken, 1)


def rms_norm(nc, k, source, dest, gain, shift, n, w):
    with stage(nc, "squared", "summed", "mean_done", "root_done", "scale_done", "scaled", "shifted") as (sems, sbuf, psum, begin):
        squared, summed, mean_done, root_done, scale_done, scaled, shifted = sems
        sq = sbuf("sq", [P, KT, n * w])
        scale = sbuf("scale", [P, 3, n, w])
        acc = psum("acc", [P, n, 512])
        block = begin()

        @block.scalar
        def _(act):
            for t in range(KT):
                act.activation(sq[:, t, :], source(t), ACT.Square).then_inc(squared, 1)
            act.wait_ge(mean_done, 1)
            act.activation(scale[:, 1], scale[:, 0], ACT.Sqrt).then_inc(root_done, 1)
            if shift is not None:
                for t in range(KT):
                    act.wait_ge(scaled, t + 1)
                    act.activation(dest(t), dest(t), ACT.Identity, bias=shift(t)).then_inc(shifted, 1)

        @block.tensor
        def _(pe):
            for half in range(n):
                for t in range(KT):
                    pe.wait_ge(squared, t + 1)
                    last = pe.matmul(acc[:, half, 0:w], k.ones[:, :], sq[:, t, half * w:(half + 1) * w],
                                     start=t == 0, stop=t == KT - 1)
            last.then_inc(summed, 1)

        @block.vector
        def _(dve):
            dve.wait_ge(summed, 1)
            dve.tensor_scalar(scale[:, 0], acc[:, :, 0:w], 1.0 / D, EPS, ALU.mult, ALU.add).then_inc(mean_done, 1)
            dve.wait_ge(root_done, 1)
            dve.reciprocal(scale[:, 2], scale[:, 1]).then_inc(scale_done, 1)
            dve.wait_ge(scale_done, 1)
            for t in range(KT):
                dve.scalar_tensor_tensor(dest(t), source(t), gain(t), scale[:, 2].rearrange("p a b -> p (a b)"),
                                         ALU.mult, ALU.mult).then_inc(scaled, 1)


def head_norms(nc, heads, ones, dim, n, w, rows=P):
    with stage(nc, "squared", "summed", "mean_done", "root_done", "inverted", "done") as (sems, sbuf, psum, begin):
        squared, summed, mean_done, root_done, inverted, done = sems
        sq = sbuf("sq", [P, 2, n * w])
        scale = sbuf("scale", [P, 2, 2, n * w])
        acc = psum("acc", [P, 2, n, 512])
        block = begin()

        def flat(a):
            return a.rearrange("p (a b) -> p a b", a=n)

        @block.scalar
        def _(act):
            for i in range(len(heads) + 1):
                if i < len(heads):
                    if i >= 2:
                        act.wait_ge(summed, i - 1)
                    act.activation(sq[0:rows, i % 2], heads[i][0], ACT.Square).then_inc(squared, 1)
                if i >= 1:
                    act.wait_ge(mean_done, i)
                    act.activation(scale[0:rows, (i - 1) % 2, 1], scale[0:rows, (i - 1) % 2, 0], ACT.Sqrt).then_inc(root_done, 1)

        @block.tensor
        def _(pe):
            for i in range(len(heads)):
                pe.wait_ge(squared, i + 1)
                if i >= 2:
                    pe.wait_ge(mean_done, i - 1)
                for half in range(n):
                    last = pe.matmul(acc[0:rows, i % 2, half, 0:w], ones[0:rows, 0:rows],
                                     sq[0:rows, i % 2, half * w:(half + 1) * w], start=True, stop=True)
                last.then_inc(summed, 1)

        @block.vector
        def _(dve):
            for i, (tile, gain) in enumerate(heads):
                dve.wait_ge(summed, i + 1)
                if i >= 2:
                    dve.wait_ge(done, i - 1)
                dve.tensor_scalar(flat(scale[0:rows, i % 2, 0]), acc[0:rows, i % 2, :, 0:w], 1.0 / dim, EPS,
                                  ALU.mult, ALU.add).then_inc(mean_done, 1)
                dve.wait_ge(root_done, i + 1)
                dve.reciprocal(scale[0:rows, i % 2, 0], scale[0:rows, i % 2, 1]).then_inc(inverted, 1)
                dve.wait_ge(inverted, i + 1)
                dve.scalar_tensor_tensor(tile, tile, gain, scale[0:rows, i % 2, 0], ALU.mult, ALU.mult).then_inc(done, 1)


class Part:

    def __init__(self, q, keys, table, values, gate=None, gate_const=None, extra=None, penalty=None):
        self.q, self.keys, self.table, self.values = q, keys, table, values
        self.gate, self.gate_const, self.extra, self.penalty = gate, gate_const, extra, penalty
        self.nq, self.nk = q.shape[1], keys.shape[1]
        self.blocks = [(c, min(P, self.nk - c)) for c in range(0, self.nk, P)]


def attend(nc, k, groups, wide):
    lag = 1 if wide else 2
    ns = lag + 1
    parts, of = [], []
    for g, (members, out) in enumerate(groups):
        for m, part in enumerate(members):
            parts.append(part)
            of.append((g, m == 0, m == len(members) - 1))
    N = len(parts)
    last_of = [max(i for i in range(N) if of[i][0] == g) for g in range(len(groups))]
    with stage(nc, "scores_ready", "max_ready", "exp_done", "row_inverted", "diag_ready", "turned", "turned_read",
               "weighted", "out_read", "biased") as (sems, sbuf, psum, begin):
        scores_ready, max_ready, exp_done, row_inverted, diag_ready, turned, turned_read, weighted, out_read, biased = sems
        width = 1024 if wide else 512
        biased_scores = sbuf("biased_scores", [P, ns, T2])
        probs = sbuf("probs", [P, ns, T2])
        bias_sum = sbuf("bias_sum", [P, T2])
        diag = sbuf("diag", [P, ns, P])
        probs_t = sbuf("probs_t", [P, 2, 512])
        low = sbuf("low", [P, ns, 1])
        row_sum = sbuf("row_sum", [P, ns, 1])
        row_inv = sbuf("row_inv", [P, ns, 1])
        scores = psum("scores", [P, ns, width])
        turn = psum("turn", [P, 2, 512])
        out_acc = psum("out_acc", [P, 2, 512])
        block = begin()

        def turn_block(i, b, kb):
            nq = parts[i].nq
            return turn[0:kb, i % 2, b * nq:(b + 1) * nq]

        def out_at(g, part, out):
            base = out.start_partition()
            return out_acc[base:base + out.shape[0], g % 2, 0:part.nq]

        @block.tensor
        def _(pe):
            for i in range(N + lag + 1):
                if i < N:
                    part = parts[i]
                    if i >= ns:
                        pe.wait_ge(max_ready, i - ns + 1)
                    for c in range(0, part.nk, 512):
                        e = min(part.nk, c + 512)
                        last = pe.matmul(scores[0:part.nq, i % ns, c:e], part.q, part.keys[:, c:e],
                                         start=True, stop=part.extra is None)
                        if part.extra is not None:
                            last = pe.matmul(scores[0:part.nq, i % ns, c:e], part.extra[0][:, 0:part.nq], part.extra[1][:, c:e],
                                             start=False, stop=True)
                    last.then_inc(scores_ready, 1)
                if lag <= i < N + lag:
                    j = i - lag
                    part = parts[j]
                    pe.wait_ge(diag_ready, j + 1)
                    if j >= 2:
                        pe.wait_ge(turned_read, j - 1)
                    for b, (c, kb) in enumerate(part.blocks):
                        last = pe.matmul(turn_block(j, b, kb), probs[0:part.nq, j % ns, c:c + kb],
                                         diag[0:part.nq, j % ns, 0:part.nq], start=True, stop=True)
                    last.then_inc(turned, 1)
                if i >= lag + 1:
                    j = i - lag - 1
                    part = parts[j]
                    g, opens, closes = of[j]
                    pe.wait_ge(turned_read, j + 1)
                    if opens and g >= 2:
                        pe.wait_ge(out_read, g - 1)
                    for b, (c, kb) in enumerate(part.blocks):
                        last = pe.matmul(out_at(g, part, groups[g][1]), part.values[b], probs_t[0:kb, j % 2, b * part.nq:(b + 1) * part.nq],
                                         start=opens and b == 0, stop=closes and b == len(part.blocks) - 1)
                    last.then_inc(weighted, 1)

        @block.vector
        def _(dve):
            n_biased = 0
            for i in range(N + 1):
                if i < N:
                    part = parts[i]
                    table = part.table
                    if part.penalty is not None:
                        if i >= 1:
                            dve.wait_ge(max_ready, i)
                        n_biased += 1
                        dve.tensor_tensor(bias_sum[0:part.nq, 0:part.nk], part.table, part.penalty, ALU.add).then_inc(biased, 1)
                        dve.wait_ge(biased, n_biased)
                        table = bias_sum[0:part.nq, 0:part.nk]
                    dve.wait_ge(scores_ready, i + 1)
                    if i >= ns:
                        dve.wait_ge(exp_done, i - ns + 1)
                    dve.tensor_tensor_reduce(biased_scores[0:part.nq, i % ns, 0:part.nk], scores[0:part.nq, i % ns, 0:part.nk], table,
                                             1.0, 3e38, ALU.add, ALU.min, low[0:part.nq, i % ns, :]).then_inc(max_ready, 1)
                if i >= 1:
                    j = i - 1
                    part = parts[j]
                    dve.wait_ge(exp_done, j + 1)
                    dve.reciprocal(row_inv[0:part.nq, j % ns, :], row_sum[0:part.nq, j % ns, :]).then_inc(row_inverted, 1)
                    dve.wait_ge(row_inverted, j + 1)
                    if j >= ns:
                        dve.wait_ge(turned, j - ns + 1)
                    d = diag[0:part.nq, j % ns, 0:part.nq]
                    if part.gate is not None:
                        dve.tensor_scalar(d, k.ident[0:part.nq, 0:part.nq], row_inv[0:part.nq, j % ns, :], part.gate,
                                          ALU.mult, ALU.mult).then_inc(diag_ready, 1)
                    else:
                        dve.tensor_scalar(d, k.ident[0:part.nq, 0:part.nq], row_inv[0:part.nq, j % ns, :], None,
                                          ALU.mult).then_inc(diag_ready, 1)

        @block.scalar
        def _(act):
            def copy_out(g):
                part, out = parts[last_of[g]], groups[g][1]
                act.wait_ge(weighted, last_of[g] + 1)
                act.activation(out, out_at(g, part, out), ACT.Copy).then_inc(out_read, 1)

            g_next = 0
            for i in range(N + lag + 1):
                if i < N:
                    part = parts[i]
                    act.wait_ge(max_ready, i + 1)
                    if i >= ns:
                        act.wait_ge(turned, i - ns + 1)
                    act.activation(probs[0:part.nq, i % ns, 0:part.nk], biased_scores[0:part.nq, i % ns, 0:part.nk], ACT.Exp,
                                   bias=low[0:part.nq, i % ns, :], scale=-1.0,
                                   accum_out=row_sum[0:part.nq, i % ns, :]).then_inc(exp_done, 1)
                if lag <= i < N + lag:
                    j = i - lag
                    part = parts[j]
                    act.wait_ge(turned, j + 1)
                    if j >= 2:
                        act.wait_ge(weighted, j - 1)
                    rows = part.blocks[0][1]
                    full = [b for b in part.blocks if b[1] == rows]
                    rest = part.blocks[len(full):]
                    last = act.activation(probs_t[0:rows, j % 2, 0:len(full) * part.nq], turn[0:rows, j % 2, 0:len(full) * part.nq], ACT.Copy)
                    for b, (c, kb) in enumerate(rest, len(full)):
                        last = act.activation(probs_t[0:kb, j % 2, b * part.nq:(b + 1) * part.nq], turn_block(j, b, kb), ACT.Copy)
                    last.then_inc(turned_read, 1)
                while g_next < len(groups) and last_of[g_next] <= i - lag - 2:
                    copy_out(g_next)
                    g_next += 1
            while g_next < len(groups):
                copy_out(g_next)
                g_next += 1


def tiles_of(buffer, n, w, offset=0):
    return lambda t: buffer[:, t, offset:offset + n * w]


def tile_at(buffer, i, n, w, offset=0):
    return buffer[:, bass.ds(i, 1), offset:offset + n * w].rearrange("p a (n w) -> p (a n) w", n=n)


def merge(nc, k, weights, h, y, ks, rows, bias_at, first, merged, n, w):
    def gate(act, chain, i, acc, tmp):
        bias = 0.0 if bias_at is None else k.vec[:, bass.ds(bias_at + i, 1)]
        return act.activation(tmp["gate"], acc(0), ACT.Sigmoid, bias=bias)

    def combine(dve, chain, i, acc, tmp):
        if first:
            return dve.tensor_tensor(tile_at(merged, i, n, w), tmp["gate"], acc(1), ALU.mult)
        chain.link(dve.tensor_tensor(tmp["gate"], tmp["gate"], acc(1), ALU.mult))
        return dve.tensor_tensor(tile_at(merged, i, n, w), tile_at(merged, i, n, w), tmp["gate"], ALU.add)

    project(nc, weights, KT, [(h, KT, P), (y, ks, rows)], n, w, gate, combine, dve_links=0 if first else 1,
            scratch=[("gate", [n, w])])


def feed_forward(nc, k, up, down, conv_w, conv_b, h, x, off, n, w):
    T = n * w
    with ExitStack() as ctx:
        hidden = ctx.enter_context(nc.sbuf_tensor(f"ffn_hidden_{nc.next_id()}", [P, FFT, T], F32))
        names = ["products_done", "gate_copied", "conv_done", "silu_done", "step_done", "dve_link", "weights_in0", "weights_in1"]
        with stage(nc, *names) as (sems, sbuf, psum, begin):
            products_done, gate_copied, conv_done, silu_done, step_done, dve_link = sems[:6]
            weights_in = sems[6:]
            ring = sbuf("weight_ring", [P, 2, 2 * KT, P])
            gate_pad = sbuf("gate_pad", [P, 2, 2 + T])
            conv = sbuf("conv", [P, 2, T])
            acc = psum("acc", [P, 2, 2, n, 512])
            block = begin()

            @block.sync
            def _(sp):
                def load(r, count, first):
                    for u in range(count):
                        if not first:
                            sp.wait_ge(products_done, (r - 1) * 2 + u + 1)
                        sp.dma_start(ring[:, u, :, :], up[bass.ds(r * 2 + u, 1)].rearrange("a p k m -> p (a k) m")
                                     ).then_inc(weights_in[u], 16)
                rounds(sp, FFT, 2, load)

            @block.tensor
            def _(pe):
                def multiply(r, count, first):
                    for u in range(count):
                        pe.wait_ge(weights_in[u], r * 16 + 16)
                        if not first:
                            pe.wait_ge(step_done, (r - 1) * 2 + u + 1)
                        for j in range(2):
                            for half in range(n):
                                for t in range(KT):
                                    last = pe.matmul(acc[:, u, j, half, 0:w], ring[:, u, j * KT + t, :],
                                                     h(t)[:, half * w:(half + 1) * w], start=t == 0, stop=t == KT - 1)
                        last.then_inc(products_done, 1)
                rounds(pe, FFT, 2, multiply)

            @block.scalar
            def _(act):
                def finish(r, count, first):
                    for u in range(count):
                        i = r * 2 + u
                        act.wait_ge(products_done, i + 1)
                        act.activation(gate_pad[:, u, 2:2 + T].rearrange("p (n w) -> p n w", n=n), acc[:, u, 0, :, 0:w],
                                       ACT.Copy).then_inc(gate_copied, 1)
                        act.wait_ge(conv_done, i + 1)
                        act.activation(conv[:, u, :], conv[:, u, :], ACT.Silu).then_inc(silu_done, 1)
                rounds(act, FFT, 2, finish)

            @block.vector
            def _(dve):
                pads = Chain(dve, dve_link)
                pads.link(dve.memset(gate_pad[:, :, 0:2], 0.0))

                def finish(r, count, first):
                    for u in range(count):
                        i = r * 2 + u
                        chain = Chain(dve, dve_link, 1 + i * 2)
                        taps = [k.vec[:, bass.ds(conv_w + FFT * tap + i, 1)] for tap in range(3)]
                        dve.wait_ge(gate_copied, i + 1)
                        chain.link(dve.tensor_scalar(conv[:, u, :], gate_pad[:, u, 0:T], taps[0],
                                                     k.vec[:, bass.ds(conv_b + i, 1)], ALU.mult, ALU.add))
                        chain.link(dve.scalar_tensor_tensor(conv[:, u, :], gate_pad[:, u, 1:1 + T], taps[1], conv[:, u, :], ALU.mult, ALU.add))
                        dve.scalar_tensor_tensor(conv[:, u, :], gate_pad[:, u, 2:2 + T], taps[2], conv[:, u, :],
                                                 ALU.mult, ALU.add).then_inc(conv_done, 1)
                        dve.wait_ge(silu_done, i + 1)
                        dve.tensor_tensor(tile_at(hidden, i, n, w), conv[:, u, :].rearrange("p (n w) -> p n w", n=n), acc[:, u, 1, :, 0:w],
                                          ALU.mult).then_inc(step_done, 1)
                rounds(dve, FFT, 2, finish)

        project(nc, down, KT, [(tiles_of(hidden, n, w), FFT, P)], n, w, None,
                lambda dve, chain, i, acc, tmp: dve.tensor_tensor(tile_at(x, i, n, w, off), tile_at(x, i, n, w, off), acc(0), ALU.add))


def copies(dest, n, w, scale=1.0, at=0):
    return lambda act, chain, i, acc, tmp: act.activation(tile_at(dest, i + at, n, w), acc(0), ACT.Copy, scale=scale)



def modulation(nc, k, A):
    steps, per = 6, 4
    with stage(nc, "c_ready", "products_done", "ada_link", "weights_in0", "weights_in1") as (sems, sbuf, psum, begin):
        c_ready, products_done, ada_link = sems[:3]
        weights_in = sems[3:]
        ring = sbuf("weight_ring", [P, 2, per * KT, P])
        c_silu = sbuf("c_silu", [P, KT])
        acc = psum("acc", [P, 3 * KT])
        block = begin()

        @block.sync
        def _(sp):
            for i in range(steps):
                if i >= 2:
                    sp.wait_ge(products_done, i - 1)
                sp.dma_start(ring[:, i % 2, :, :], A["w_ada"][i]).then_inc(weights_in[i % 2], 16)

        @block.scalar
        def _(act):
            act.activation(c_silu[:, :], k.col("c"), ACT.Silu).then_inc(c_ready, 1)

        @block.tensor
        def _(pe):
            pe.wait_ge(c_ready, 1)
            for i in range(steps):
                pe.wait_ge(weights_in[i % 2], 16 * (i // 2 + 1))
                for j in range(per):
                    for t in range(KT):
                        last = pe.matmul(acc[:, i * per + j:i * per + j + 1], ring[:, i % 2, j * KT + t, :], c_silu[:, t:t + 1],
                                         start=t == 0, stop=t == KT - 1)
                last.then_inc(products_done, 1)

        @block.vector
        def _(dve):
            chain = Chain(dve, ada_link)
            dve.wait_ge(products_done, steps)
            chain.link(dve.tensor_tensor(k.ada[:, :], acc[:, :], k.col("b_ada"), ALU.add))
            chain.link(dve.scalar_tensor_tensor(k.ada[:, KT:2 * KT], k.ada[:, KT:2 * KT], 1.0, k.col("g_pre"), ALU.add, ALU.mult))
            chain.link(dve.tensor_tensor(k.ada[:, 2 * KT:], k.ada[:, 2 * KT:], k.col("g_post"), ALU.mult))


def conv_mixer(nc, k, A, h, y):
    cw, cb = k.at("conv_w"), k.at("conv_b")

    def ahead(act, chain, i, acc, tmp):
        act.activation(tmp["xin"], acc(2), ACT.Copy)
        return act.activation(tmp["z"], acc(3), ACT.Silu)

    def mix(dve, chain, i, acc, tmp):
        pad, conv = tmp["pad"], tmp["conv"]
        chain.link(dve.memset(pad[:, 0:2], 0.0))
        chain.link(dve.tensor_tensor(pad[:, 2:2 + S].unsqueeze(1), acc(1), tmp["xin"], ALU.mult))
        taps = [k.vec[:, bass.ds(cw + KT * tap + i, 1)] for tap in range(3)]
        chain.link(dve.tensor_scalar(conv, pad[:, 0:S], taps[0], k.vec[:, bass.ds(cb + i, 1)], ALU.mult, ALU.add))
        chain.link(dve.scalar_tensor_tensor(conv, pad[:, 1:1 + S], taps[1], conv, ALU.mult, ALU.add))
        chain.link(dve.scalar_tensor_tensor(conv, pad[:, 2:2 + S], taps[2], conv, ALU.mult, ALU.add))
        chain.link(dve.tensor_tensor(conv.unsqueeze(1), conv.unsqueeze(1), acc(0), ALU.mult))
        return dve.tensor_tensor(tile_at(y, i, 1, S), conv.unsqueeze(1), tmp["z"], ALU.mult)

    project(nc, A["w_conv"], KT, [(h, KT, P)] * 4, 1, S, ahead, mix, dve_links=6,
            scratch=[("xin", [1, S]), ("z", [1, S]), ("pad", [2 + S]), ("conv", [S])])


def compress(nc, k, A, kv, k_cmp, v_cmp):
    with stage(nc, "loaded", "hidden_ready", "pos_copied", "hidden_done", "out_ready", "copied") as (sems, sbuf, psum, begin):
        loaded, hidden_ready, pos_copied, hidden_done, out_ready, copied = sems
        w1 = sbuf("w1", [HD, 2, 32, P])
        pos = sbuf("pos", [HD, 2, 32])
        w2 = sbuf("w2", [P, 2, P])
        pos_term = sbuf("pos_term", [P, 2])
        hidden = sbuf("hidden", [P, 2, NKV * N_CMP])
        acc = psum("acc", [P, 2, 512])
        pos_acc = psum("pos_acc", [P, 2, 512])
        out = psum("out", [P, 2, 512])
        block = begin()

        @block.sync
        def _(sp):
            sp.dma_start(w1[:, :, :, :], A["w_cmp1"]).then_inc(loaded, 16)
            sp.dma_start(pos[:, :, :], A["pos_cmp"]).then_inc(loaded, 16)
            sp.dma_start(w2[:, :, :], A["w_cmp2"]).then_inc(loaded, 16)

        @block.tensor
        def _(pe):
            pe.wait_ge(loaded, 48)
            for a in range(2):
                for s in range(32):
                    pe.matmul(acc[:, a, 0:NKV * N_CMP].rearrange("p (g n) -> p g n", g=NKV), w1[:, a, s, :],
                              kv[0:HD, a * NKV:(a + 1) * NKV, s:s + 16 * (N_CMP - 1) + 1:16], start=s == 0, stop=s == 31)
                for s in range(32):
                    last = pe.matmul(pos_acc[:, a, 0:1], w1[:, a, s, :], pos[:, a, s:s + 1], start=s == 0, stop=s == 31)
                last.then_inc(hidden_ready, 1)
            pe.wait_ge(hidden_done, 1)
            pe.matmul(out[:, 0, 0:NKV * N_CMP], w2[:, 0, :], hidden[:, 0, :], start=True, stop=True).then_inc(out_ready, 1)
            pe.wait_ge(hidden_done, 2)
            for g in range(NKV):
                last = pe.matmul(out[0:N_CMP, 1, g * HD:(g + 1) * HD], hidden[:, 1, g * N_CMP:(g + 1) * N_CMP], w2[:, 1, 0:HD],
                                 start=True, stop=True)
            last.then_inc(out_ready, 1)

        @block.vector
        def _(dve):
            for a in range(2):
                dve.wait_ge(hidden_ready, a + 1)
                dve.tensor_copy(pos_term[:, a:a + 1], pos_acc[:, a, 0:1]).then_inc(pos_copied, 1)
            dve.wait_ge(out_ready, 1)
            dve.tensor_copy(k_cmp[:, :], out[:, 0, 0:NKV * N_CMP]).then_inc(copied, 1)
            dve.wait_ge(out_ready, 2)
            dve.tensor_copy(v_cmp[0:N_CMP, :], out[0:N_CMP, 1, 0:NKV * HD]).then_inc(copied, 1)

        @block.scalar
        def _(act):
            for a in range(2):
                act.wait_ge(pos_copied, a + 1)
                act.activation(hidden[:, a, :], acc[:, a, 0:NKV * N_CMP], ACT.Silu, bias=pos_term[:, a:a + 1]).then_inc(hidden_done, 1)


def sparse_mixer(nc, k, A, h, y):
    with ExitStack() as ctx:
        def sbuf(name, shape):
            return ctx.enter_context(nc.sbuf_tensor(f"{name}_{nc.next_id()}", shape, F32))

        q = sbuf("q_t", [P, KT, S])
        keys = sbuf("keys_t", [P, 2 * NKV, S])
        v_tok = sbuf("v_tok", [P, S // P, 2 * NKV * HD])
        gates = sbuf("gates", [P, S // P, 3 * NH])
        k_cmp = sbuf("k_cmp", [P, NKV * N_CMP])
        v_cmp = sbuf("v_cmp", [N_CMP, NKV * HD])
        project(nc, A["w_q"], KT, [(h, KT, P)], 1, S, copies(q, 1, S, Q_SCALE), unroll=4)
        with nc.sbuf_tensor(f"kv_cmp_{nc.next_id()}", [P, 2 * NKV, S], F32) as kv:
            project(nc, A["w_kv_cmp"], 2 * NKV, [(h, KT, P)], 1, S, copies(kv, 1, S), unroll=4)
            compress(nc, k, A, kv, k_cmp, v_cmp)
        project(nc, A["w_keys"], 2 * NKV, [(h, KT, P)], 1, S, copies(keys, 1, S), unroll=4)

        def take(act, t, rows, c, width, acc):
            if c == 0:
                return act.activation(v_tok[0:rows, t, :], acc, ACT.Copy)
            return act.activation(gates[0:rows, t, :], acc, ACT.Sigmoid)

        project_tokens(nc, A["w_v_gates"], 512 + 3 * NH, h, S, take)

        table = sbuf("alibi", [P, NH, TAB])
        table_cmp = sbuf("alibi_cmp", [P, NH, 4 * N_CMP])
        slopes = [float(np.float32(2.0) ** np.float32(-8.0 * i / NH)) for i in range(1, NH + 1)]
        with stage(nc, "tables_done") as ((tables_done,), _, _, begin):
            block = begin()

            @block.vector
            def _(dve):
                for head in range(NH):
                    dve.tensor_scalar(table[:, head, :], k.distance, slopes[head], None, ALU.mult).then_inc(tables_done, 1)
                for head in range(NH):
                    dve.tensor_scalar(table_cmp[:, head, :], k.distance_cmp, slopes[head], None, ALU.mult).then_inc(tables_done, 1)
                first = gates[:, 0, 0:3 * NH:3]
                dve.tensor_scalar(first, first, k.sees_cmp, None, ALU.mult).then_inc(tables_done, 1)

        groups = []
        for head in range(NH):
            base, g = (head % 2) * HD, head // (NH // NKV)
            rows = slice(base, base + HD)
            for t in range(S // P):
                cols = slice(t * P, (t + 1) * P)
                qb = q[rows, head // 2, cols]
                members = [Part(qb, k_cmp[rows, g * N_CMP:(g + 1) * N_CMP], table_cmp[:, head, t * N_CMP:(t + 1) * N_CMP],
                                [v_cmp[0:N_CMP, g * HD:(g + 1) * HD]], gate=gates[:, t, 3 * head:3 * head + 1])]
                for branch in range(2):
                    c = (branch * NKV + g) * HD
                    members.append(Part(qb, keys[rows, branch * NKV + g, 0:(t + 1) * P], table[:, head, OFF - t * P:TAB],
                                        [v_tok[:, b, c:c + HD] for b in range(t + 1)],
                                        gate=gates[:, t, 3 * head + 1 + branch:3 * head + 2 + branch]))
                groups.append((members, y[rows, head // 2, cols]))
        attend(nc, k, groups, wide=False)

    project(nc, A["w_z"], KT, [(h, KT, P)], 1, S,
            lambda act, chain, i, acc, tmp: act.activation(tmp["z"], acc(0), ACT.Silu),
            lambda dve, chain, i, acc, tmp: dve.tensor_tensor(tile_at(y, i, 1, S), tile_at(y, i, 1, S), tmp["z"], ALU.mult),
            unroll=4, scratch=[("z", [1, S])])


def gmlp_mixer(nc, k, A, h, y):
    chunks = S // P
    with ExitStack() as ctx:
        v_tok = ctx.enter_context(nc.sbuf_tensor(f"v_tok_{nc.next_id()}", [P, chunks, MIX], F32))
        mixed = ctx.enter_context(nc.sbuf_tensor(f"mixed_{nc.next_id()}", [P, KT, S], F32))
        project_tokens(nc, A["w_v"], MIX, h, S,
                       lambda act, t, rows, c, width, acc: act.activation(v_tok[0:rows, t, c:c + width], acc, ACT.Gelu_apprx_tanh))
        with stage(nc, "loaded", "mask_done", "var_ready", "root_done", "normed", "mixed_ready", "taken", "dve_link") as (sems, sbuf, psum, begin):
            loaded, mask_done, var_ready, root_done, normed, mixed_ready, taken, dve_link = sems
            w_s = sbuf("w_s", [P, KT, P])
            b_s = sbuf("b_s", [1, KT, P])
            ln = sbuf("ln", [P, 2, MIX])
            stats = sbuf("stats", [P, 2, 6])
            moments = sbuf("moments", [P, chunks, 2])
            root = sbuf("root", [P, chunks, 2])
            acc = psum("acc", [P, 2, chunks, P])
            block = begin()

            @block.sync
            def _(sp):
                sp.dma_start(w_s[:, :, :], A["w_s_t"]).then_inc(loaded, 16)
                sp.dma_start(b_s[:, :, :], A["b_s"]).then_inc(loaded, 16)
                sp.dma_start(ln[:, 0, :], A["ln_g"].partition_broadcast(P)).then_inc(loaded, 16)
                sp.dma_start(ln[:, 1, :], A["ln_b"].partition_broadcast(P)).then_inc(loaded, 16)

            @block.gpsimd
            def _(pool):
                pool.wait_ge(loaded, 64)
                pool.affine_select(w_s[:, :, :], w_s[:, :, :], pattern=[[0, KT], [1, P]], compare_op=ALU.is_ge, fill=0.0, base=0,
                                   channel_multiplier=-1).then_inc(mask_done, 1)

            @block.vector
            def _(dve):
                chain = Chain(dve, dve_link)
                for t in range(chunks):
                    chain.link(dve.bn_stats(stats[:, 0, :], v_tok[:, t, 0:512]))
                    chain.link(dve.bn_stats(stats[:, 1, :], v_tok[:, t, 512:1024]))
                    chain.link(dve.bn_aggr(moments[:, t, :], stats[:, :, :]))
                    dve.tensor_scalar(root[:, t, 0:1], moments[:, t, 1:2], EPS, None, ALU.add).then_inc(var_ready, 1)
                dve.wait_ge(loaded, 64)
                for t in range(chunks):
                    dve.wait_ge(root_done, t + 1)
                    chain.link(dve.reciprocal(root[:, t, 0:1], root[:, t, 1:2]))
                    chain.link(dve.tensor_scalar(v_tok[:, t, :], v_tok[:, t, :], moments[:, t, 0:1], root[:, t, 0:1], ALU.subtract, ALU.mult))
                    chain.link(dve.tensor_tensor(v_tok[:, t, :], v_tok[:, t, :], ln[:, 0, :], ALU.mult))
                    dve.tensor_tensor(v_tok[:, t, :], v_tok[:, t, :], ln[:, 1, :], ALU.add).then_inc(normed, 1)

            @block.scalar
            def _(act):
                for t in range(chunks):
                    act.wait_ge(var_ready, t + 1)
                    act.activation(root[:, t, 1:2], root[:, t, 0:1], ACT.Sqrt).then_inc(root_done, 1)
                for g in range(KT):
                    act.wait_ge(mixed_ready, g + 1)
                    act.activation(mixed[:, g, :], acc[:, g % 2].rearrange("p n i -> p (n i)"), ACT.Copy).then_inc(taken, 1)

            @block.tensor
            def _(pe):
                pe.wait_ge(mask_done, 1)
                pe.wait_ge(normed, chunks)
                for g in range(KT):
                    if g >= 2:
                        pe.wait_ge(taken, g - 1)
                    for t in range(chunks):
                        pe.matmul(acc[:, g % 2, t, :], v_tok[:, t, g * P:(g + 1) * P], w_s[:, g, :], start=True, stop=False)
                        last = pe.matmul(acc[:, g % 2, t, :], k.ones[0:1, :], b_s[0:1, g, :], start=False, stop=True)
                    last.then_inc(mixed_ready, 1)

        def ahead(act, chain, i, acc, tmp):
            act.activation(tmp["u"], acc(0), ACT.Gelu_apprx_tanh)
            return act.activation(tmp["z"], acc(1), ACT.Silu)

        def mix(dve, chain, i, acc, tmp):
            chain.link(dve.tensor_tensor(tmp["u"], tmp["u"], tile_at(mixed, i, 1, S), ALU.mult))
            return dve.tensor_tensor(tile_at(y, i, 1, S), tmp["u"], tmp["z"], ALU.mult)

        project(nc, A["w_uz"], KT, [(h, KT, P)] * 2, 1, S, ahead, mix, dve_links=1, scratch=[("u", [1, S]), ("z", [1, S])])


def add_tiles(nc, x, o, off, T):
    with stage(nc, "added") as ((added,), _, _, begin):
        block = begin()

        @block.vector
        def _(dve):
            for t in range(KT):
                dve.tensor_tensor(x[:, t, off:off + T], x[:, t, off:off + T], o[:, t, 0:T], ALU.add).then_inc(added, 1)


def first_block(nc, k, A, b):
    n, w = 1, S
    x, h, y, merged = tiles_of(b.x, n, w, META), tiles_of(b.h, n, w), tiles_of(b.y, n, w), tiles_of(b.merged, n, w)
    modulation(nc, k, A)
    rms_norm(nc, k, x, h, lambda t: k.ada[:, KT + t:KT + t + 1], lambda t: k.ada[:, t:t + 1], n, w)
    conv_mixer(nc, k, A, h, b.y)
    merge(nc, k, A["w_merge0"], h, y, KT, P, None, True, b.merged, n, w)
    sparse_mixer(nc, k, A, h, b.y)
    merge(nc, k, A["w_merge1"], h, y, KT, P, None, False, b.merged, n, w)
    gmlp_mixer(nc, k, A, h, b.y)
    merge(nc, k, A["w_merge2"], h, y, KT, P, None, False, b.merged, n, w)
    project(nc, A["w_out"], KT, [(merged, KT, P)], n, w, copies(b.y, n, w), unroll=4)
    rms_norm(nc, k, y, h, lambda t: k.ada[:, 2 * KT + t:2 * KT + t + 1], None, n, w)
    add_tiles(nc, b.x, b.h, META, S)



SB_Q, SB_K, SP_Q, SP_K, IX_Q, IX_K, DF_Q, DF_K, FM2 = 0, 2, 4, 6, 8, 10, 11, 15, 19
SB_V, SP_V, DF_V, IX_W, TM2 = 0, 256, 512, 1024, 1032
N2, W2 = 2, T2 // 2
QT2 = (T2 + P - 1) // P
ROWS2 = [min(P, T2 - t * P) for t in range(QT2)]
REPLACED = -3e38
PAD = -2e30


def stick_breaking(nc, k, fm, v_tok, y):
    scale = HD ** -0.5
    units = [(head, half) for head in range(4) for half in range(N2)]
    kbs = {half: [kb for kb in reversed(range(QT2)) if kb * P < (half + 1) * W2] for half in range(N2)}
    steps = [(u, head, half, kb) for u, (head, half) in enumerate(units) for kb in kbs[half]]
    N = len(steps)
    first_of = {u: min(i for i in range(N) if steps[i][0] == u) for u in range(len(units))}
    last_of = {u: max(i for i in range(N) if steps[i][0] == u) for u in range(len(units))}
    names = ["scores_ready", "scaled_done", "abs_done", "exp_done", "log_done", "scores_masked", "soft_masked", "sums_ready", "exponent_ready",
             "weights_done", "out_ready", "out_copied", "act_link", "dve_link", "hidden"]
    with stage(nc, *names) as (sems, sbuf, psum, begin):
        (scores_ready, scaled_done, abs_done, exp_done, log_done, scores_masked, soft_masked, sums_ready, exponent_ready, weights_done, out_ready,
         out_copied, act_link, dve_link, hidden) = sems
        hide = sbuf("hide", [P, k.before.shape[1]])
        scaled = sbuf("scaled", [P, 2, W2])
        masked = sbuf("masked", [P, 2, W2])
        soft = sbuf("soft", [P, 2, QT2, W2])
        log_part = sbuf("log_part", [P, 2, W2])
        relu_part = sbuf("relu_part", [P, W2])
        weight = sbuf("weight", [P, 2, W2])
        scores = psum("scores", [P, 2, 512])
        sums = psum("sums", [P, 2, 512])
        out = psum("out", [P, 2, 512])
        block = begin()

        def window(half, kb):
            c = half * W2 - kb * P + 256
            return slice(c, c + W2)

        @block.tensor
        def _(pe):
            def score(i):
                u, head, half, kb = steps[i]
                rows = slice((head % 2) * HD, (head % 2) * HD + HD)
                if i >= 2:
                    pe.wait_ge(abs_done, i - 1)
                pe.matmul(scores[0:ROWS2[kb], i % 2, 0:W2], fm[rows, SB_K + head // 2, kb * P:kb * P + ROWS2[kb]],
                          fm[rows, SB_Q + head // 2, half * W2:(half + 1) * W2], start=True, stop=True).then_inc(scores_ready, 1)

            def add_up(i):
                u, head, half, kb = steps[i]
                pe.wait_ge(soft_masked, i + 1)
                if i >= 2:
                    pe.wait_ge(exponent_ready, i - 1)
                after = [b for b in kbs[half] if b > kb]
                for b in after:
                    pe.matmul(sums[0:ROWS2[kb], i % 2, 0:W2], k.ones[0:ROWS2[b], 0:ROWS2[kb]], soft[0:ROWS2[b], u % 2, b, :],
                              start=b == after[0], stop=False)
                pe.matmul(sums[0:ROWS2[kb], i % 2, 0:W2], k.later[0:ROWS2[kb], 0:ROWS2[kb]], soft[0:ROWS2[kb], u % 2, kb, :],
                          start=not after, stop=True).then_inc(sums_ready, 1)

            def weigh(i):
                u, head, half, kb = steps[i]
                base = (head % 2) * HD
                pe.wait_ge(weights_done, i + 1)
                if i == first_of[u] and u >= 2:
                    pe.wait_ge(out_copied, u - 1)
                last = pe.matmul(out[base:base + HD, u % 2, 0:W2], v_tok[0:ROWS2[kb], kb, SB_V + head * HD:SB_V + (head + 1) * HD],
                                 weight[0:ROWS2[kb], i % 2, :], start=i == first_of[u], stop=i == last_of[u])
                last.then_inc(out_ready, 1)

            for i in range(N + 2):
                if i < N:
                    score(i)
                if 1 <= i <= N:
                    add_up(i - 1)
                if i >= 2:
                    weigh(i - 2)

        @block.scalar
        def _(act):
            chain = Chain(act, act_link)
            for i in range(N + 2):
                if i < N:
                    u, head, half, kb = steps[i]
                    r = ROWS2[kb]
                    act.wait_ge(scores_ready, i + 1)
                    if i >= 2:
                        act.wait_ge(soft_masked, i - 1)
                    act.activation(scaled[0:r, i % 2, :], scores[0:r, i % 2, 0:W2], ACT.Copy, scale=scale).then_inc(scaled_done, 1)
                    act.activation(log_part[0:r, i % 2, :], scores[0:r, i % 2, 0:W2], ACT.Abs, scale=scale).then_inc(abs_done, 1)
                    act.wait_ge(abs_done, i + 1)
                    chain.link(act.activation(log_part[0:r, i % 2, :], log_part[0:r, i % 2, :], ACT.Exp, scale=-1.0))
                    act.activation(log_part[0:r, i % 2, :], log_part[0:r, i % 2, :], ACT.Ln, bias=1.0).then_inc(log_done, 1)
                if i >= 1 and i <= N:
                    j = i - 1
                    r = ROWS2[steps[j][3]]
                    act.wait_ge(exponent_ready, j + 1)
                    act.activation(weight[0:r, j % 2, :], masked[0:r, j % 2, :], ACT.Exp).then_inc(weights_done, 1)
                if i >= 2:
                    j = i - 2
                    u, head, half, kb = steps[j]
                    if j == last_of[u]:
                        rows = slice((head % 2) * HD, (head % 2) * HD + HD)
                        act.wait_ge(out_ready, j + 1)
                        act.activation(y[rows, head // 2, half * W2:(half + 1) * W2], out[rows, u % 2, 0:W2], ACT.Copy).then_inc(out_copied, 1)

        @block.vector
        def _(dve):
            chain = Chain(dve, dve_link)
            dve.tensor_scalar(hide[:, :], k.before, 1.0, BIG, ALU.subtract, ALU.mult).then_inc(hidden, 1)
            dve.wait_ge(hidden, 1)
            for i in range(N + 1):
                if i < N:
                    u, head, half, kb = steps[i]
                    r = ROWS2[kb]
                    dve.wait_ge(scaled_done, i + 1)
                    if i >= 2:
                        dve.wait_ge(weights_done, i - 1)
                    chain.link(dve.tensor_tensor(masked[0:r, i % 2, :], scaled[0:r, i % 2, :], hide[0:r, window(half, kb)], ALU.add))
                    dve.wait_ge(log_done, i + 1)
                    chain.link(dve.scalar_tensor_tensor(relu_part[0:r, :], scaled[0:r, i % 2, :], 0.0, log_part[0:r, i % 2, :],
                                                        ALU.max, ALU.add))
                    if i == first_of[u] and u >= 2:
                        dve.wait_ge(sums_ready, last_of[u - 2] + 1)
                    dve.tensor_tensor(soft[0:r, u % 2, kb, :], relu_part[0:r, :], k.before[0:r, window(half, kb)], ALU.mult).then_inc(soft_masked, 1)
                    dve.wait_ge(soft_masked, i + 1)
                if i >= 1:
                    j = i - 1
                    r = ROWS2[steps[j][3]]
                    dve.wait_ge(sums_ready, j + 1)
                    dve.tensor_tensor(masked[0:r, j % 2, :], masked[0:r, j % 2, :], sums[0:r, j % 2, 0:W2], ALU.subtract).then_inc(exponent_ready, 1)


def select_keys(nc, k, fm, v_tok, penalty):
    heads = 8
    full_rounds, rest = divmod(TOP_K, 8)
    jobs = [(t, j) for t in range(1, QT2) for j in range(heads)]
    with stage(nc, "dots_ready", "relu_done", "added", "link") as (sems, sbuf, psum, begin):
        dots_ready, relu_done, added, dve_link = sems
        relu = sbuf("relu", [P, 2, T2])
        score = sbuf("score", [P, T2 + 8])
        top = sbuf("top", [P, 8])
        dots = psum("dots", [P, 2, 1024])
        block = begin()

        def keys_of(t):
            return min((t + 1) * P, T2)

        @block.tensor
        def _(pe):
            for i, (t, j) in enumerate(jobs):
                rows = slice((j % 4) * 32, (j % 4) * 32 + 32)
                if i >= 2:
                    pe.wait_ge(relu_done, i - 1)
                for c in range(0, keys_of(t), 512):
                    e = min(c + 512, keys_of(t))
                    last = pe.matmul(dots[0:ROWS2[t], i % 2, c:e], fm[rows, IX_Q + j // 4, t * P:t * P + ROWS2[t]], fm[rows, IX_K, c:e],
                                     start=True, stop=True, tile_position=((j % 4) * 32, 0))
                last.then_inc(dots_ready, 1)

        @block.scalar
        def _(act):
            for i, (t, j) in enumerate(jobs):
                act.wait_ge(dots_ready, i + 1)
                if i >= 2:
                    act.wait_ge(added, i - 1)
                act.activation(relu[0:ROWS2[t], i % 2, 0:keys_of(t)], dots[0:ROWS2[t], i % 2, 0:keys_of(t)], ACT.Relu).then_inc(relu_done, 1)

        @block.vector
        def _(dve):
            chain = Chain(dve, dve_link)
            for i, (t, j) in enumerate(jobs):
                r, nk = ROWS2[t], keys_of(t)
                s = score[0:r, 0:nk]
                weight = v_tok[0:r, t, IX_W + j:IX_W + j + 1]
                dve.wait_ge(relu_done, i + 1)
                if j == 0:
                    ins = dve.tensor_scalar(s, relu[0:r, i % 2, 0:nk], weight, None, ALU.mult)
                else:
                    ins = dve.scalar_tensor_tensor(s, relu[0:r, i % 2, 0:nk], weight, s, ALU.mult, ALU.add)
                ins.then_inc(added, 1)
                dve.wait_ge(added, i + 1)
                if j < heads - 1:
                    continue
                chain.link(dve.tensor_tensor(s, s, k.causal[0:r, OFF - t * P:OFF - t * P + nk], ALU.subtract))
                chain.link(dve.memset(score[0:r, nk:nk + 8], PAD))
                s = score[0:r, 0:nk + 8]
                for n in range(full_rounds + (rest > 0)):
                    chain.link(dve.max(top[0:r, :], s))
                    if n == full_rounds:
                        chain.link(dve.memset(top[0:r, rest:8], PAD))
                    chain.link(dve.match_replace(s, top[0:r, :], s, REPLACED))
                chain.link(dve.tensor_scalar(penalty[0:r, t, 0:nk], score[0:r, 0:nk], REPLACED, BIG, ALU.not_equal, ALU.mult))


def bias_tables(nc, k, A, scratch, table):
    with stage(nc, "loaded", "rows_ready", "rows_copied", "rows_stored", "tables_in0", "tables_in1", "turned", "turned_copied") as (sems, sbuf, psum, begin):
        loaded, rows_ready, rows_copied, rows_stored = sems[:4]
        tables_in, (turned, turned_copied) = sems[4:6], sems[6:]
        width = TAB + P - 1
        by_bucket = sbuf("by_bucket", [33, 8])
        bucket = sbuf("bucket", [33, width])
        rows = sbuf("rows", [8, width])
        flipped = sbuf("flipped", [P, 2, TAB])
        acc = psum("acc", [8, 2, 512])
        turn = psum("turn", [P, 2, 2, 512])
        block = begin()
        half = (width + 1) // 2
        spans = [(0, half), (half, width)]

        @block.sync
        def _(sp):
            sp.dma_start(by_bucket[:, :], A["rel_bias"]).then_inc(loaded, 16)
            sp.dma_start(bucket[:, :], A["bucket"]).then_inc(loaded, 16)
            sp.wait_ge(rows_copied, 2)
            sp.dma_start(scratch, rows[:, :]).then_inc(rows_stored, 16)
            sp.wait_ge(rows_stored, 16)
            for head in range(8):
                if head >= 2:
                    sp.wait_ge(turned, head - 1)
                src = bass.AP(tensor=scratch.tensor, offset=head * width, ap=[[1, P], [1, TAB]])
                sp.dma_start(flipped[:, head % 2, :], src).then_inc(tables_in[head % 2], 16)

        @block.tensor
        def _(pe):
            pe.wait_ge(loaded, 32)
            for i, (a, e) in enumerate(spans):
                pe.matmul(acc[:, i, 0:e - a], by_bucket[:, :], bucket[:, a:e], start=True, stop=True).then_inc(rows_ready, 1)
            for head in range(8):
                pe.wait_ge(tables_in[head % 2], 16 * (head // 2 + 1))
                if head >= 2:
                    pe.wait_ge(turned_copied, head - 1)
                for i in range(2):
                    last = pe.matmul(turn[:, head % 2, i, 0:TAB // 2], k.mirror, flipped[:, head % 2, i * TAB // 2:(i + 1) * TAB // 2],
                                     start=True, stop=True)
                last.then_inc(turned, 1)

        @block.scalar
        def _(act):
            for i, (a, e) in enumerate(spans):
                act.wait_ge(rows_ready, i + 1)
                act.activation(rows[:, a:e], acc[:, i, 0:e - a], ACT.Copy).then_inc(rows_copied, 1)
            for head in range(8):
                act.wait_ge(turned, head + 1)
                act.activation(table[:, head, :].rearrange("p (a b) -> p a b", a=2), turn[:, head % 2, :, 0:TAB // 2],
                               ACT.Copy).then_inc(turned_copied, 1)


def mixing_scalars(nc, k, neg_lam, q_sp, q_df):
    with stage(nc, "products_ready", "sums_ready", "exp_done", "link") as (sems, sbuf, psum, begin):
        products_ready, sums_ready, exp_done, dve_link = sems
        prod = sbuf("prod", [P, 2])
        e = sbuf("e", [P, 2])
        acc = psum("acc", [P, 2])
        block = begin()

        @block.vector
        def _(dve):
            chain = Chain(dve, dve_link)
            lam = k.col("lam")
            dve.tensor_tensor(prod[:, :], lam[:, 0:2], lam[:, 2:4], ALU.mult).then_inc(products_ready, 1)
            chain.link(dve.tensor_scalar(q_sp, k.col("q_norm_sp"), Q_SCALE, None, ALU.mult))
            chain.link(dve.tensor_scalar(q_df, k.col("q_norm_df"), Q_SCALE, None, ALU.mult))
            dve.wait_ge(exp_done, 1)
            chain.link(dve.tensor_tensor(neg_lam, e[:, 1:2], e[:, 0:1], ALU.subtract))
            chain.link(dve.tensor_scalar(neg_lam, neg_lam, LAM_INIT, None, ALU.subtract))

        @block.tensor
        def _(pe):
            pe.wait_ge(products_ready, 1)
            pe.matmul(acc[:, :], k.ones, prod[:, :], start=True, stop=True).then_inc(sums_ready, 1)

        @block.scalar
        def _(act):
            act.wait_ge(sums_ready, 1)
            act.activation(e[:, :], acc[:, :], ACT.Exp).then_inc(exp_done, 1)


def scale_columns(nc, out, col, factor):
    with stage(nc, "scaled") as ((scaled,), _, _, begin):
        block = begin()

        @block.vector
        def _(dve):
            dve.tensor_scalar(out, col, factor, None, ALU.mult).then_inc(scaled, 1)


def second_attention(nc, k, A, h, y, scratch):
    n, w = N2, W2
    with ExitStack() as ctx:
        def sbuf(name, shape):
            return ctx.enter_context(nc.sbuf_tensor(f"{name}_{nc.next_id()}", shape, F32))

        fm = sbuf("fm", [P, FM2, T2])
        v_tok = sbuf("v_tok", [P, QT2, TM2])
        small = sbuf("small", [P, 4])
        project(nc, A["w_fm_2"], FM2, [(h, KT, P)], n, w, copies(fm, n, w), unroll=4)
        project_tokens(nc, A["w_tok_2"], TM2, h, T2,
                       lambda act, t, rows, c, width, acc: act.activation(v_tok[0:rows, t, c:c + width], acc, ACT.Copy))
        mixing_scalars(nc, k, small[:, 0:1], small[:, 1:2], small[:, 2:3])
        scale_columns(nc, small[:, 3:4], k.col("subln_df"), 1.0 - LAM_INIT)
        tiles = tiles_of(fm, n, w)
        head_norms(nc, [(tiles(SP_Q + i), small[:, 1:2]) for i in range(2)] + [(tiles(SP_K + i), k.col("k_norm_sp")) for i in range(2)]
                   + [(tiles(DF_Q + i), small[:, 2:3]) for i in range(4)] + [(tiles(DF_K + i), k.col("k_norm_df")) for i in range(4)],
                   k.half_ones, HD, n, w)
        stick_breaking(nc, k, fm, v_tok, y)
        table = sbuf("table", [P, 8, TAB])
        penalty = sbuf("penalty", [P, QT2, T2])
        bias_tables(nc, k, A, scratch, table)
        select_keys(nc, k, fm, v_tok, penalty)
        groups = []
        for t in range(QT2):
            nq, nk = ROWS2[t], min((t + 1) * P, T2)
            cols = slice(t * P, t * P + nq)
            for head in range(4):
                rows = slice((head % 2) * HD, (head % 2) * HD + HD)
                groups.append(([Part(fm[rows, SP_Q + head // 2, cols], fm[rows, SP_K + head // 2, 0:nk],
                                     table[0:nq, head, OFF - t * P:OFF - t * P + nk],
                                     [v_tok[0:ROWS2[b], b, SP_V + head * HD:SP_V + (head + 1) * HD] for b in range(t + 1)],
                                     penalty=penalty[0:nq, t, 0:nk] if t >= 1 else None)], y[rows, 2 + head // 2, cols]))
            for head in range(4):
                members = []
                for m in range(2):
                    rows = slice(m * HD, (m + 1) * HD)
                    members.append(Part(fm[rows, DF_Q + head, cols], fm[rows, DF_K + head, 0:nk],
                                        table[0:nq, 4 + head, OFF - t * P:OFF - t * P + nk],
                                        [v_tok[0:ROWS2[b], b, DF_V + head * P:DF_V + (head + 1) * P] for b in range(t + 1)],
                                        gate=small[0:nq, 0:1] if m == 1 else None))
                groups.append((members, y[:, 4 + head, cols]))
        attend(nc, k, groups, wide=True)
        head_norms(nc, [(y[:, 4 + head, 0:T2], small[:, 3:4]) for head in range(4)], k.ones, P, n, w)


def second_block(nc, k, A, b, scratch):
    n, w = N2, W2
    x, h, merged = tiles_of(b.x, n, w), tiles_of(b.h, n, w), tiles_of(b.merged, n, w)
    norm, gate = k.at("attn_norm"), k.at("b_gate")
    rms_norm(nc, k, x, h, lambda t: k.vec[:, norm + t:norm + t + 1], None, n, w)
    second_attention(nc, k, A, h, b.y, scratch)
    for i, (at, ks) in enumerate([(0, 2), (2, 2), (4, 4)]):
        merge(nc, k, A[f"w_merge_2_{i}"], h, lambda t, at=at: b.y[:, at + t, 0:T2], ks, P, gate + i * KT, i == 0, b.merged, n, w)
    project(nc, A["w_out_2"], KT, [(merged, KT, P)], n, w, None,
            lambda dve, chain, i, acc, tmp: dve.tensor_tensor(tile_at(b.x, i, n, w), tile_at(b.x, i, n, w), acc(0), ALU.add), unroll=4)
    ffn = k.at("ffn_norm")
    rms_norm(nc, k, x, h, lambda t: k.vec[:, ffn + t:ffn + t + 1], None, n, w)
    feed_forward(nc, k, A["w_up_2"], A["w_down_2"], k.at("conv_w_2"), k.at("conv_b_2"), h, b.x, 0, n, w)


def lay_out_second(v, A):
    w = v["w_in_2"][0]
    widths = [256] * 6 + [256, 32, 8, 512, 512, 512, D, D, D]
    at = np.concatenate([[0], np.cumsum(widths)])
    part = lambda i: w[:, at[i]:at[i + 1]]
    A["w_fm_2"] = np.concatenate([tiled(part(0)), tiled(part(1)), tiled(part(3)), tiled(part(4)), tiled(part(6)),
                                  doubled(part(7), 32, 4), tiled(part(9)), tiled(part(10))])
    A["w_tok_2"] = by_k(np.concatenate([part(2), part(5), part(11), part(8)], axis=1))
    A["rel_bias"] = np.concatenate([v["rel_bias_2"], np.ones((1, 8), np.float32)])
    A["bucket"] = buckets()
    for i, name in enumerate(("w_br_sb_2", "w_br_sp_2", "w_br_df_2")):
        A[f"w_merge_2_{i}"] = beside(tiled(part(12 + i)), tiled(v[name][0]))
    A["w_out_2"] = tiled(v["w_out_2"][0])
    A["w_up_2"] = beside(tiled(v["w_up_2"][0][:, :D_FF]), tiled(v["w_up_2"][0][:, D_FF:]))
    A["w_down_2"] = tiled(v["w_down_2"][0])



FQ, FK, HQ, HF, HG_G, CA, CB, FF, FM3 = 0, 3, 6, 10, 14, 18, 20, 22, 23
FV, HV, TM3 = 0, FOX * HD, 2 * FOX * HD
LEVELS = [1, 2, 4, 8, 16, 32]
TILES3 = S // P
CHUNKS = S // CH


def forget_sums(nc, k, ff, sums):
    with stage(nc, "link", "ones_done", "log_done") as (sems, sbuf, psum, begin):
        dve_link, ones_done, log_done = sems
        a = sbuf("a", [FOX, 3, S])
        ones = sbuf("ones", [FOX, S])
        block = begin()

        @block.vector
        def _(dve):
            chain = Chain(dve, dve_link)
            dve.memset(ones[:, :], 1.0).then_inc(ones_done, 1)
            dve.wait_ge(ones_done, 1)
            chain.link(dve.tensor_scalar(a[:, 0, :], ff, k.one("fox_forget_b")[0:FOX], -1.0, ALU.add, ALU.mult))
            dve.wait_ge(log_done, 3)
            chain.link(dve.scalar_tensor_tensor(a[:, 2, :], a[:, 0, :], 0.0, a[:, 1, :], ALU.max, ALU.add))
            chain.link(dve.tensor_tensor_scan(sums, ones[:, :], a[:, 2, :], 0.0, ALU.mult, ALU.add))

        @block.scalar
        def _(act):
            act.wait_ge(dve_link, 1)
            chain = Chain(act, log_done)
            chain.link(act.activation(a[:, 1, :], a[:, 0, :], ACT.Abs))
            chain.link(act.activation(a[:, 1, :], a[:, 1, :], ACT.Exp, scale=-1.0))
            chain.link(act.activation(a[:, 1, :], a[:, 1, :], ACT.Ln, bias=1.0))


def hgrn(nc, k, A, fm, v_tok, yh):
    names = ["hf_done", "gate_link", "key_done", "sums_done", "apart_done", "decay_done", "factors_done", "pairs_ready", "pairs_taken",
             "last_done", "kd_done", "turned", "turned_copied", "update_ready", "state_done", "out_ready", "out_copied", "dve_link", "loaded", "pool_link"]
    with stage(nc, *names) as (sems, sbuf, psum, begin):
        (hf_done, gate_link, key_done, sums_done, apart_done, decay_done, factors_done, pairs_ready, pairs_taken,
         last_done, kd_done, turned, turned_copied, update_ready, state_done, out_ready, out_copied, dve_link, loaded, pool_link) = sems
        masks = sbuf("masks", [P, 1 + len(LEVELS), P], mybir.dt.uint32)
        log_part = sbuf("log_part", [P, 2, S])
        sums = sbuf("sums", [P, HG, S])
        key = sbuf("key", [P, HG, S])
        apart = sbuf("apart", [P, 2, S])
        decay = sbuf("decay", [P, 2, S])
        k_part = sbuf("k_part", [P, 2, S])
        q_part = sbuf("q_part", [P, 2, S])
        pairs = sbuf("pairs", [P, 2, TILES3, P])
        q_in = sbuf("q_in", [P, S])
        kd = sbuf("kd", [P, S])
        kd_tok = sbuf("kd_tok", [P, TILES3, P])
        last = sbuf("last", [P, CHUNKS])
        states = sbuf("states", [P, CHUNKS - 1, HG_V])
        pair_acc = psum("pair_acc", [P, 2, TILES3, P])
        turn_acc = psum("turn_acc", [P, TILES3, P])
        update = psum("update", [P, 2, 512])
        out = psum("out", [P, 2, 512])
        block = begin()
        NL = len(LEVELS)

        def halves(a, m):
            return a.rearrange("p (n a m) -> p n a m", a=2, m=m)

        def update_at(c):
            return update[:, c % 2, (c // 2) * HG_V:(c // 2 + 1) * HG_V]

        @block.sync
        def _(sp):
            sp.dma_start(masks[:, :, :], A["level_masks"]).then_inc(loaded, 16)

        @block.scalar
        def _(act):
            links = Chain(act, gate_link)
            for head in range(HG):
                hf = fm[:, HF + head, 0:S]
                if head >= 2:
                    act.wait_ge(sums_done, 2 * (head - 1))
                links.link(act.activation(log_part[:, head % 2, :], hf, ACT.Abs))
                links.link(act.activation(log_part[:, head % 2, :], log_part[:, head % 2, :], ACT.Exp, scale=-1.0))
                act.activation(log_part[:, head % 2, :], log_part[:, head % 2, :], ACT.Ln, bias=1.0).then_inc(hf_done, 1)
            for head in range(HG):
                act.activation(key[:, head, :], fm[:, HF + head, 0:S], ACT.Sigmoid, scale=-1.0).then_inc(key_done, 1)
            for head in range(HG):
                for l in range(NL):
                    i = head * NL + l
                    act.wait_ge(apart_done, 2 * (i + 1) + 2 * head)
                    if i >= 2:
                        act.wait_ge(factors_done, 2 * (i - 1))
                    act.activation(decay[:, i % 2, :], apart[:, i % 2, :], ACT.Exp).then_inc(decay_done, 1)
                act.wait_ge(apart_done, 2 * NL * (head + 1) + 2 * head + 2)
                act.activation(q_in[:, :], q_in[:, :], ACT.Exp, scale=-1.0).then_inc(last_done, 1)
                act.activation(last[:, :], sums[:, head, CH - 1:S:CH], ACT.Exp, scale=-1.0).then_inc(last_done, 1)
                act.activation(kd[:, :], kd[:, :], ACT.Exp).then_inc(last_done, 1)
                act.wait_ge(turned, head + 1)
                act.activation(kd_tok[:, :, :], turn_acc[:, :, :], ACT.Copy).then_inc(turned_copied, 1)
                act.wait_ge(out_ready, head + 1)
                act.activation(yh[0:HG_V, head, :], out[0:HG_V, head % 2, :], ACT.Copy).then_inc(out_copied, 1)

        @block.vector
        def _(dve):
            chain = Chain(dve, dve_link)
            dve.wait_ge(loaded, 16)
            for head in range(HG):
                hf = fm[:, HF + head, 0:S]
                dve.wait_ge(hf_done, head + 1)
                dve.scalar_tensor_tensor(log_part[:, head % 2, :], hf, 0.0, log_part[:, head % 2, :], ALU.min, ALU.subtract).then_inc(sums_done, 1)
                dve.wait_ge(sums_done, 2 * head + 1)
                dve.tensor_tensor_scan(sums[:, head, :], k.resets, log_part[:, head % 2, :], 0.0, ALU.mult, ALU.subtract).then_inc(sums_done, 1)
            dve.wait_ge(sums_done, 2 * HG)
            dve.wait_ge(key_done, HG)
            for head in range(HG):
                q = fm[:, HQ + head, 0:S]
                keys, b = key[:, head, :], sums[:, head, :]
                dve.wait_ge(pairs_ready, head * (NL + 1) + 1)
                if head >= 2:
                    dve.wait_ge(out_ready, head - 1)
                dve.tensor_tensor(pairs[:, head % 2], pair_acc[:, (head * (NL + 1)) % 2], masks[:, 0:1, :].to_broadcast([P, TILES3, P]),
                                  ALU.mult).then_inc(pairs_taken, 1)
                dve.wait_ge(pairs_taken, head * (NL + 1) + 1)

                def split(l):
                    i = head * NL + l
                    m = LEVELS[l]
                    if i >= 2:
                        dve.wait_ge(decay_done, i - 1)
                    to, of = halves(apart[:, i % 2, :], m), halves(b, m)
                    meet = of[:, :, 0, m - 1:m].to_broadcast([P, S // (2 * m), m])
                    dve.tensor_tensor(to[:, :, 0, :], of[:, :, 0, :], meet, ALU.subtract).then_inc(apart_done, 1)
                    dve.tensor_tensor(to[:, :, 1, :], meet, of[:, :, 1, :], ALU.subtract).then_inc(apart_done, 1)

                def factors(l):
                    i = head * NL + l
                    dve.wait_ge(decay_done, i + 1)
                    if i >= 2:
                        dve.wait_ge(pairs_ready, (i - 2) // NL * (NL + 1) + (i - 2) % NL + 2)
                    dve.tensor_tensor(k_part[:, i % 2, :], keys, decay[:, i % 2, :], ALU.mult).then_inc(factors_done, 1)
                    dve.tensor_tensor(q_part[:, i % 2, :], q, decay[:, i % 2, :], ALU.mult).then_inc(factors_done, 1)

                def take(l):
                    n = head * (NL + 1) + 1 + l
                    dve.wait_ge(pairs_ready, n + 1)
                    dve.copy_predicated(pairs[:, head % 2], masks[:, l + 1:l + 2, :].to_broadcast([P, TILES3, P]),
                                        pair_acc[:, n % 2]).then_inc(pairs_taken, 1)
                    dve.wait_ge(pairs_taken, n + 1)

                split(0)
                for l in range(NL):
                    if l + 1 < NL:
                        split(l + 1)
                    factors(l)
                    if l >= 1:
                        take(l - 1)
                take(NL - 1)

                if head >= 1:
                    dve.wait_ge(out_ready, head)
                dve.tensor_copy(q_in[:, :], b).then_inc(apart_done, 1)
                ends = b.rearrange("p (c t) -> p c t", t=CH)[:, :, CH - 1:CH].to_broadcast([P, CHUNKS, CH])
                dve.tensor_tensor(kd[:, :].rearrange("p (c t) -> p c t", t=CH), b.rearrange("p (c t) -> p c t", t=CH), ends,
                                  ALU.subtract).then_inc(apart_done, 1)
                dve.wait_ge(last_done, 3 * (head + 1))
                dve.tensor_tensor(q_in[:, :], q_in[:, :], q, ALU.mult).then_inc(kd_done, 1)
                dve.tensor_tensor(kd[:, :], kd[:, :], keys, ALU.mult).then_inc(kd_done, 1)
                dve.wait_ge(update_ready, head + 1)
                for c in range(CHUNKS - 1):
                    if c == 0:
                        ins = dve.tensor_copy(states[:, 0, :], update_at(0))
                    else:
                        ins = dve.scalar_tensor_tensor(states[:, c, :], states[:, c - 1, :], last[:, c:c + 1], update_at(c), ALU.mult, ALU.add)
                    ins.then_inc(state_done, 1)
                    dve.wait_ge(state_done, head * (CHUNKS - 1) + c + 1)

        @block.tensor
        def _(pe):
            pe.wait_ge(key_done, HG)
            for head in range(HG):
                q, keys = fm[:, HQ + head, 0:S], key[:, head, :]
                values = lambda t: v_tok[:, t, HV + head * HG_V:HV + (head + 1) * HG_V]
                for l in range(NL + 1):
                    n = head * (NL + 1) + l
                    if n >= 2:
                        pe.wait_ge(pairs_taken, n - 1)
                    if l >= 1:
                        i = head * NL + l - 1
                        pe.wait_ge(factors_done, 2 * (i + 1))
                        left, right = k_part[:, i % 2, :], q_part[:, i % 2, :]
                    else:
                        left, right = keys, q
                    for t in range(TILES3):
                        mm = pe.matmul(pair_acc[:, n % 2, t, :], left[:, t * P:(t + 1) * P], right[:, t * P:(t + 1) * P], start=True, stop=True)
                    mm.then_inc(pairs_ready, 1)
                pe.wait_ge(kd_done, 2 * (head + 1))
                if head >= 1:
                    pe.wait_ge(turned_copied, head)
                for t in range(TILES3):
                    mm = pe.transpose(turn_acc[:, t, :], kd[:, t * P:(t + 1) * P], k.ident)
                mm.then_inc(turned, 1)
                pe.wait_ge(turned_copied, head + 1)
                if head >= 1:
                    pe.wait_ge(state_done, head * (CHUNKS - 1))
                for c in range(CHUNKS - 1):
                    rows = slice((c % 2) * CH, (c % 2 + 1) * CH)
                    mm = pe.matmul(update_at(c), kd_tok[rows, c // 2, :], v_tok[rows, c // 2, HV + head * HG_V:HV + (head + 1) * HG_V],
                                   start=True, stop=True)
                mm.then_inc(update_ready, 1)
                if head >= 2:
                    pe.wait_ge(out_copied, head - 1)
                pe.wait_ge(pairs_taken, (head + 1) * (NL + 1))
                pe.wait_ge(state_done, (head + 1) * (CHUNKS - 1))
                for t in range(TILES3):
                    pe.matmul(out[0:HG_V, head % 2, t * P:(t + 1) * P], values(t), pairs[:, head % 2, t, :], start=True, stop=False)
                    for c in range(max(1, 2 * t), 2 * t + 2):
                        mm = pe.matmul(out[0:HG_V, head % 2, c * CH:(c + 1) * CH], states[:, c - 1, :], q_in[:, c * CH:(c + 1) * CH],
                                       start=False, stop=c == 2 * t + 1)
                mm.then_inc(out_ready, 1)


def conv_branch(nc, k, fm):
    tiles, back = 2, CONV_W - 1
    with stage(nc, "gate_done", "link", "conv_done", "summed", "centred", "squared", "var_ready", "root_done", "scaled", "done") as (sems, sbuf, psum, begin):
        gate_done, dve_link, conv_done, summed, centred, squared, var_ready, root_done, scaled, done = sems
        pad = sbuf("pad", [P, tiles, back + S])
        gate = sbuf("gate", [P, tiles, S])
        conv = sbuf("conv", [P, tiles, S])
        scale = sbuf("scale", [P, 2, S])
        acc = psum("acc", [P, 2, S])
        block = begin()

        @block.scalar
        def _(act):
            for t in range(tiles):
                act.activation(gate[:, t, :], fm[:, CB + t, 0:S], ACT.Sigmoid).then_inc(gate_done, 1)
            for t in range(tiles):
                act.wait_ge(centred, t + 1)
                act.activation(gate[:, t, :], conv[:, t, :], ACT.Square).then_inc(squared, 1)
            act.wait_ge(var_ready, 1)
            act.activation(scale[:, 1, :], scale[:, 0, :], ACT.Sqrt).then_inc(root_done, 1)
            for t in range(tiles):
                act.wait_ge(scaled, t + 1)
                act.activation(fm[:, CA + t, 0:S], conv[:, t, :], ACT.Silu, bias=k.one("dw_ln_b", t)).then_inc(done, 1)

        @block.vector
        def _(dve):
            chain = Chain(dve, dve_link)
            chain.link(dve.memset(pad[:, :, 0:back], 0.0))
            for t in range(tiles):
                dve.wait_ge(gate_done, t + 1)
                chain.link(dve.tensor_tensor(pad[:, t, back:back + S], fm[:, CA + t, 0:S], gate[:, t, :], ALU.mult))
            for i in range(CONV_W):
                for t in range(tiles):
                    tap = k.one("dw_w", i * tiles + t)
                    if i >= 1:
                        dve.wait_ge(conv_done, (i - 1) * tiles + t + 1)
                        ins = dve.scalar_tensor_tensor(conv[:, t, :], pad[:, t, i:i + S], tap, conv[:, t, :], ALU.mult, ALU.add)
                    else:
                        ins = dve.tensor_scalar(conv[:, t, :], pad[:, t, 0:S], tap, k.one("dw_b", t), ALU.mult, ALU.add)
                    ins.then_inc(conv_done, 1)
            dve.wait_ge(summed, 1)
            dve.wait_ge(conv_done, CONV_W * tiles)
            for t in range(tiles):
                dve.scalar_tensor_tensor(conv[:, t, :], acc[:, 0, :], -1.0 / (tiles * P), conv[:, t, :], ALU.mult, ALU.add).then_inc(centred, 1)
            dve.wait_ge(summed, 2)
            dve.tensor_scalar(scale[:, 0, :], acc[:, 1, :], 1.0 / (tiles * P), EPS, ALU.mult, ALU.add).then_inc(var_ready, 1)
            dve.wait_ge(root_done, 1)
            chain.link(dve.reciprocal(scale[:, 0, :], scale[:, 1, :]))
            dve.wait_ge(centred, tiles)
            for t in range(tiles):
                dve.scalar_tensor_tensor(conv[:, t, :], conv[:, t, :], k.one("dw_ln_g", t), scale[:, 0, :], ALU.mult, ALU.mult).then_inc(scaled, 1)

        @block.tensor
        def _(pe):
            for t in range(tiles):
                pe.wait_ge(conv_done, (CONV_W - 1) * tiles + t + 1)
                last = pe.matmul(acc[:, 0, :], k.ones, conv[:, t, :], start=t == 0, stop=t == tiles - 1)
            last.then_inc(summed, 1)
            for t in range(tiles):
                pe.wait_ge(squared, t + 1)
                last = pe.matmul(acc[:, 1, :], k.ones, gate[:, t, :], start=t == 0, stop=t == tiles - 1)
            last.then_inc(summed, 1)


def gate_heads(nc, yh, fm):
    with stage(nc, "silu_done", "gated") as ((silu_done, gated), sbuf, _, begin):
        silu = sbuf("silu", [P, HG, S])
        block = begin()

        @block.scalar
        def _(act):
            for head in range(HG):
                act.activation(silu[0:HG_V, head, :], fm[0:HG_V, HG_G + head, 0:S], ACT.Silu).then_inc(silu_done, 1)

        @block.vector
        def _(dve):
            for head in range(HG):
                dve.wait_ge(silu_done, head + 1)
                dve.tensor_tensor(yh[0:HG_V, head, :], yh[0:HG_V, head, :], silu[0:HG_V, head, :], ALU.mult).then_inc(gated, 1)


def third_block(nc, k, A, b):
    n, w = 1, S
    x, h, merged = tiles_of(b.x, n, w, META), tiles_of(b.h, n, w), tiles_of(b.merged, n, w)
    norm, gate = k.at("norm_mix_3"), k.at("gate_b_3")
    rms_norm(nc, k, x, h, lambda t: k.vec[:, norm + t:norm + t + 1], None, n, w)
    with ExitStack() as ctx:
        def sbuf(name, shape):
            return ctx.enter_context(nc.sbuf_tensor(f"{name}_{nc.next_id()}", shape, F32))

        fm = sbuf("fm", [P, FM3, S])
        v_tok = sbuf("v_tok", [P, TILES3, TM3])
        yh = sbuf("yh", [P, HG, S])
        small = sbuf("small", [P, 1])
        forgotten = sbuf("forgotten", [FOX, S])
        project(nc, A["w_fm_3"], FM3, [(h, KT, P)], n, w, copies(fm, n, w), unroll=4)
        project_tokens(nc, A["w_tok_3"], TM3, h, S,
                       lambda act, t, rows, c, width, acc: act.activation(v_tok[0:rows, t, c:c + width], acc, ACT.Copy))
        scale_columns(nc, small[:, 0:1], k.col("fox_q_norm"), Q_SCALE)
        tiles = tiles_of(fm, n, w)
        head_norms(nc, [(tiles(FQ + i), small[:, 0:1]) for i in range(3)] + [(tiles(FK + i), k.col("fox_k_norm")) for i in range(3)],
                   k.half_ones, HD, n, w)
        forget_sums(nc, k, fm[0:FOX, FF, 0:S], forgotten[:, :])
        groups = []
        for head in range(FOX):
            rows = slice((head % 2) * HD, (head % 2) * HD + HD)
            for t in range(TILES3):
                cols, nk = slice(t * P, (t + 1) * P), (t + 1) * P
                groups.append(([Part(fm[rows, FQ + head // 2, cols], fm[rows, FK + head // 2, 0:nk], k.causal[:, OFF - t * P:TAB],
                                     [v_tok[:, j, FV + head * HD:FV + (head + 1) * HD] for j in range(t + 1)],
                                     extra=(k.fox_rows[0:FOX, head * P:(head + 1) * P], forgotten[:, 0:nk]))],
                               b.y[rows, head // 2, cols]))
        attend(nc, k, groups, wide=False)
        hgrn(nc, k, A, fm, v_tok, yh)
        head_norms(nc, [(yh[0:HG_V, head, :], k.col("hgrn_norm")[0:HG_V]) for head in range(HG)], k.ones, HG_V, n, w, rows=HG_V)
        gate_heads(nc, yh, fm)
        conv_branch(nc, k, fm)
        merge(nc, k, A["w_merge_3_0"], h, tiles_of(b.y, n, w), 3, P, gate, True, b.merged, n, w)
        merge(nc, k, A["w_merge_3_1"], h, lambda t: yh[0:HG_V, t, :], HG, HG_V, gate + KT, False, b.merged, n, w)
        merge(nc, k, A["w_merge_3_2"], h, lambda t: fm[:, CA + t, 0:S], 2, P, gate + 2 * KT, False, b.merged, n, w)
    project(nc, A["w_out_3"], KT, [(merged, KT, P)], n, w, None,
            lambda dve, chain, i, acc, tmp: dve.tensor_tensor(tile_at(b.x, i, n, w, META), tile_at(b.x, i, n, w, META), acc(0), ALU.add), unroll=4)
    ffn = k.at("norm_ffn_3")
    rms_norm(nc, k, x, h, lambda t: k.vec[:, ffn + t:ffn + t + 1], None, n, w)
    feed_forward(nc, k, A["w_up_3"], A["w_down_3"], k.at("ffn_dw_w"), k.at("ffn_dw_b"), h, b.x, META, n, w)


def lay_out_third(v, A):
    w = v["w_in_3"][0]
    widths = [FOX * HD] * 3 + [FOX, 512, 512, HG * HG_V, HG * HG_V, 256, 256, 3 * D]
    at = np.concatenate([[0], np.cumsum(widths)])
    part = lambda i: w[:, at[i]:at[i + 1]]
    A["w_fm_3"] = np.concatenate([tiled(part(0)), tiled(part(1)), tiled(part(4)), tiled(part(5)), tiled(part(7), HG_V),
                                  tiled(part(8)), tiled(part(9)), tiled(part(3), FOX)])
    A["w_tok_3"] = by_k(np.concatenate([part(2), part(6)], axis=1))
    A["level_masks"] = level_masks()
    wb, gates = v["w_branch_3"][0], part(10)
    fox, hg = FOX * HD, HG * HG_V
    rows_of_head = np.zeros((HG, P, D), np.float32)
    rows_of_head[:, 0:HG_V] = wb[fox:fox + hg].reshape(HG, HG_V, D)
    branch = [wb[0:fox], rows_of_head.reshape(HG * P, D), wb[fox + hg:]]
    for i in range(3):
        A[f"w_merge_3_{i}"] = beside(tiled(gates[:, i * D:(i + 1) * D]), tiled(branch[i]))
    A["w_out_3"] = tiled(v["w_out_3"][0])
    A["w_up_3"] = beside(tiled(v["w_up_3"][0][:, :D_FF]), tiled(v["w_up_3"][0][:, D_FF:]))
    A["w_down_3"] = tiled(v["w_down_3"][0])



class Consts:

    def __init__(self, vec, places):
        self.vec, self.places = vec, places

    def at(self, name):
        return self.places[name][0]

    def col(self, name):
        a, n = self.places[name]
        return self.vec[:, a:a + n]

    def one(self, name, i=0):
        a = self.places[name][0] + i
        return self.vec[:, a:a + 1]


class Buffers:
    def __init__(self, x, h, y, merged):
        self.x, self.h, self.y, self.merged = x, h, y, merged


def build(nc, A, out, vec_places, const_places, scratch):
    with ExitStack() as ctx:
        def sbuf(name, shape):
            return ctx.enter_context(nc.sbuf_tensor(name, shape, F32))

        vec = sbuf("vec", [P, A["vec"].shape[1]])
        const = sbuf("const", [P, A["const"].shape[1]])
        k = Consts(vec, vec_places)

        def c(name):
            a, n = const_places[name]
            return const[:, a:a + n]
        k.ones, k.ident, k.mirror, k.half_ones, k.later = c("ones"), c("ident"), c("mirror"), c("half_ones"), c("later")
        k.distance, k.distance_cmp, k.sees_cmp, k.causal = c("distance"), c("distance_cmp"), c("sees_cmp"), c("causal")
        k.before, k.resets, k.fox_rows = c("before"), c("resets"), c("fox_rows")
        k.ada = sbuf("ada", [P, 3 * KT])
        b = Buffers(sbuf("x", [P, KT, T2]), sbuf("h", [P, KT, T2]), sbuf("y", [P, KT, T2]), sbuf("merged", [P, KT, T2]))
        with stage(nc, "loaded") as ((loaded,), _, _, begin):
            block = begin()

            @block.sync
            def _(sp):
                sp.dma_start(vec[:, :], A["vec"]).then_inc(loaded, 16)
                sp.dma_start(const[:, :], A["const"]).then_inc(loaded, 16)
                sp.dma_start(b.x[:, :, 0:META], A["meta"]).then_inc(loaded, 16)
                sp.dma_start(b.x[:, :, META:T2], A["x"]).then_inc(loaded, 16)
                sp.wait_ge(loaded, 64)
        first_block(nc, k, A, b)
        second_block(nc, k, A, b, scratch)
        third_block(nc, k, A, b)
        stored = nc.alloc_semaphore("stored")
        block = ctx.enter_context(nc.Block())

        @block.sync
        def _(sp):
            sp.dma_start(out, b.x[:, :, META:T2]).then_inc(stored, 16)
            sp.wait_ge(stored, 16)



def columns(v):
    return np.asarray(v).reshape(-1, P).T


def padded(v):
    out = np.zeros((P, 1), np.float32)
    out[:np.size(v), 0] = np.asarray(v).reshape(-1)
    return out


def tiled(w, cols=P):
    w = np.asarray(w)
    kt, nt = w.shape[0] // P, w.shape[1] // cols
    out = w.reshape(kt, P, nt, cols).transpose(2, 1, 0, 3)
    if cols < P:
        out = np.concatenate([out, np.zeros(out.shape[:3] + (P - cols,), np.float32)], axis=3)
    return out


def doubled(w, cols, times):
    t = tiled(w, cols)[..., :cols]
    return np.concatenate([t] * times, axis=3)


def beside(*tiles):
    return np.concatenate(tiles, axis=2)


def by_k(w):
    w = np.asarray(w)
    return w.reshape(-1, P, w.shape[1]).transpose(1, 0, 2)


def tokens_last(x):
    return np.asarray(x).T.reshape(KT, P, -1).transpose(1, 0, 2)


def shape_constants():
    p = np.arange(P)[:, None]
    rel = p - np.arange(TAB)[None, :] + OFF
    t = p + P * np.arange(S // P)[None, :]
    end = 16 * np.arange(N_CMP) + 31
    d = t[:, :, None] - end[None, None, :]
    c = np.arange(2 * T2 - 272) - 256
    same_half = (np.arange(P)[:, None] // HD) == (np.arange(P)[None, :] // HD)
    fox_rows = np.zeros((P, FOX, P))
    for i in range(FOX):
        fox_rows[i, i, :] = -1.0
    return {
        "ones": np.ones((P, P)), "ident": np.eye(P), "mirror": np.eye(P)[::-1], "half_ones": same_half,
        "later": np.arange(P)[:, None] >= np.arange(P)[None, :],
        "distance": np.where(rel >= 0, rel, FAR), "distance_cmp": np.where(d >= 0, d, FAR).reshape(P, -1),
        "sees_cmp": p >= 31, "causal": np.where(rel >= 0, 0.0, BIG),
        "before": (p < c[None, :]), "resets": np.broadcast_to(np.arange(S)[None, :] % CH != 0, (P, S)),
        "fox_rows": fox_rows.reshape(P, -1),
    }


def buckets():
    rel = OFF + P - 1 - np.arange(TAB + P - 1)
    n = np.maximum(rel, 0)
    nf = np.maximum(n, 1).astype(np.float32)
    large = 16 + (np.log(nf / np.float32(16)) / np.float32(math.log(8)) * np.float32(16)).astype(np.int32)
    bucket = np.where(n < 16, n, np.minimum(large, 31))
    out = np.zeros((33, rel.size), np.float32)
    out[bucket, np.arange(rel.size)] = -1.0
    out[:, rel < 0] = 0.0
    out[32, rel < 0] = BIG
    return out


def level_masks():
    s, t = np.arange(P)[:, None], np.arange(P)[None, :]
    out = [s == t]
    for m in (1, 2, 4, 8, 16, 32):
        out.append((s // (2 * m) == t // (2 * m)) & (s % (2 * m) < m) & (t % (2 * m) >= m))
    return np.stack(out, axis=1).astype(np.uint32)


def pack(named):
    places, parts, at = {}, [], 0
    for name, a in named.items():
        a = np.asarray(a, np.float32).reshape(P, -1)
        places[name] = (at, a.shape[1])
        parts.append(a)
        at += a.shape[1]
    return np.ascontiguousarray(np.concatenate(parts, axis=1)), places


def lay_out(v):
    A = {}
    v = {name: np.asarray(a) for name, a in v.items()}
    A["x"], A["meta"] = tokens_last(v["x"][0]), tokens_last(v["meta_tokens_2"])
    twice = lambda a: np.concatenate([a.reshape(-1), a.reshape(-1)])
    A["vec"], vec_places = pack({
        "c": columns(v["c"]), "b_ada": columns(v["b_ada"]), "g_pre": columns(v["g_pre"]), "g_post": columns(v["g_post"]),
        "conv_w": columns(v["conv_w"]), "conv_b": columns(v["conv_b"]),
        "attn_norm": columns(v["attn_norm_2"]), "b_gate": columns(v["b_gate_2"]), "ffn_norm": columns(v["ffn_norm_2"]),
        "conv_w_2": columns(v["conv_w_2"]), "conv_b_2": columns(v["conv_b_2"]),
        "q_norm_sp": padded(twice(v["q_norm_sp_2"])), "k_norm_sp": padded(twice(v["k_norm_sp_2"])),
        "q_norm_df": padded(twice(v["q_norm_df_2"])), "k_norm_df": padded(twice(v["k_norm_df_2"])),
        "lam": np.concatenate([padded(v[n]) for n in ("lam_q1_2", "lam_q2_2", "lam_k1_2", "lam_k2_2")], axis=1),
        "subln_df": padded(v["subln_df_2"]),
        "norm_mix_3": columns(v["norm_mix_g_3"]), "gate_b_3": columns(v["gate_b_3"]), "norm_ffn_3": columns(v["norm_ffn_g_3"]),
        "fox_forget_b": padded(v["fox_forget_b_3"]), "fox_q_norm": padded(twice(v["fox_q_norm_g_3"])),
        "fox_k_norm": padded(twice(v["fox_k_norm_g_3"])), "hgrn_norm": padded(v["hgrn_out_norm_g_3"]),
        "dw_w": np.concatenate([columns(v["conv_dw_w_3"][0][i]) for i in range(CONV_W)], axis=1), "dw_b": columns(v["conv_dw_b_3"]),
        "dw_ln_g": columns(v["conv_norm_g_3"]), "dw_ln_b": columns(v["conv_norm_b_3"]),
        "ffn_dw_w": columns(v["ffn_dw_w_3"]), "ffn_dw_b": columns(v["ffn_dw_b_3"]),
    })
    A["const"], const_places = pack(shape_constants())

    w = v["w_in"][0]
    cols = lambda a, n: w[:, a:a + n]
    ada = tiled(v["w_ada"][0])
    A["w_ada"] = ada.reshape(6, 4, P, KT, P).transpose(0, 2, 1, 3, 4).reshape(6, P, 4 * KT, P)
    A["w_conv"] = beside(*[tiled(cols(i * MIX, MIX)) for i in range(4)])
    B = 4 * MIX
    kv = lambda i: cols(B + MIX + i * 256, 256)
    z_at = B + MIX + 6 * 256
    A["w_q"] = tiled(cols(B, MIX))
    A["w_kv_cmp"] = np.concatenate([doubled(kv(0), HD, 2), doubled(kv(1), HD, 2)])
    A["w_keys"] = np.concatenate([doubled(kv(2), HD, 2), doubled(kv(4), HD, 2)])
    A["w_v_gates"] = by_k(np.concatenate([kv(3), kv(5), cols(z_at + MIX, 3 * NH)], axis=1))
    A["w_z"] = tiled(cols(z_at, MIX))
    A["w_cmp1"] = np.stack([v[n][0].reshape(32, HD, P).transpose(1, 0, 2) for n in ("w_ck1", "w_cv1")], axis=1)
    A["pos_cmp"] = np.stack([v[n][0].T for n in ("pos_ck", "pos_cv")], axis=1)
    A["w_cmp2"] = np.stack([np.concatenate([v[n][0]] * 2, axis=1) for n in ("w_ck2", "w_cv2")], axis=1)
    C = z_at + MIX + 3 * NH
    A["w_v"] = by_k(cols(C + MIX, MIX))
    A["w_uz"] = beside(tiled(cols(C, MIX)), tiled(cols(C + 2 * MIX, MIX)))
    A["w_s_t"], A["b_s"] = v["w_s"][0].transpose(2, 0, 1), v["b_s"]
    A["ln_g"], A["ln_b"] = v["ln_g"], v["ln_b"]
    G = C + 3 * MIX
    for i in range(3):
        A[f"w_merge{i}"] = beside(tiled(cols(G + i * D, D)), tiled(v["w_br"][0, i]))
    A["w_out"] = tiled(v["w_out"][0])
    lay_out_second(v, A)
    lay_out_third(v, A)
    return {name: np.ascontiguousarray(a) for name, a in A.items()}, vec_places, const_places


def kernel(**inputs):
    import concourse.bacc as bacc
    from concourse.bass_utils import run_bass_kernel_spmd

    arrays, vec_places, const_places = lay_out(inputs)
    nc = bacc.Bacc("TRN2", target_bir_lowering=False, num_devices=1)
    A = {name: nc.dram_tensor(f"in_{name}", a.shape, mybir.dt.from_np(a.dtype), kind="ExternalInput").ap() for name, a in arrays.items()}
    out = nc.dram_tensor("out", (P, KT, S), F32, kind="ExternalOutput").ap()
    scratch = nc.dram_tensor("bias_rows", (8, TAB + P - 1), F32, kind="Internal").ap()
    build(nc, A, out, vec_places, const_places, scratch)
    r = run_bass_kernel_spmd(nc, [{f"in_{name}": a for name, a in arrays.items()}], core_ids=[0])
    return r.results[0]["out"].transpose(1, 0, 2).reshape(D, S).T.reshape(1, S, D)
```

```python
import math
from contextlib import ExitStack, contextmanager

import numpy as np

import concourse.bass as bass
from concourse import mybir

F32 = mybir.dt.float32
F32R = mybir.dt.float32r
ALU = mybir.AluOpType
ACT = mybir.ActivationFunctionType
AX_X = mybir.AxisListType.X

P = 128
D = 1024
KT = D // P
S = 512
META = 16
T2 = META + S
HD = 64
EPS = 1e-6
BIG = 1e30
FAR = 1e33
Q_SCALE = -(HD ** -0.5)

MIX = 1024
NH, NKV = 16, 4
N_CMP = (S - 32) // 16 + 1
FF_PARTS = [(0, 16), (16, 22)]
TOP_K = min(256, T2 // 4)
D_FF = 2816
FFT = D_FF // P
LAM_INIT = 0.8 - 0.6 * math.exp(-0.3 * 0)
FOX = 6
HG = 4
HG_V = 96
CH = 64
CONV_W = 31

OFF = 512
TAB = OFF + P


class Chain:

    def __init__(self, eng, done, base=0):
        self.eng, self.done, self.base, self.n = eng, done, base, 0

    def link(self, ins):
        self.n += 1
        ins.then_inc(self.done, 1)
        self.eng.wait_ge(self.done, self.base + self.n)


@contextmanager
def stage(nc, *names):
    sems = [nc.alloc_semaphore(f"{n}_{nc.next_id()}") for n in names]
    with ExitStack() as ctx:
        def sbuf(name, shape, dtype=F32):
            return ctx.enter_context(nc.sbuf_tensor(f"{name}_{nc.next_id()}", shape, dtype))

        def psum(name, shape):
            return ctx.enter_context(nc.psum_tensor(f"{name}_{nc.next_id()}", shape, F32))

        with ExitStack() as inner:
            def begin():
                return inner.enter_context(nc.Block())
            yield sems, sbuf, psum, begin
    if sems:
        nc.clear_and_free_semaphores(sems)
        nc.all_engine_barrier()


RAW, CUT = 2, 4


class Halves:

    def __init__(self, hi, lo):
        self.hi, self.lo = hi, lo

    def tile(self, t, T, rows=P):
        return self.hi[0:rows, t, 0:T], self.lo[0:rows, t, 0:T]


class WeightStream:

    def __init__(self, nc, ctx, stream):
        self.stream, self.total = stream, stream.shape[0]
        self.raw = ctx.enter_context(nc.sbuf_tensor("weights_raw", [P, RAW, KT * P], F32))
        self.hi = ctx.enter_context(nc.sbuf_tensor("weights_hi", [P, CUT, KT * P], F32R))
        self.lo = ctx.enter_context(nc.sbuf_tensor("weights_lo", [P, CUT, KT * P], F32R))
        self.raw_in = [nc.alloc_semaphore(f"weights_raw_in{i}") for i in range(RAW)]
        self.hi_done = nc.alloc_semaphore("weights_hi_done")
        self.lo_done = nc.alloc_semaphore("weights_lo_done")
        self.used = nc.alloc_semaphore("weights_used")
        self.next = 0

    def take(self, n):
        first, self.next = self.next, self.next + n
        return first

    def load(self, sp, first, c, r=0, per=0):
        at = first + c
        if not per and at >= self.total:
            return
        if at >= RAW or per:
            sp.wait_ge(self.lo_done, at + r * per - RAW + 1)
        sp.dma_start(self.raw[:, at % RAW, :], self.stream[bass.ds(at + r * per, 1)].rearrange("a p m -> p (a m)")
                     ).then_inc(self.raw_in[at % RAW], 16)

    def round(self, act, first, c, r=0, per=0):
        at = first + c
        if not per and at >= self.total:
            return
        act.wait_ge(self.raw_in[at % RAW], 16 * (at // RAW + 1) + r * (per // RAW) * 16)
        if at >= CUT or per:
            act.wait_ge(self.used, at + r * per - CUT + 1)
        act.activation(self.hi[:, at % CUT, :], self.raw[:, at % RAW, :], ACT.Copy).then_inc(self.hi_done, 1)

    def rest(self, pool, first, c, r=0, per=0):
        at = first + c
        if not per and at >= self.total:
            return
        pool.wait_ge(self.hi_done, at + r * per + 1)
        pool.tensor_tensor(self.lo[:, at % CUT, :], self.raw[:, at % RAW, :], self.hi[:, at % CUT, :].bitcast(F32),
                           ALU.subtract).then_inc(self.lo_done, 1)

    def ready(self, pe, first, c, r=0, per=0):
        pe.wait_ge(self.lo_done, first + c + r * per + 1)
        return (first + c) % CUT

    def begin(self, nc):
        with stage(nc) as (_, _, _, begin):
            block = begin()

            @block.sync
            def _(sp):
                for c in range(RAW + CUT):
                    self.load(sp, 0, c)

            @block.scalar
            def _(act):
                for c in range(CUT):
                    self.round(act, 0, c)

            @block.gpsimd
            def _(pool):
                for c in range(CUT):
                    self.rest(pool, 0, c)


def rounds(eng, steps, unroll, body):
    full = steps // unroll
    if full:
        body(0, unroll, True)
    if full > 2:
        with eng.Fori(1, full) as r:
            body(r, unroll, False)
    elif full == 2:
        body(1, unroll, False)
    if steps % unroll:
        body(full, steps % unroll, full == 0)


class Round:

    def __init__(self, first, r, per):
        if isinstance(r, int):
            self.args = lambda c: (first + r * per, c)
        else:
            self.args = lambda c: (first, c, r, per)


def products(pe, accs, w, passes_of, n):
    for half in range(n):
        cols = slice(half * w, (half + 1) * w)
        for start, stop, w_hi, w_lo, x_hi, x_lo in passes_of:
            pe.matmul(accs[half], w_hi, x_hi[:, cols], start=start, stop=False)
            pe.matmul(accs[half], w_hi, x_lo[:, cols], start=False, stop=False)
            last = pe.matmul(accs[half], w_lo, x_hi[:, cols], start=False, stop=stop)
    return last


def project(nc, ws, steps, tiles, n, w, act_step=None, dve_step=None, unroll=2, act_links=0, dve_links=0, scratch=(),
            parts=None):
    per_step = sum((ks + KT - 1) // KT for _, ks, _ in tiles)
    per = per_step * unroll
    first = ws.take(per_step * steps)
    assert per % CUT == 0 or steps <= 2 * unroll
    with stage(nc, "act_done", "step_done", "act_link", "dve_link", "rest_done") as (sems, sbuf, psum, begin):
        act_done, step_done, act_link, dve_link, rest_done = sems
        tmp = {name: sbuf(name, [P, unroll] + shape) for name, shape in scratch}
        acc = psum("acc", [P, unroll, len(tiles) * n, 512])
        block = begin()

        def out_of(u, j):
            return acc[:, u, j * n:(j + 1) * n, 0:w]

        @block.sync
        def _(sp):
            def ahead(r, count, _):
                at = Round(first, r, per)
                for c in range(count * per_step):
                    ws.load(sp, *at.args(c + CUT + RAW))
            rounds(sp, steps, unroll, ahead)

        @block.gpsimd
        def _(pool):
            def ahead(r, count, _):
                at = Round(first, r, per)
                for u in range(count):
                    for c in range(u * per_step, (u + 1) * per_step):
                        ws.rest(pool, *at.args(c + CUT))
                    if parts is not None:
                        i = r * unroll + u
                        pool.wait_ge(step_done, i + 1)
                        full, hi, lo = parts
                        pool.tensor_tensor(lo(i), full(i, tmp, u), hi(i).bitcast(F32), ALU.subtract).then_inc(rest_done, 1)
            rounds(pool, steps, unroll, ahead)

        @block.tensor
        def _(pe):
            def multiply(r, count, start):
                at = Round(first, r, per)
                for u in range(count):
                    if not start:
                        pe.wait_ge(step_done, (r - 1) * unroll + u + 1)
                    c = u * per_step
                    for j, (source, ks, rows) in enumerate(tiles):
                        accs = [acc[:, u, j * n + half, 0:w] for half in range(n)]
                        for k0 in range(0, ks, KT):
                            slot = ws.ready(pe, *at.args(c))
                            passes = []
                            for k in range(k0, min(ks, k0 + KT)):
                                block_of = slice((k - k0) * P, (k - k0 + 1) * P)
                                passes.append((k == 0, k == ks - 1, ws.hi[0:rows, slot, block_of], ws.lo[0:rows, slot, block_of], *source(k)))
                            products(pe, accs, w, passes, n).then_inc(ws.used, 1)
                            c += 1
            rounds(pe, steps, unroll, multiply)

        @block.scalar
        def _(act):
            def finish(r, count, start):
                at = Round(first, r, per)
                for u in range(count):
                    i = r * unroll + u
                    for c in range(u * per_step, (u + 1) * per_step):
                        ws.round(act, *at.args(c + CUT))
                    if act_step is not None:
                        act.wait_ge(ws.used, first + (i + 1) * per_step)
                        chain = Chain(act, act_link, i * act_links)
                        last = act_step(act, chain, i, lambda j: out_of(u, j), {k: v[:, u] for k, v in tmp.items()})
                        last.then_inc(step_done if dve_step is None else act_done, 1)
                        assert chain.n == act_links
            rounds(act, steps, unroll, finish)

        if dve_step is not None:
            cuts = 0 if parts is None else 1

            @block.vector
            def _(dve):
                def finish(r, count, start):
                    for u in range(count):
                        i = r * unroll + u
                        if act_step is not None:
                            dve.wait_ge(act_done, i + 1)
                        else:
                            dve.wait_ge(ws.used, first + (i + 1) * per_step)
                        if parts is not None and not start:
                            dve.wait_ge(rest_done, (r - 1) * unroll + u + 1)
                        chain = Chain(dve, dve_link, i * (dve_links + cuts))
                        last = dve_step(dve, chain, i, lambda j: out_of(u, j), {k: v[:, u] for k, v in tmp.items()})
                        if parts is not None:
                            chain.link(last)
                            last = dve.tensor_copy(parts[1](i), parts[0](i, tmp, u))
                        last.then_inc(step_done, 1)
                        assert chain.n == dve_links + cuts, (chain.n, dve_links)
                rounds(dve, steps, unroll, finish)


def project_tokens(nc, ws, pairs, source, tok, epilogue):
    nt = (tok + P - 1) // P
    first = ws.take(2 * pairs)
    assert first % 2 == 0
    with stage(nc, "products_done", "taken") as (sems, sbuf, psum, begin):
        products_done, taken = sems
        acc = psum("acc", [P, 8, 512])
        block = begin()

        @block.sync
        def _(sp):
            for c in range(2 * pairs):
                ws.load(sp, first, c + CUT + RAW)

        @block.gpsimd
        def _(pool):
            for c in range(2 * pairs):
                ws.rest(pool, first, c + CUT)

        @block.tensor
        def _(pe):
            for p in range(pairs):
                slot = ws.ready(pe, first, 2 * p)
                ws.ready(pe, first, 2 * p + 1)
                for t in range(nt):
                    rows = min(P, tok - t * P)
                    i = p * nt + t
                    if i >= 8:
                        pe.wait_ge(taken, i - 7)
                    out = acc[0:rows, i % 8, 0:2 * P]
                    for k in range(KT):
                        x_hi, x_lo = (a[:, t * P:t * P + rows] for a in source(k))
                        w_hi, w_lo = (a[:, slot:slot + 2, k * P:(k + 1) * P] for a in (ws.hi, ws.lo))
                        pe.matmul(out, x_hi, w_hi, start=k == 0, stop=False)
                        pe.matmul(out, x_lo, w_hi, start=False, stop=False)
                        last = pe.matmul(out, x_hi, w_lo, start=False, stop=k == KT - 1)
                    if t < nt - 1:
                        last.then_inc(products_done, 1)
                last.then_inc(ws.used, 2)

        @block.scalar
        def _(act):
            for p in range(pairs):
                for t in range(nt):
                    rows = min(P, tok - t * P)
                    i = p * nt + t
                    if t < nt - 1:
                        act.wait_ge(products_done, p * (nt - 1) + t + 1)
                    else:
                        act.wait_ge(ws.used, first + 2 * p + 2)
                    epilogue(act, t, rows, p, acc[0:rows, i % 8, 0:2 * P]).then_inc(taken, 1)
                for c in range(2 * p, 2 * p + 2):
                    ws.round(act, first, c + CUT)


def rms_norm(nc, k, source, T, n, w, gain, shift=None, halves=None, dest=None):
    with stage(nc, "squared", "summed", "mean_done", "root_done", "scale_done", "scaled", "full_done", "hi_done", "lo_done", "added") as (sems, sbuf, psum, begin):
        squared, summed, mean_done, root_done, scale_done, scaled, full_done, hi_done, lo_done, added = sems
        sq = sbuf("sq", [P, 4, T])
        full = sbuf("full", [P, 4, T])
        scale = sbuf("scale", [P, 2, n, w])
        acc = psum("acc", [P, n, 512])
        block = begin()

        @block.scalar
        def _(act):
            for t in range(0, KT, 2):
                if t >= 4:
                    act.wait_ge(summed, t - 3)
                act.activation(sq[:, t % 4, :], source(t), ACT.Square).then_inc(squared, 1)
            act.wait_ge(mean_done, 1)
            act.activation(scale[:, 1], scale[:, 0], ACT.Sqrt).then_inc(root_done, 1)
            if halves is not None:
                for t in range(KT):
                    act.wait_ge(scaled, t + 1)
                    if shift is not None:
                        act.activation(full[:, t % 4, :], full[:, t % 4, :], ACT.Identity, bias=shift(t)).then_inc(full_done, 1)
                        act.wait_ge(full_done, t + 1)
                    act.activation(halves.hi[:, t, 0:T], full[:, t % 4, :], ACT.Copy).then_inc(hi_done, 1)

        @block.gpsimd
        def _(pool):
            if halves is not None:
                for t in range(0, KT, 2):
                    pool.wait_ge(hi_done, t + 1)
                    pool.tensor_tensor(halves.lo[:, t, 0:T], full[:, t % 4, :], halves.hi[:, t, 0:T].bitcast(F32),
                                       ALU.subtract).then_inc(lo_done, 1)

        @block.tensor
        def _(pe):
            for t in range(KT):
                if t % 2 == 0:
                    pe.wait_ge(squared, t // 2 + 1)
                else:
                    pe.wait_ge(added, t // 2 + 1)
                for half in range(n):
                    last = pe.matmul(acc[:, half, 0:w], k.ones, sq[:, t % 4, half * w:(half + 1) * w], start=t == 0, stop=t == KT - 1)
                last.then_inc(summed, 1)

        @block.vector
        def _(dve):
            for t in range(1, KT, 2):
                if t >= 4:
                    dve.wait_ge(summed, t - 3)
                dve.tensor_tensor(sq[:, t % 4, :], source(t), source(t), ALU.mult).then_inc(added, 1)
            dve.wait_ge(summed, KT)
            dve.tensor_scalar(scale[:, 0], acc[:, :, 0:w], 1.0 / D, EPS, ALU.mult, ALU.add).then_inc(mean_done, 1)
            dve.wait_ge(root_done, 1)
            dve.reciprocal(scale[:, 0], scale[:, 1]).then_inc(scale_done, 1)
            dve.wait_ge(scale_done, 1)

            def rest(t):
                dve.wait_ge(hi_done, t + 1)
                dve.tensor_tensor(halves.lo[:, t, 0:T], full[:, t % 4, :], halves.hi[:, t, 0:T].bitcast(F32), ALU.subtract).then_inc(added, 1)

            for t in range(KT):
                if halves is not None and t >= 4:
                    if t % 2 == 0:
                        dve.wait_ge(lo_done, t // 2 - 1)
                    else:
                        dve.wait_ge(added, KT // 2 + (t - 3) // 2)
                ins = dve.scalar_tensor_tensor(full[:, t % 4, :], source(t), gain(t), scale[:, 0].rearrange("p a b -> p (a b)"), ALU.mult, ALU.mult)
                ins.then_inc(scaled, 1)
                if dest is not None:
                    dve.wait_ge(scaled, t + 1)
                    dve.tensor_tensor(dest(t), dest(t), full[:, t % 4, :], ALU.add).then_inc(added, 1)
                    if t >= 3:
                        dve.wait_ge(added, KT // 2 + t - 2)
                elif t >= 2 and t % 2 == 0:
                    rest(t - 1)
            if dest is None:
                rest(KT - 1)


def cut_tiles(nc, tiles):
    with stage(nc, "hi_done", "lo_done") as ((hi_done, lo_done), _, _, begin):
        block = begin()

        @block.scalar
        def _(act):
            for full, hi, lo in tiles:
                act.activation(hi, full, ACT.Copy).then_inc(hi_done, 1)

        @block.vector
        def _(dve):
            for i, (full, hi, lo) in enumerate(tiles):
                if i % 3 < 2:
                    dve.wait_ge(hi_done, i + 1)
                    dve.tensor_tensor(lo, full, hi.bitcast(F32), ALU.subtract).then_inc(lo_done, 1)

        @block.gpsimd
        def _(pool):
            for i, (full, hi, lo) in enumerate(tiles):
                if i % 3 == 2:
                    pool.wait_ge(hi_done, i + 1)
                    pool.tensor_tensor(lo, full, hi.bitcast(F32), ALU.subtract).then_inc(lo_done, 1)


def head_norms(nc, heads, ones, dim, n, w, rows=P):
    with stage(nc, "squared", "summed", "mean_done", "root_done", "inverted", "done") as (sems, sbuf, psum, begin):
        squared, summed, mean_done, root_done, inverted, done = sems
        sq = sbuf("sq", [P, 2, n * w])
        scale = sbuf("scale", [P, 2, 2, n * w])
        acc = psum("acc", [P, 2, n, 512])
        block = begin()

        def flat(a):
            return a.rearrange("p (a b) -> p a b", a=n)

        @block.scalar
        def _(act):
            for i in range(len(heads) + 1):
                if i < len(heads):
                    if i >= 2:
                        act.wait_ge(summed, i - 1)
                    act.activation(sq[0:rows, i % 2], heads[i][0], ACT.Square).then_inc(squared, 1)
                if i >= 1:
                    act.wait_ge(mean_done, i)
                    act.activation(scale[0:rows, (i - 1) % 2, 1], scale[0:rows, (i - 1) % 2, 0], ACT.Sqrt).then_inc(root_done, 1)

        @block.tensor
        def _(pe):
            for i in range(len(heads)):
                pe.wait_ge(squared, i + 1)
                if i >= 2:
                    pe.wait_ge(mean_done, i - 1)
                for half in range(n):
                    last = pe.matmul(acc[0:rows, i % 2, half, 0:w], ones[0:rows, 0:rows],
                                     sq[0:rows, i % 2, half * w:(half + 1) * w], start=True, stop=True)
                last.then_inc(summed, 1)

        @block.vector
        def _(dve):
            for i, (tile, gain) in enumerate(heads):
                dve.wait_ge(summed, i + 1)
                if i >= 2:
                    dve.wait_ge(done, i - 1)
                dve.tensor_scalar(flat(scale[0:rows, i % 2, 0]), acc[0:rows, i % 2, :, 0:w], 1.0 / dim, EPS,
                                  ALU.mult, ALU.add).then_inc(mean_done, 1)
                dve.wait_ge(root_done, i + 1)
                dve.reciprocal(scale[0:rows, i % 2, 0], scale[0:rows, i % 2, 1]).then_inc(inverted, 1)
                dve.wait_ge(inverted, i + 1)
                dve.scalar_tensor_tensor(tile, tile, gain, scale[0:rows, i % 2, 0], ALU.mult, ALU.mult).then_inc(done, 1)


class Part:

    def __init__(self, q, keys, table, values, gate=None, gate_const=None, extra=None, penalty=None):
        self.q, self.keys, self.table, self.values = q, keys, table, values
        self.gate, self.gate_const, self.extra, self.penalty = gate, gate_const, extra, penalty
        self.nq, self.nk = q.shape[1], keys.shape[1]
        self.blocks = [(c, min(P, self.nk - c)) for c in range(0, self.nk, P)]


def attend(nc, k, groups, wide, longest=T2, build_tables=None, build_every=0):
    lag = 1 if wide else 2
    ns = lag + 1
    parts, of = [], []
    for g, (members, out) in enumerate(groups):
        for m, part in enumerate(members):
            parts.append(part)
            of.append((g, m == 0, m == len(members) - 1))
    N = len(parts)
    last_of = [max(i for i in range(N) if of[i][0] == g) for g in range(len(groups))]
    with stage(nc, "scores_ready", "max_ready", "exp_done", "row_inverted", "diag_ready", "turned", "turned_read",
               "weighted", "out_read", "biased", "built") as (sems, sbuf, psum, begin):
        scores_ready, max_ready, exp_done, row_inverted, diag_ready, turned, turned_read, weighted, out_read, biased, built = sems
        width = 1024 if wide else 512
        biased_scores = sbuf("biased_scores", [P, ns, longest])
        probs = sbuf("probs", [P, ns, longest])
        penalties = any(part.penalty is not None for part in parts)
        bias_sum = sbuf("bias_sum", [P, longest]) if penalties else None
        diag = sbuf("diag", [P, ns, P])
        probs_t = sbuf("probs_t", [P, 2, 512])
        low = sbuf("low", [P, ns, 1])
        row_sum = sbuf("row_sum", [P, ns, 1])
        row_inv = sbuf("row_inv", [P, ns, 1])
        scores = psum("scores", [P, ns, width])
        turn = psum("turn", [P, 2, 512])
        out_acc = psum("out_acc", [P, 2, 512])
        block = begin()

        def turn_block(i, b, kb):
            nq = parts[i].nq
            return turn[0:kb, i % 2, b * nq:(b + 1) * nq]

        def out_at(g, part, out):
            base = out.start_partition()
            return out_acc[base:base + out.shape[0], g % 2, 0:part.nq]

        if build_tables is not None:
            @block.gpsimd
            def _(pool):
                for i in range(0, len(groups), build_every):
                    if i >= 2 * build_every:
                        pool.wait_ge(max_ready, last_of[i - build_every - 1] + 1)
                    build_tables(pool, i // build_every).then_inc(built, 1)

        @block.tensor
        def _(pe):
            for i in range(N + lag + 1):
                if i < N:
                    part = parts[i]
                    if i >= ns:
                        pe.wait_ge(max_ready, i - ns + 1)
                    for c in range(0, part.nk, 512):
                        e = min(part.nk, c + 512)
                        last = pe.matmul(scores[0:part.nq, i % ns, c:e], part.q, part.keys[:, c:e],
                                         start=True, stop=part.extra is None)
                        if part.extra is not None:
                            last = pe.matmul(scores[0:part.nq, i % ns, c:e], part.extra[0][:, 0:part.nq], part.extra[1][:, c:e],
                                             start=False, stop=True)
                    last.then_inc(scores_ready, 1)
                if lag <= i < N + lag:
                    j = i - lag
                    part = parts[j]
                    pe.wait_ge(diag_ready, j + 1)
                    if j >= 2:
                        pe.wait_ge(turned_read, j - 1)
                    for b, (c, kb) in enumerate(part.blocks):
                        last = pe.matmul(turn_block(j, b, kb), probs[0:part.nq, j % ns, c:c + kb],
                                         diag[0:part.nq, j % ns, 0:part.nq], start=True, stop=True)
                    last.then_inc(turned, 1)
                if i >= lag + 1:
                    j = i - lag - 1
                    part = parts[j]
                    g, opens, closes = of[j]
                    pe.wait_ge(turned_read, j + 1)
                    if opens and g >= 2:
                        pe.wait_ge(out_read, g - 1)
                    for b, (c, kb) in enumerate(part.blocks):
                        last = pe.matmul(out_at(g, part, groups[g][1]), part.values[b], probs_t[0:kb, j % 2, b * part.nq:(b + 1) * part.nq],
                                         start=opens and b == 0, stop=closes and b == len(part.blocks) - 1)
                    last.then_inc(weighted, 1)

        @block.vector
        def _(dve):
            n_biased = 0
            for i in range(N + 1):
                if i < N:
                    part = parts[i]
                    table = part.table
                    if build_tables is not None and of[i][1] and of[i][0] % build_every == 0:
                        dve.wait_ge(built, of[i][0] // build_every + 1)
                    if part.penalty is not None:
                        if i >= 1:
                            dve.wait_ge(max_ready, i)
                        n_biased += 1
                        dve.tensor_tensor(bias_sum[0:part.nq, 0:part.nk], part.table, part.penalty, ALU.add).then_inc(biased, 1)
                        dve.wait_ge(biased, n_biased)
                        table = bias_sum[0:part.nq, 0:part.nk]
                    dve.wait_ge(scores_ready, i + 1)
                    if i >= ns:
                        dve.wait_ge(exp_done, i - ns + 1)
                    dve.tensor_tensor_reduce(biased_scores[0:part.nq, i % ns, 0:part.nk], scores[0:part.nq, i % ns, 0:part.nk], table,
                                             1.0, 3e38, ALU.add, ALU.min, low[0:part.nq, i % ns, :]).then_inc(max_ready, 1)
                if i >= 1:
                    j = i - 1
                    part = parts[j]
                    dve.wait_ge(exp_done, j + 1)
                    dve.reciprocal(row_inv[0:part.nq, j % ns, :], row_sum[0:part.nq, j % ns, :]).then_inc(row_inverted, 1)
                    dve.wait_ge(row_inverted, j + 1)
                    if j >= ns:
                        dve.wait_ge(turned, j - ns + 1)
                    d = diag[0:part.nq, j % ns, 0:part.nq]
                    if part.gate is not None:
                        dve.tensor_scalar(d, k.ident[0:part.nq, 0:part.nq], row_inv[0:part.nq, j % ns, :], part.gate,
                                          ALU.mult, ALU.mult).then_inc(diag_ready, 1)
                    else:
                        dve.tensor_scalar(d, k.ident[0:part.nq, 0:part.nq], row_inv[0:part.nq, j % ns, :], None,
                                          ALU.mult).then_inc(diag_ready, 1)

        @block.scalar
        def _(act):
            def copy_out(g):
                part, out = parts[last_of[g]], groups[g][1]
                act.wait_ge(weighted, last_of[g] + 1)
                act.activation(out, out_at(g, part, out), ACT.Copy).then_inc(out_read, 1)

            g_next = 0
            for i in range(N + lag + 1):
                if i < N:
                    part = parts[i]
                    act.wait_ge(max_ready, i + 1)
                    if i >= ns:
                        act.wait_ge(turned, i - ns + 1)
                    act.activation(probs[0:part.nq, i % ns, 0:part.nk], biased_scores[0:part.nq, i % ns, 0:part.nk], ACT.Exp,
                                   bias=low[0:part.nq, i % ns, :], scale=-1.0,
                                   accum_out=row_sum[0:part.nq, i % ns, :]).then_inc(exp_done, 1)
                if lag <= i < N + lag:
                    j = i - lag
                    part = parts[j]
                    act.wait_ge(turned, j + 1)
                    if j >= 2:
                        act.wait_ge(weighted, j - 1)
                    rows = part.blocks[0][1]
                    full = [b for b in part.blocks if b[1] == rows]
                    rest = part.blocks[len(full):]
                    last = act.activation(probs_t[0:rows, j % 2, 0:len(full) * part.nq], turn[0:rows, j % 2, 0:len(full) * part.nq], ACT.Copy)
                    for b, (c, kb) in enumerate(rest, len(full)):
                        last = act.activation(probs_t[0:kb, j % 2, b * part.nq:(b + 1) * part.nq], turn_block(j, b, kb), ACT.Copy)
                    last.then_inc(turned_read, 1)
                while g_next < len(groups) and last_of[g_next] <= i - lag - 2:
                    copy_out(g_next)
                    g_next += 1
            while g_next < len(groups):
                copy_out(g_next)
                g_next += 1


def tiles_of(buffer, n, w, offset=0):
    return lambda t: buffer[:, t, offset:offset + n * w]


def tile_at(buffer, i, n, w, offset=0):
    return buffer[:, bass.ds(i, 1), offset:offset + n * w].rearrange("p a (n w) -> p (a n) w", n=n)


def merge(nc, k, ws, h, y, ks, rows, bias_at, first, merged, n, w, out=None):
    def gate(act, chain, i, acc, tmp):
        bias = 0.0 if bias_at is None else k.vec[:, bass.ds(bias_at + i, 1)]
        return act.activation(tmp["gate"], acc(0), ACT.Sigmoid, bias=bias)

    def combine(dve, chain, i, acc, tmp):
        if first:
            return dve.tensor_tensor(tile_at(merged, i, n, w), tmp["gate"], acc(1), ALU.mult)
        chain.link(dve.tensor_tensor(tmp["gate"], tmp["gate"], acc(1), ALU.mult))
        return dve.tensor_tensor(tile_at(merged, i, n, w), tile_at(merged, i, n, w), tmp["gate"], ALU.add)

    parts = None
    if out is not None:
        parts = (lambda i, tmp, u: tile_at(merged, i, n, w), lambda i: tile_at(out.hi, i, n, w), lambda i: tile_at(out.lo, i, n, w))
    project(nc, ws, KT, [(h, KT, P), (y, ks, rows)], n, w, gate, combine, unroll=4 if n == 1 else 2,
            dve_links=0 if first else 1, scratch=[("gate", [n, w])], parts=parts)


def feed_forward(nc, k, ws, conv_w, conv_b, h, x, off, n, w):
    T, U = n * w, 2
    for f0, f1 in FF_PARTS:
        with ExitStack() as ctx:
            hidden = halves_of(nc, ctx, "hidden", f1 - f0, T)
            steps, per = f1 - f0, 2 * U
            first = ws.take(2 * steps)
            with stage(nc, "gate_copied", "conv_done", "silu_done", "step_done", "dve_link", "rest_done") as (sems, sbuf, psum, begin):
                gate_copied, conv_done, silu_done, step_done, dve_link, rest_done = sems
                gate_pad = sbuf("gate_pad", [P, U, 2 + T])
                conv = sbuf("conv", [P, U, T])
                full = sbuf("full", [P, U, n, w])
                acc = psum("acc", [P, U, 2, n, 512])
                block = begin()

                @block.sync
                def _(sp):
                    def ahead(r, count, _):
                        at = Round(first, r, per)
                        for c in range(count * 2):
                            ws.load(sp, *at.args(c + CUT + RAW))
                    rounds(sp, steps, U, ahead)

                @block.gpsimd
                def _(pool):
                    def ahead(r, count, _):
                        at = Round(first, r, per)
                        for u in range(count):
                            for c in range(2 * u, 2 * u + 2):
                                ws.rest(pool, *at.args(c + CUT))
                            i = r * U + u
                            pool.wait_ge(step_done, i + 1)
                            pool.tensor_tensor(tile_at(hidden.lo, i, n, w), full[:, u], tile_at(hidden.hi, i, n, w).bitcast(F32),
                                               ALU.subtract).then_inc(rest_done, 1)
                    rounds(pool, steps, U, ahead)

                @block.tensor
                def _(pe):
                    def multiply(r, count, start):
                        at = Round(first, r, per)
                        for u in range(count):
                            if not start:
                                pe.wait_ge(step_done, (r - 1) * U + u + 1)
                            for j in range(2):
                                slot = ws.ready(pe, *at.args(2 * u + j))
                                passes = [(t == 0, t == KT - 1, ws.hi[:, slot, t * P:(t + 1) * P], ws.lo[:, slot, t * P:(t + 1) * P], *h(t))
                                          for t in range(KT)]
                                products(pe, [acc[:, u, j, half, 0:w] for half in range(n)], w, passes, n).then_inc(ws.used, 1)
                    rounds(pe, steps, U, multiply)

                @block.scalar
                def _(act):
                    def finish(r, count, start):
                        at = Round(first, r, per)
                        for u in range(count):
                            i = r * U + u
                            for c in range(2 * u, 2 * u + 2):
                                ws.round(act, *at.args(c + CUT))
                            act.wait_ge(ws.used, first + 2 * (i + 1))
                            act.activation(gate_pad[:, u, 2:2 + T].rearrange("p (n w) -> p n w", n=n), acc[:, u, 0, :, 0:w],
                                           ACT.Copy).then_inc(gate_copied, 1)
                            act.wait_ge(conv_done, i + 1)
                            act.activation(conv[:, u, :], conv[:, u, :], ACT.Silu).then_inc(silu_done, 1)
                    rounds(act, steps, U, finish)

                @block.vector
                def _(dve):
                    pads = Chain(dve, dve_link)
                    pads.link(dve.memset(gate_pad[:, :, 0:2], 0.0))

                    def finish(r, count, start):
                        for u in range(count):
                            i = r * U + u
                            chain = Chain(dve, dve_link, 1 + i * 3)
                            taps = [k.vec[:, bass.ds(conv_w + FFT * tap + f0 + i, 1)] for tap in range(3)]
                            dve.wait_ge(gate_copied, i + 1)
                            chain.link(dve.tensor_scalar(conv[:, u, :], gate_pad[:, u, 0:T], taps[0],
                                                         k.vec[:, bass.ds(conv_b + f0 + i, 1)], ALU.mult, ALU.add))
                            chain.link(dve.scalar_tensor_tensor(conv[:, u, :], gate_pad[:, u, 1:1 + T], taps[1], conv[:, u, :], ALU.mult, ALU.add))
                            dve.scalar_tensor_tensor(conv[:, u, :], gate_pad[:, u, 2:2 + T], taps[2], conv[:, u, :],
                                                     ALU.mult, ALU.add).then_inc(conv_done, 1)
                            dve.wait_ge(silu_done, i + 1)
                            if not start:
                                dve.wait_ge(rest_done, (r - 1) * U + u + 1)
                            chain.link(dve.tensor_tensor(full[:, u], conv[:, u, :].rearrange("p (n w) -> p n w", n=n), acc[:, u, 1, :, 0:w], ALU.mult))
                            dve.tensor_copy(tile_at(hidden.hi, i, n, w), full[:, u]).then_inc(step_done, 1)
                    rounds(dve, steps, U, finish)

            project(nc, ws, KT, [(lambda t: hidden.tile(t, T), f1 - f0, P)], n, w, None,
                    lambda dve, chain, i, acc, tmp: dve.tensor_tensor(tile_at(x, i, n, w, off), tile_at(x, i, n, w, off), acc(0), ALU.add),
                    unroll=4)


def halves_of(nc, ctx, name, tiles, T):
    return Halves(*(ctx.enter_context(nc.sbuf_tensor(f"{name}_{part}_{nc.next_id()}", [P, tiles, T], F32R)) for part in ("hi", "lo")))


def parts_of(halves, name, n, w):
    return (lambda i, tmp, u: tmp[name][:, u], lambda i: tile_at(halves.hi, i, n, w), lambda i: tile_at(halves.lo, i, n, w))


def copies(dest, n, w, scale=1.0, at=0):
    return lambda act, chain, i, acc, tmp: act.activation(tile_at(dest, i + at, n, w), acc(0), ACT.Copy, scale=scale)



def modulation(nc, k, A):
    tiles, ring_size = 3 * KT, 8
    with stage(nc, "c_ready", "products_done", "ada_link", *[f"weights_in{u}" for u in range(ring_size)]) as (sems, sbuf, psum, begin):
        c_ready, products_done, ada_link = sems[:3]
        weights_in = sems[3:]
        ring = sbuf("weight_ring", [P, ring_size, KT, P])
        c_silu = sbuf("c_silu", [P, KT])
        acc = psum("acc", [P, tiles])
        block = begin()

        @block.sync
        def _(sp):
            for i in range(tiles):
                if i >= ring_size:
                    sp.wait_ge(products_done, i - ring_size + 1)
                sp.dma_start(ring[:, i % ring_size], A["w_ada"][i]).then_inc(weights_in[i % ring_size], 16)

        @block.scalar
        def _(act):
            act.activation(c_silu[:, :], k.col("c"), ACT.Silu).then_inc(c_ready, 1)

        @block.tensor
        def _(pe):
            pe.wait_ge(c_ready, 1)
            for i in range(tiles):
                pe.wait_ge(weights_in[i % ring_size], 16 * (i // ring_size + 1))
                for t in range(KT):
                    last = pe.matmul(acc[:, i:i + 1], ring[:, i % ring_size, t, :], c_silu[:, t:t + 1], start=t == 0, stop=t == KT - 1)
                last.then_inc(products_done, 1)

        @block.vector
        def _(dve):
            chain = Chain(dve, ada_link)
            dve.wait_ge(products_done, tiles)
            chain.link(dve.tensor_tensor(k.ada[:, :], acc[:, :], k.col("b_ada"), ALU.add))
            chain.link(dve.scalar_tensor_tensor(k.ada[:, KT:2 * KT], k.ada[:, KT:2 * KT], 1.0, k.col("g_pre"), ALU.add, ALU.mult))
            chain.link(dve.tensor_tensor(k.ada[:, 2 * KT:], k.ada[:, 2 * KT:], k.col("g_post"), ALU.mult))


def conv_mixer(nc, k, ws, h, y):
    cw, cb = k.at("conv_w"), k.at("conv_b")

    def ahead(act, chain, i, acc, tmp):
        act.activation(tmp["xin"], acc(2), ACT.Copy)
        return act.activation(tmp["z"], acc(3), ACT.Silu)

    def mix(dve, chain, i, acc, tmp):
        pad, conv = tmp["pad"], tmp["conv"]
        chain.link(dve.memset(pad[:, 0:2], 0.0))
        chain.link(dve.tensor_tensor(pad[:, 2:2 + S].unsqueeze(1), acc(1), tmp["xin"], ALU.mult))
        taps = [k.vec[:, bass.ds(cw + KT * tap + i, 1)] for tap in range(3)]
        chain.link(dve.tensor_scalar(conv, pad[:, 0:S], taps[0], k.vec[:, bass.ds(cb + i, 1)], ALU.mult, ALU.add))
        chain.link(dve.scalar_tensor_tensor(conv, pad[:, 1:1 + S], taps[1], conv, ALU.mult, ALU.add))
        chain.link(dve.scalar_tensor_tensor(conv, pad[:, 2:2 + S], taps[2], conv, ALU.mult, ALU.add))
        chain.link(dve.tensor_tensor(conv.unsqueeze(1), conv.unsqueeze(1), acc(0), ALU.mult))
        return dve.tensor_tensor(tmp["z"], conv.unsqueeze(1), tmp["z"], ALU.mult)

    project(nc, ws, KT, [(h, KT, P)] * 4, 1, S, ahead, mix, dve_links=6,
            scratch=[("xin", [1, S]), ("z", [1, S]), ("pad", [2 + S]), ("conv", [S])], parts=parts_of(y, "z", 1, S))


def compress(nc, k, A, kv, k_cmp, v_cmp):
    with stage(nc, "loaded", "hidden_ready", "pos_copied", "hidden_done", "out_ready", "copied") as (sems, sbuf, psum, begin):
        loaded, hidden_ready, pos_copied, hidden_done, out_ready, copied = sems
        w1 = sbuf("w1", [HD, 2, 32, P])
        pos = sbuf("pos", [HD, 2, 32])
        w2 = sbuf("w2", [P, 2, P])
        pos_term = sbuf("pos_term", [P, 2])
        hidden = sbuf("hidden", [P, 2, NKV * N_CMP])
        acc = psum("acc", [P, 2, 512])
        pos_acc = psum("pos_acc", [P, 2, 512])
        out = psum("out", [P, 2, 512])
        block = begin()

        @block.sync
        def _(sp):
            sp.dma_start(w1[:, :, :, :], A["w_cmp1"]).then_inc(loaded, 16)
            sp.dma_start(pos[:, :, :], A["pos_cmp"]).then_inc(loaded, 16)
            sp.dma_start(w2[:, :, :], A["w_cmp2"]).then_inc(loaded, 16)

        @block.tensor
        def _(pe):
            pe.wait_ge(loaded, 48)
            for a in range(2):
                for s in range(32):
                    pe.matmul(acc[:, a, 0:NKV * N_CMP].rearrange("p (g n) -> p g n", g=NKV), w1[:, a, s, :],
                              kv[0:HD, a * NKV:(a + 1) * NKV, s:s + 16 * (N_CMP - 1) + 1:16], start=s == 0, stop=s == 31)
                for s in range(32):
                    last = pe.matmul(pos_acc[:, a, 0:1], w1[:, a, s, :], pos[:, a, s:s + 1], start=s == 0, stop=s == 31)
                last.then_inc(hidden_ready, 1)
            pe.wait_ge(hidden_done, 1)
            pe.matmul(out[:, 0, 0:NKV * N_CMP], w2[:, 0, :], hidden[:, 0, :], start=True, stop=True).then_inc(out_ready, 1)
            pe.wait_ge(hidden_done, 2)
            for g in range(NKV):
                last = pe.matmul(out[0:N_CMP, 1, g * HD:(g + 1) * HD], hidden[:, 1, g * N_CMP:(g + 1) * N_CMP], w2[:, 1, 0:HD],
                                 start=True, stop=True)
            last.then_inc(out_ready, 1)

        @block.vector
        def _(dve):
            for a in range(2):
                dve.wait_ge(hidden_ready, a + 1)
                dve.tensor_copy(pos_term[:, a:a + 1], pos_acc[:, a, 0:1]).then_inc(pos_copied, 1)
            dve.wait_ge(out_ready, 1)
            dve.tensor_copy(k_cmp[:, :], out[:, 0, 0:NKV * N_CMP]).then_inc(copied, 1)
            dve.wait_ge(out_ready, 2)
            dve.tensor_copy(v_cmp[0:N_CMP, :], out[0:N_CMP, 1, 0:NKV * HD]).then_inc(copied, 1)

        @block.scalar
        def _(act):
            for a in range(2):
                act.wait_ge(pos_copied, a + 1)
                act.activation(hidden[:, a, :], acc[:, a, 0:NKV * N_CMP], ACT.Silu, bias=pos_term[:, a:a + 1]).then_inc(hidden_done, 1)


def sparse_mixer(nc, k, A, ws, h, branch):
    y = branch.enter_context(nc.sbuf_tensor(f"y_{nc.next_id()}", [P, KT, S], F32))
    with ExitStack() as ctx:
        def sbuf(name, shape):
            return ctx.enter_context(nc.sbuf_tensor(f"{name}_{nc.next_id()}", shape, F32))

        q = sbuf("q_t", [P, KT, S])
        k_cmp = sbuf("k_cmp", [P, NKV * N_CMP])
        v_cmp = sbuf("v_cmp", [N_CMP, NKV * HD])
        project(nc, ws, KT, [(h, KT, P)], 1, S, copies(q, 1, S, Q_SCALE), unroll=4)
        with nc.sbuf_tensor(f"kv_cmp_{nc.next_id()}", [P, 2 * NKV, S], F32) as kv:
            project(nc, ws, 2 * NKV, [(h, KT, P)], 1, S, copies(kv, 1, S), unroll=4)
            compress(nc, k, A, kv, k_cmp, v_cmp)
        keys = sbuf("keys_t", [P, 2 * NKV, S])
        v_tok = sbuf("v_tok", [P, S // P, 2 * NKV * HD])
        gates = sbuf("gates", [P, S // P, 3 * NH])
        project(nc, ws, 2 * NKV, [(h, KT, P)], 1, S, copies(keys, 1, S), unroll=4)

        def take(act, t, rows, p, acc):
            if p < 2:
                return act.activation(v_tok[0:rows, t, p * 2 * P:(p + 1) * 2 * P], acc, ACT.Copy)
            return act.activation(gates[0:rows, t, :], acc[:, 0:3 * NH], ACT.Sigmoid)

        project_tokens(nc, ws, 3, h, S, take)
        distance = sbuf("distance", [P, TAB])
        distance_cmp = sbuf("distance_cmp", [P, 4 * N_CMP])
        with stage(nc, "hidden", "loaded") as ((hidden, loaded), _, _, begin):
            block = begin()

            @block.sync
            def _(sp):
                sp.dma_start(distance[:, :], A["distance"]).then_inc(loaded, 16)
                sp.dma_start(distance_cmp[:, :], A["distance_cmp"]).then_inc(loaded, 16)
                sp.wait_ge(loaded, 32)

            @block.vector
            def _(dve):
                first = gates[:, 0, 0:3 * NH:3]
                dve.tensor_scalar(first, first, k.sees_cmp, None, ALU.mult).then_inc(hidden, 1)

        table = sbuf("alibi", [P, 2, TAB])
        table_cmp = sbuf("alibi_cmp", [P, 2, 4 * N_CMP])
        slopes = [float(np.float32(2.0) ** np.float32(-8.0 * i / NH)) for i in range(1, NH + 1)]

        def build_tables(pool, head):
            pool.tensor_scalar(table_cmp[:, head % 2, :], distance_cmp[:, :], slopes[head], None, ALU.mult)
            return pool.tensor_scalar(table[:, head % 2, :], distance[:, :], slopes[head], None, ALU.mult)

        groups = []
        for head in range(NH):
            base, g = (head % 2) * HD, head // (NH // NKV)
            rows = slice(base, base + HD)
            for t in range(S // P):
                cols = slice(t * P, (t + 1) * P)
                qb = q[rows, head // 2, cols]
                members = [Part(qb, k_cmp[rows, g * N_CMP:(g + 1) * N_CMP], table_cmp[:, head % 2, t * N_CMP:(t + 1) * N_CMP],
                                [v_cmp[0:N_CMP, g * HD:(g + 1) * HD]], gate=gates[:, t, 3 * head:3 * head + 1])]
                for kind in range(2):
                    c = (kind * NKV + g) * HD
                    members.append(Part(qb, keys[rows, kind * NKV + g, 0:(t + 1) * P], table[:, head % 2, OFF - t * P:TAB],
                                        [v_tok[:, b, c:c + HD] for b in range(t + 1)],
                                        gate=gates[:, t, 3 * head + 1 + kind:3 * head + 2 + kind]))
                groups.append((members, y[rows, head // 2, cols]))
        attend(nc, k, groups, wide=False, longest=S, build_tables=build_tables, build_every=S // P)

    out = halves_of(nc, branch, "y", KT, S)
    project(nc, ws, KT, [(h, KT, P)], 1, S,
            lambda act, chain, i, acc, tmp: act.activation(tmp["z"], acc(0), ACT.Silu),
            lambda dve, chain, i, acc, tmp: dve.tensor_tensor(tile_at(y, i, 1, S), tile_at(y, i, 1, S), tmp["z"], ALU.mult),
            unroll=4, scratch=[("z", [1, S])],
            parts=(lambda i, tmp, u: tile_at(y, i, 1, S), lambda i: tile_at(out.hi, i, 1, S), lambda i: tile_at(out.lo, i, 1, S)))
    return out


def gmlp_mixer(nc, k, A, ws, h, y):
    chunks = S // P
    with ExitStack() as ctx:
        mixed = ctx.enter_context(nc.sbuf_tensor(f"mixed_{nc.next_id()}", [P, KT, S], F32))
        inner = ctx.enter_context(ExitStack())
        v_tok = inner.enter_context(nc.sbuf_tensor(f"v_tok_{nc.next_id()}", [P, chunks, MIX], F32))
        project_tokens(nc, ws, MIX // (2 * P), h, S,
                       lambda act, t, rows, p, acc: act.activation(v_tok[0:rows, t, p * 2 * P:(p + 1) * 2 * P], acc, ACT.Gelu_apprx_tanh))
        with stage(nc, "loaded", "mask_done", "var_ready", "root_done", "normed", "mixed_ready", "taken", "dve_link") as (sems, sbuf, psum, begin):
            loaded, mask_done, var_ready, root_done, normed, mixed_ready, taken, dve_link = sems
            w_s = sbuf("w_s", [P, KT, P])
            b_s = sbuf("b_s", [1, KT, P])
            ln = sbuf("ln", [P, 2, MIX])
            stats = sbuf("stats", [P, 2, 6])
            moments = sbuf("moments", [P, chunks, 2])
            root = sbuf("root", [P, chunks, 2])
            acc = psum("acc", [P, 2, chunks, P])
            block = begin()

            @block.sync
            def _(sp):
                sp.dma_start(w_s[:, :, :], A["w_s_t"]).then_inc(loaded, 16)
                sp.dma_start(b_s[:, :, :], A["b_s"]).then_inc(loaded, 16)
                sp.dma_start(ln[:, 0, :], A["ln_g"].partition_broadcast(P)).then_inc(loaded, 16)
                sp.dma_start(ln[:, 1, :], A["ln_b"].partition_broadcast(P)).then_inc(loaded, 16)

            @block.gpsimd
            def _(pool):
                pool.wait_ge(loaded, 64)
                pool.affine_select(w_s[:, :, :], w_s[:, :, :], pattern=[[0, KT], [1, P]], compare_op=ALU.is_ge, fill=0.0, base=0,
                                   channel_multiplier=-1).then_inc(mask_done, 1)

            @block.vector
            def _(dve):
                chain = Chain(dve, dve_link)
                for t in range(chunks):
                    chain.link(dve.bn_stats(stats[:, 0, :], v_tok[:, t, 0:512]))
                    chain.link(dve.bn_stats(stats[:, 1, :], v_tok[:, t, 512:1024]))
                    chain.link(dve.bn_aggr(moments[:, t, :], stats[:, :, :]))
                    dve.tensor_scalar(root[:, t, 0:1], moments[:, t, 1:2], EPS, None, ALU.add).then_inc(var_ready, 1)
                dve.wait_ge(loaded, 64)
                for t in range(chunks):
                    dve.wait_ge(root_done, t + 1)
                    chain.link(dve.reciprocal(root[:, t, 0:1], root[:, t, 1:2]))
                    chain.link(dve.tensor_scalar(v_tok[:, t, :], v_tok[:, t, :], moments[:, t, 0:1], root[:, t, 0:1], ALU.subtract, ALU.mult))
                    chain.link(dve.tensor_tensor(v_tok[:, t, :], v_tok[:, t, :], ln[:, 0, :], ALU.mult))
                    dve.tensor_tensor(v_tok[:, t, :], v_tok[:, t, :], ln[:, 1, :], ALU.add).then_inc(normed, 1)

            @block.scalar
            def _(act):
                for t in range(chunks):
                    act.wait_ge(var_ready, t + 1)
                    act.activation(root[:, t, 1:2], root[:, t, 0:1], ACT.Sqrt).then_inc(root_done, 1)
                for g in range(KT):
                    act.wait_ge(mixed_ready, g + 1)
                    act.activation(mixed[:, g, :], acc[:, g % 2].rearrange("p n i -> p (n i)"), ACT.Copy).then_inc(taken, 1)

            @block.tensor
            def _(pe):
                pe.wait_ge(mask_done, 1)
                pe.wait_ge(normed, chunks)
                for g in range(KT):
                    if g >= 2:
                        pe.wait_ge(taken, g - 1)
                    for t in range(chunks):
                        pe.matmul(acc[:, g % 2, t, :], v_tok[:, t, g * P:(g + 1) * P], w_s[:, g, :], start=True, stop=False)
                        last = pe.matmul(acc[:, g % 2, t, :], k.ones[0:1, :], b_s[0:1, g, :], start=False, stop=True)
                    last.then_inc(mixed_ready, 1)

        inner.close()

        def ahead(act, chain, i, acc, tmp):
            act.activation(tmp["u"], acc(0), ACT.Gelu_apprx_tanh)
            return act.activation(tmp["z"], acc(1), ACT.Silu)

        def mix(dve, chain, i, acc, tmp):
            chain.link(dve.tensor_tensor(tmp["u"], tmp["u"], tile_at(mixed, i, 1, S), ALU.mult))
            return dve.tensor_tensor(tmp["u"], tmp["u"], tmp["z"], ALU.mult)

        project(nc, ws, KT, [(h, KT, P)] * 2, 1, S, ahead, mix, dve_links=1, scratch=[("u", [1, S]), ("z", [1, S])],
                parts=parts_of(y, "u", 1, S))


def first_block(nc, k, A, ws, b):
    n, w = 1, S
    x = tiles_of(b.x, n, w, META)
    modulation(nc, k, A)
    with ExitStack() as ctx:
        halves = halves_of(nc, ctx, "h", KT, S)
        h = lambda t: halves.tile(t, S)
        rms_norm(nc, k, x, S, n, w, lambda t: k.ada[:, KT + t:KT + t + 1], lambda t: k.ada[:, t:t + 1], halves=halves)
        merged = ctx.enter_context(nc.sbuf_tensor(f"merged_{nc.next_id()}", [P, KT, S], F32))
        with ExitStack() as branch:
            y = sparse_mixer(nc, k, A, ws, h, branch)
            merge(nc, k, ws, h, lambda t: y.tile(t, S), KT, P, None, True, merged, n, w)
        with ExitStack() as branch:
            y = halves_of(nc, branch, "y", KT, S)
            conv_mixer(nc, k, ws, h, y)
            merge(nc, k, ws, h, lambda t: y.tile(t, S), KT, P, None, False, merged, n, w)
            gmlp_mixer(nc, k, A, ws, h, y)
            out = halves_of(nc, branch, "merged", KT, S)
            merge(nc, k, ws, h, lambda t: y.tile(t, S), KT, P, None, False, merged, n, w, out)
            project(nc, ws, KT, [(lambda t: out.tile(t, S), KT, P)], n, w, copies(merged, n, w), unroll=4)
        rms_norm(nc, k, tiles_of(merged, n, w), S, n, w, lambda t: k.ada[:, 2 * KT + t:2 * KT + t + 1], dest=x)



SB_Q, SP_Q, DF_Q, QM2 = 0, 2, 4, 8
SB_K, SP_K, IX_Q, IX_K, DF_K, FM2 = 0, 2, 4, 6, 7, 11
SB_V, SP_V, DF_V, IX_W, TM2 = 0, 256, 512, 1024, 1032
N2, W2 = 2, T2 // 2
QT2 = (T2 + P - 1) // P
ROWS2 = [min(P, T2 - t * P) for t in range(QT2)]
REPLACED = -3e38
PAD = -2e30


def stick_breaking(nc, k, A, qm, fm, v_tok):
    scale = HD ** -0.5
    units = [(head, half) for head in range(4) for half in range(N2)]
    kbs = {half: [kb for kb in reversed(range(QT2)) if kb * P < (half + 1) * W2] for half in range(N2)}
    steps = [(u, head, half, kb) for u, (head, half) in enumerate(units) for kb in kbs[half]]
    N = len(steps)
    first_of = {u: min(i for i in range(N) if steps[i][0] == u) for u in range(len(units))}
    last_of = {u: max(i for i in range(N) if steps[i][0] == u) for u in range(len(units))}
    names = ["scores_ready", "scaled_done", "abs_done", "exp_done", "log_done", "scores_masked", "soft_masked", "sums_ready", "exponent_ready",
             "weights_done", "out_ready", "out_copied", "act_link", "dve_link", "hidden", "loaded"]
    with stage(nc, *names) as (sems, sbuf, psum, begin):
        (scores_ready, scaled_done, abs_done, exp_done, log_done, scores_masked, soft_masked, sums_ready, exponent_ready, weights_done, out_ready,
         out_copied, act_link, dve_link, hidden, loaded) = sems
        before = sbuf("before", list(A["before"].shape))
        hide = sbuf("hide", list(A["before"].shape))
        scaled = sbuf("scaled", [P, 2, W2])
        masked = sbuf("masked", [P, 2, W2])
        soft = sbuf("soft", [P, 2, QT2, W2])
        log_part = sbuf("log_part", [P, 2, W2])
        relu_part = sbuf("relu_part", [P, W2])
        weight = sbuf("weight", [P, 2, W2])
        scores = psum("scores", [P, 2, 512])
        sums = psum("sums", [P, 2, 512])
        out = psum("out", [P, 2, 512])
        block = begin()

        @block.sync
        def _(sp):
            sp.dma_start(before[:, :], A["before"]).then_inc(loaded, 16)

        def window(half, kb):
            c = half * W2 - kb * P + 256
            return slice(c, c + W2)

        @block.tensor
        def _(pe):
            def score(i):
                u, head, half, kb = steps[i]
                rows = slice((head % 2) * HD, (head % 2) * HD + HD)
                if i >= 2:
                    pe.wait_ge(abs_done, i - 1)
                pe.matmul(scores[0:ROWS2[kb], i % 2, 0:W2], fm[rows, SB_K + head // 2, kb * P:kb * P + ROWS2[kb]],
                          qm[rows, SB_Q + head // 2, half * W2:(half + 1) * W2], start=True, stop=True).then_inc(scores_ready, 1)

            def add_up(i):
                u, head, half, kb = steps[i]
                pe.wait_ge(soft_masked, i + 1)
                if i >= 2:
                    pe.wait_ge(exponent_ready, i - 1)
                after = [b for b in kbs[half] if b > kb]
                for b in after:
                    pe.matmul(sums[0:ROWS2[kb], i % 2, 0:W2], k.ones[0:ROWS2[b], 0:ROWS2[kb]], soft[0:ROWS2[b], u % 2, b, :],
                              start=b == after[0], stop=False)
                pe.matmul(sums[0:ROWS2[kb], i % 2, 0:W2], k.later[0:ROWS2[kb], 0:ROWS2[kb]], soft[0:ROWS2[kb], u % 2, kb, :],
                          start=not after, stop=True).then_inc(sums_ready, 1)

            def weigh(i):
                u, head, half, kb = steps[i]
                base = (head % 2) * HD
                pe.wait_ge(weights_done, i + 1)
                if i == first_of[u] and u >= 2:
                    pe.wait_ge(out_copied, u - 1)
                last = pe.matmul(out[base:base + HD, u % 2, 0:W2], v_tok[0:ROWS2[kb], kb, SB_V + head * HD:SB_V + (head + 1) * HD],
                                 weight[0:ROWS2[kb], i % 2, :], start=i == first_of[u], stop=i == last_of[u])
                last.then_inc(out_ready, 1)

            for i in range(N + 2):
                if i < N:
                    score(i)
                if 1 <= i <= N:
                    add_up(i - 1)
                if i >= 2:
                    weigh(i - 2)

        @block.scalar
        def _(act):
            chain = Chain(act, act_link)
            for i in range(N + 2):
                if i < N:
                    u, head, half, kb = steps[i]
                    r = ROWS2[kb]
                    act.wait_ge(scores_ready, i + 1)
                    if i >= 2:
                        act.wait_ge(soft_masked, i - 1)
                    act.activation(scaled[0:r, i % 2, :], scores[0:r, i % 2, 0:W2], ACT.Copy, scale=scale).then_inc(scaled_done, 1)
                    act.activation(log_part[0:r, i % 2, :], scores[0:r, i % 2, 0:W2], ACT.Abs, scale=scale).then_inc(abs_done, 1)
                    act.wait_ge(abs_done, i + 1)
                    chain.link(act.activation(log_part[0:r, i % 2, :], log_part[0:r, i % 2, :], ACT.Exp, scale=-1.0))
                    act.activation(log_part[0:r, i % 2, :], log_part[0:r, i % 2, :], ACT.Ln, bias=1.0).then_inc(log_done, 1)
                if i >= 1 and i <= N:
                    j = i - 1
                    r = ROWS2[steps[j][3]]
                    act.wait_ge(exponent_ready, j + 1)
                    act.activation(weight[0:r, j % 2, :], masked[0:r, j % 2, :], ACT.Exp).then_inc(weights_done, 1)
                if i >= 2:
                    j = i - 2
                    u, head, half, kb = steps[j]
                    if j == last_of[u]:
                        rows = slice((head % 2) * HD, (head % 2) * HD + HD)
                        act.wait_ge(out_ready, j + 1)
                        act.activation(qm[rows, SB_Q + head // 2, half * W2:(half + 1) * W2], out[rows, u % 2, 0:W2], ACT.Copy).then_inc(out_copied, 1)

        @block.vector
        def _(dve):
            chain = Chain(dve, dve_link)
            dve.wait_ge(loaded, 16)
            dve.tensor_scalar(hide[:, :], before[:, :], 1.0, BIG, ALU.subtract, ALU.mult).then_inc(hidden, 1)
            dve.wait_ge(hidden, 1)
            for i in range(N + 1):
                if i < N:
                    u, head, half, kb = steps[i]
                    r = ROWS2[kb]
                    dve.wait_ge(scaled_done, i + 1)
                    if i >= 2:
                        dve.wait_ge(weights_done, i - 1)
                    chain.link(dve.tensor_tensor(masked[0:r, i % 2, :], scaled[0:r, i % 2, :], hide[0:r, window(half, kb)], ALU.add))
                    dve.wait_ge(log_done, i + 1)
                    chain.link(dve.scalar_tensor_tensor(relu_part[0:r, :], scaled[0:r, i % 2, :], 0.0, log_part[0:r, i % 2, :],
                                                        ALU.max, ALU.add))
                    if i == first_of[u] and u >= 2:
                        dve.wait_ge(sums_ready, last_of[u - 2] + 1)
                    dve.tensor_tensor(soft[0:r, u % 2, kb, :], relu_part[0:r, :], before[0:r, window(half, kb)], ALU.mult).then_inc(soft_masked, 1)
                    dve.wait_ge(soft_masked, i + 1)
                if i >= 1:
                    j = i - 1
                    r = ROWS2[steps[j][3]]
                    dve.wait_ge(sums_ready, j + 1)
                    dve.tensor_tensor(masked[0:r, j % 2, :], masked[0:r, j % 2, :], sums[0:r, j % 2, 0:W2], ALU.subtract).then_inc(exponent_ready, 1)


def select_keys(nc, k, fm, v_tok, penalty):
    heads = 8
    full_rounds, rest = divmod(TOP_K, 8)
    jobs = [(t, j) for t in range(1, QT2) for j in range(heads)]
    with stage(nc, "dots_ready", "relu_done", "added", "link") as (sems, sbuf, psum, begin):
        dots_ready, relu_done, added, dve_link = sems
        relu = sbuf("relu", [P, 2, T2])
        score = sbuf("score", [P, T2 + 8])
        top = sbuf("top", [P, 8])
        dots = psum("dots", [P, 2, 1024])
        block = begin()

        def keys_of(t):
            return min((t + 1) * P, T2)

        @block.tensor
        def _(pe):
            for i, (t, j) in enumerate(jobs):
                rows = slice((j % 4) * 32, (j % 4) * 32 + 32)
                if i >= 2:
                    pe.wait_ge(relu_done, i - 1)
                for c in range(0, keys_of(t), 512):
                    e = min(c + 512, keys_of(t))
                    last = pe.matmul(dots[0:ROWS2[t], i % 2, c:e], fm[rows, IX_Q + j // 4, t * P:t * P + ROWS2[t]], fm[rows, IX_K, c:e],
                                     start=True, stop=True, tile_position=((j % 4) * 32, 0))
                last.then_inc(dots_ready, 1)

        @block.scalar
        def _(act):
            for i, (t, j) in enumerate(jobs):
                act.wait_ge(dots_ready, i + 1)
                if i >= 2:
                    act.wait_ge(added, i - 1)
                act.activation(relu[0:ROWS2[t], i % 2, 0:keys_of(t)], dots[0:ROWS2[t], i % 2, 0:keys_of(t)], ACT.Relu).then_inc(relu_done, 1)

        @block.vector
        def _(dve):
            chain = Chain(dve, dve_link)
            for i, (t, j) in enumerate(jobs):
                r, nk = ROWS2[t], keys_of(t)
                s = score[0:r, 0:nk]
                weight = v_tok[0:r, t, IX_W + j:IX_W + j + 1]
                dve.wait_ge(relu_done, i + 1)
                if j == 0:
                    ins = dve.tensor_scalar(s, relu[0:r, i % 2, 0:nk], weight, None, ALU.mult)
                else:
                    ins = dve.scalar_tensor_tensor(s, relu[0:r, i % 2, 0:nk], weight, s, ALU.mult, ALU.add)
                ins.then_inc(added, 1)
                dve.wait_ge(added, i + 1)
                if j < heads - 1:
                    continue
                chain.link(dve.tensor_tensor(s, s, k.causal[0:r, OFF - t * P:OFF - t * P + nk], ALU.subtract))
                chain.link(dve.memset(score[0:r, nk:nk + 8], PAD))
                s = score[0:r, 0:nk + 8]
                for n in range(full_rounds + (rest > 0)):
                    chain.link(dve.max(top[0:r, :], s))
                    if n == full_rounds:
                        chain.link(dve.memset(top[0:r, rest:8], PAD))
                    chain.link(dve.match_replace(s, top[0:r, :], s, REPLACED))
                chain.link(dve.tensor_scalar(penalty[0:r, t, 0:nk], score[0:r, 0:nk], REPLACED, BIG, ALU.not_equal, ALU.mult))


def bias_tables(nc, k, A, scratch, table):
    with stage(nc, "loaded", "rows_ready", "rows_copied", "rows_stored", "tables_in0", "tables_in1", "turned", "turned_copied") as (sems, sbuf, psum, begin):
        loaded, rows_ready, rows_copied, rows_stored = sems[:4]
        tables_in, (turned, turned_copied) = sems[4:6], sems[6:]
        width = TAB + P - 1
        by_bucket = sbuf("by_bucket", [33, 8])
        bucket = sbuf("bucket", [33, width])
        rows = sbuf("rows", [8, width])
        flipped = sbuf("flipped", [P, 2, TAB])
        acc = psum("acc", [8, 2, 512])
        turn = psum("turn", [P, 2, 2, 512])
        block = begin()
        half = (width + 1) // 2
        spans = [(0, half), (half, width)]

        @block.sync
        def _(sp):
            sp.dma_start(by_bucket[:, :], A["rel_bias"]).then_inc(loaded, 16)
            sp.dma_start(bucket[:, :], A["bucket"]).then_inc(loaded, 16)
            sp.wait_ge(rows_copied, 2)
            sp.dma_start(scratch, rows[:, :]).then_inc(rows_stored, 16)
            sp.wait_ge(rows_stored, 16)
            for head in range(8):
                if head >= 2:
                    sp.wait_ge(turned, head - 1)
                src = bass.AP(tensor=scratch.tensor, offset=head * width, ap=[[1, P], [1, TAB]])
                sp.dma_start(flipped[:, head % 2, :], src).then_inc(tables_in[head % 2], 16)

        @block.tensor
        def _(pe):
            pe.wait_ge(loaded, 32)
            for i, (a, e) in enumerate(spans):
                pe.matmul(acc[:, i, 0:e - a], by_bucket[:, :], bucket[:, a:e], start=True, stop=True).then_inc(rows_ready, 1)
            for head in range(8):
                pe.wait_ge(tables_in[head % 2], 16 * (head // 2 + 1))
                if head >= 2:
                    pe.wait_ge(turned_copied, head - 1)
                for i in range(2):
                    last = pe.matmul(turn[:, head % 2, i, 0:TAB // 2], k.mirror, flipped[:, head % 2, i * TAB // 2:(i + 1) * TAB // 2],
                                     start=True, stop=True)
                last.then_inc(turned, 1)

        @block.scalar
        def _(act):
            for i, (a, e) in enumerate(spans):
                act.wait_ge(rows_ready, i + 1)
                act.activation(rows[:, a:e], acc[:, i, 0:e - a], ACT.Copy).then_inc(rows_copied, 1)
            for head in range(8):
                act.wait_ge(turned, head + 1)
                act.activation(table[:, head, :].rearrange("p (a b) -> p a b", a=2), turn[:, head % 2, :, 0:TAB // 2],
                               ACT.Copy).then_inc(turned_copied, 1)


def mixing_scalars(nc, k, neg_lam, q_sp, q_df):
    with stage(nc, "products_ready", "sums_ready", "exp_done", "link") as (sems, sbuf, psum, begin):
        products_ready, sums_ready, exp_done, dve_link = sems
        prod = sbuf("prod", [P, 2])
        e = sbuf("e", [P, 2])
        acc = psum("acc", [P, 2])
        block = begin()

        @block.vector
        def _(dve):
            chain = Chain(dve, dve_link)
            lam = k.col("lam")
            dve.tensor_tensor(prod[:, :], lam[:, 0:2], lam[:, 2:4], ALU.mult).then_inc(products_ready, 1)
            chain.link(dve.tensor_scalar(q_sp, k.col("q_norm_sp"), Q_SCALE, None, ALU.mult))
            chain.link(dve.tensor_scalar(q_df, k.col("q_norm_df"), Q_SCALE, None, ALU.mult))
            dve.wait_ge(exp_done, 1)
            chain.link(dve.tensor_tensor(neg_lam, e[:, 1:2], e[:, 0:1], ALU.subtract))
            chain.link(dve.tensor_scalar(neg_lam, neg_lam, LAM_INIT, None, ALU.subtract))

        @block.tensor
        def _(pe):
            pe.wait_ge(products_ready, 1)
            pe.matmul(acc[:, :], k.ones, prod[:, :], start=True, stop=True).then_inc(sums_ready, 1)

        @block.scalar
        def _(act):
            act.wait_ge(sums_ready, 1)
            act.activation(e[:, :], acc[:, :], ACT.Exp).then_inc(exp_done, 1)


def scale_columns(nc, out, col, factor):
    with stage(nc, "scaled") as ((scaled,), _, _, begin):
        block = begin()

        @block.vector
        def _(dve):
            dve.tensor_scalar(out, col, factor, None, ALU.mult).then_inc(scaled, 1)


def second_attention(nc, k, A, ws, h, qm, scratch):
    n, w = N2, W2
    with ExitStack() as ctx:
        def sbuf(name, shape):
            return ctx.enter_context(nc.sbuf_tensor(f"{name}_{nc.next_id()}", shape, F32))

        fm = sbuf("fm", [P, FM2, T2])
        v_tok = sbuf("v_tok", [P, QT2, TM2])
        small = sbuf("small", [P, 4])
        def take(act, t, rows, p, acc):
            width = min(2 * P, TM2 - p * 2 * P)
            return act.activation(v_tok[0:rows, t, p * 2 * P:p * 2 * P + width], acc[:, 0:width], ACT.Copy)

        project_tokens(nc, ws, (TM2 + 2 * P - 1) // (2 * P), h, T2, take)
        project(nc, ws, QM2, [(h, KT, P)], n, w, copies(qm, n, w), unroll=4)
        project(nc, ws, FM2, [(h, KT, P)], n, w, copies(fm, n, w), unroll=4)
        mixing_scalars(nc, k, small[:, 0:1], small[:, 1:2], small[:, 2:3])
        scale_columns(nc, small[:, 3:4], k.col("subln_df"), 1.0 - LAM_INIT)
        queries, tiles = tiles_of(qm, n, w), tiles_of(fm, n, w)
        head_norms(nc, [(queries(SP_Q + i), small[:, 1:2]) for i in range(2)] + [(tiles(SP_K + i), k.col("k_norm_sp")) for i in range(2)]
                   + [(queries(DF_Q + i), small[:, 2:3]) for i in range(4)] + [(tiles(DF_K + i), k.col("k_norm_df")) for i in range(4)],
                   k.half_ones, HD, n, w)
        stick_breaking(nc, k, A, qm, fm, v_tok)
        table = sbuf("table", [P, 8, TAB])
        bias_tables(nc, k, A, scratch, table)
        penalty = sbuf("penalty", [P, QT2, T2])
        select_keys(nc, k, fm, v_tok, penalty)
        groups = []
        for t in range(QT2):
            nq, nk = ROWS2[t], min((t + 1) * P, T2)
            cols = slice(t * P, t * P + nq)
            for head in range(4):
                rows = slice((head % 2) * HD, (head % 2) * HD + HD)
                groups.append(([Part(qm[rows, SP_Q + head // 2, cols], fm[rows, SP_K + head // 2, 0:nk],
                                     table[0:nq, head, OFF - t * P:OFF - t * P + nk],
                                     [v_tok[0:ROWS2[b], b, SP_V + head * HD:SP_V + (head + 1) * HD] for b in range(t + 1)],
                                     penalty=penalty[0:nq, t, 0:nk] if t >= 1 else None)], qm[rows, SP_Q + head // 2, cols]))
            for head in range(4):
                members = []
                for m in range(2):
                    rows = slice(m * HD, (m + 1) * HD)
                    members.append(Part(qm[rows, DF_Q + head, cols], fm[rows, DF_K + head, 0:nk],
                                        table[0:nq, 4 + head, OFF - t * P:OFF - t * P + nk],
                                        [v_tok[0:ROWS2[b], b, DF_V + head * P:DF_V + (head + 1) * P] for b in range(t + 1)],
                                        gate=small[0:nq, 0:1] if m == 1 else None))
                groups.append((members, qm[:, DF_Q + head, cols]))
        attend(nc, k, groups, wide=True)
        head_norms(nc, [(queries(DF_Q + head), small[:, 3:4]) for head in range(4)], k.ones, P, n, w)


def second_block(nc, k, A, ws, b, scratch):
    n, w = N2, W2
    x = tiles_of(b.x, n, w)
    norm, gate = k.at("attn_norm"), k.at("b_gate")
    with ExitStack() as ctx:
        halves = halves_of(nc, ctx, "h", KT, T2)
        h = lambda t: halves.tile(t, T2)
        rms_norm(nc, k, x, T2, n, w, lambda t: k.vec[:, norm + t:norm + t + 1], halves=halves)
        qm = ctx.enter_context(nc.sbuf_tensor(f"qm_{nc.next_id()}", [P, QM2, T2], F32))
        second_attention(nc, k, A, ws, h, qm, scratch)
        cut = halves_of(nc, ctx, "y", KT, T2)
        cut_tiles(nc, [(qm[:, t, :], *cut.tile(t, T2)) for t in range(KT)])
        out = halves_of(nc, ctx, "merged", KT, T2)
        merged = qm
        for i, (at, ks) in enumerate([(0, 2), (2, 2), (4, 4)]):
            merge(nc, k, ws, h, lambda t, at=at: cut.tile(at + t, T2), ks, P, gate + i * KT, i == 0, merged, n, w, out if i == 2 else None)
        project(nc, ws, KT, [(lambda t: out.tile(t, T2), KT, P)], n, w, None,
                lambda dve, chain, i, acc, tmp: dve.tensor_tensor(tile_at(b.x, i, n, w), tile_at(b.x, i, n, w), acc(0), ALU.add), unroll=4)
    ffn = k.at("ffn_norm")
    with ExitStack() as ctx:
        halves = halves_of(nc, ctx, "h", KT, T2)
        rms_norm(nc, k, x, T2, n, w, lambda t: k.vec[:, ffn + t:ffn + t + 1], halves=halves)
        feed_forward(nc, k, ws, k.at("conv_w_2"), k.at("conv_b_2"), lambda t: halves.tile(t, T2), b.x, 0, n, w)


def lay_out_second(v, A):
    w = v["w_in_2"][0]
    widths = [256] * 6 + [256, 32, 8, 512, 512, 512, D, D, D]
    at = np.concatenate([[0], np.cumsum(widths)])
    part = lambda i: w[:, at[i]:at[i + 1]]
    A["rel_bias"] = np.concatenate([v["rel_bias_2"], np.ones((1, 8), np.float32)])
    A["bucket"] = buckets()
    tiles = padded_tiles(np.concatenate([part(2), part(5), part(11), part(8)], axis=1), 2 * P)
    tiles += [tiled(part(0)), tiled(part(3)), tiled(part(9))]
    tiles += [tiled(part(1)), tiled(part(4)), tiled(part(6)), doubled(part(7), 32, 4), tiled(part(10))]
    for i, name in enumerate(("w_br_sb_2", "w_br_sp_2", "w_br_df_2")):
        tiles += in_turn(tiled(part(12 + i)), tiled(v[name][0]))
    tiles += [tiled(v["w_out_2"][0])]
    return tiles + ff_tiles(v["w_up_2"][0], v["w_down_2"][0])



FQ, HQ, CA, QM3 = 0, 3, 7, 9
FK, HF, HG_G, CB, FF, FM3 = 0, 3, 7, 11, 13, 14
FV, HV, TM3 = 0, FOX * HD, 2 * FOX * HD
LEVELS = [1, 2, 4, 8, 16, 32]
TILES3 = S // P
CHUNKS = S // CH


def forget_sums(nc, k, ff, sums):
    with stage(nc, "link", "ones_done", "log_done") as (sems, sbuf, psum, begin):
        dve_link, ones_done, log_done = sems
        a = sbuf("a", [FOX, 3, S])
        ones = sbuf("ones", [FOX, S])
        block = begin()

        @block.vector
        def _(dve):
            chain = Chain(dve, dve_link)
            dve.memset(ones[:, :], 1.0).then_inc(ones_done, 1)
            dve.wait_ge(ones_done, 1)
            chain.link(dve.tensor_scalar(a[:, 0, :], ff, k.one("fox_forget_b")[0:FOX], -1.0, ALU.add, ALU.mult))
            dve.wait_ge(log_done, 3)
            chain.link(dve.scalar_tensor_tensor(a[:, 2, :], a[:, 0, :], 0.0, a[:, 1, :], ALU.max, ALU.add))
            chain.link(dve.tensor_tensor_scan(sums, ones[:, :], a[:, 2, :], 0.0, ALU.mult, ALU.add))

        @block.scalar
        def _(act):
            act.wait_ge(dve_link, 1)
            chain = Chain(act, log_done)
            chain.link(act.activation(a[:, 1, :], a[:, 0, :], ACT.Abs))
            chain.link(act.activation(a[:, 1, :], a[:, 1, :], ACT.Exp, scale=-1.0))
            chain.link(act.activation(a[:, 1, :], a[:, 1, :], ACT.Ln, bias=1.0))


def hgrn(nc, k, A, qm, fm, v_tok):
    names = ["hf_done", "gate_link", "key_done", "sums_done", "apart_done", "decay_done", "factors_done", "pairs_ready", "pairs_taken",
             "last_done", "kd_done", "turned", "turned_copied", "update_ready", "state_done", "out_ready", "out_copied", "dve_link", "loaded", "pool_link"]
    with stage(nc, *names) as (sems, sbuf, psum, begin):
        (hf_done, gate_link, key_done, sums_done, apart_done, decay_done, factors_done, pairs_ready, pairs_taken,
         last_done, kd_done, turned, turned_copied, update_ready, state_done, out_ready, out_copied, dve_link, loaded, pool_link) = sems
        masks = sbuf("masks", [P, 1 + len(LEVELS), P], mybir.dt.uint32)
        resets = sbuf("resets", [P, S])
        log_part = sbuf("log_part", [P, 2, S])
        sums = sbuf("sums", [P, HG, S])
        apart = sbuf("apart", [P, 2, S])
        decay = sbuf("decay", [P, 2, S])
        k_part = sbuf("k_part", [P, 2, S])
        q_part = sbuf("q_part", [P, 2, S])
        pairs = sbuf("pairs", [P, 2, TILES3, P])
        q_in = sbuf("q_in", [P, S])
        kd = sbuf("kd", [P, S])
        kd_tok = sbuf("kd_tok", [P, TILES3, P])
        last = sbuf("last", [P, CHUNKS])
        states = sbuf("states", [P, CHUNKS - 1, HG_V])
        pair_acc = psum("pair_acc", [P, 2, TILES3, P])
        turn_acc = psum("turn_acc", [P, TILES3, P])
        update = psum("update", [P, 2, 512])
        out = psum("out", [P, 2, 512])
        block = begin()
        NL = len(LEVELS)

        def halves(a, m):
            return a.rearrange("p (n a m) -> p n a m", a=2, m=m)

        def key(head):
            return fm[:, HF + head, 0:S]

        def update_at(c):
            return update[:, c % 2, (c // 2) * HG_V:(c // 2 + 1) * HG_V]

        @block.sync
        def _(sp):
            sp.dma_start(masks[:, :, :], A["level_masks"]).then_inc(loaded, 16)
            sp.dma_start(resets[:, :], A["resets"]).then_inc(loaded, 16)

        @block.scalar
        def _(act):
            links = Chain(act, gate_link)
            for head in range(HG):
                hf = fm[:, HF + head, 0:S]
                if head >= 2:
                    act.wait_ge(sums_done, 2 * (head - 1))
                links.link(act.activation(log_part[:, head % 2, :], hf, ACT.Abs))
                links.link(act.activation(log_part[:, head % 2, :], log_part[:, head % 2, :], ACT.Exp, scale=-1.0))
                act.activation(log_part[:, head % 2, :], log_part[:, head % 2, :], ACT.Ln, bias=1.0).then_inc(hf_done, 1)
            act.wait_ge(sums_done, 2 * HG)
            for head in range(HG):
                act.activation(key(head), key(head), ACT.Sigmoid, scale=-1.0).then_inc(key_done, 1)
            for head in range(HG):
                for l in range(NL):
                    i = head * NL + l
                    act.wait_ge(apart_done, 2 * (i + 1) + 2 * head)
                    if i >= 2:
                        act.wait_ge(factors_done, 2 * (i - 1))
                    act.activation(decay[:, i % 2, :], apart[:, i % 2, :], ACT.Exp).then_inc(decay_done, 1)
                act.wait_ge(apart_done, 2 * NL * (head + 1) + 2 * head + 2)
                act.activation(q_in[:, :], q_in[:, :], ACT.Exp, scale=-1.0).then_inc(last_done, 1)
                act.activation(last[:, :], sums[:, head, CH - 1:S:CH], ACT.Exp, scale=-1.0).then_inc(last_done, 1)
                act.activation(kd[:, :], kd[:, :], ACT.Exp).then_inc(last_done, 1)
                act.wait_ge(turned, head + 1)
                act.activation(kd_tok[:, :, :], turn_acc[:, :, :], ACT.Copy).then_inc(turned_copied, 1)
                act.wait_ge(out_ready, head + 1)
                act.activation(qm[0:HG_V, HQ + head, :], out[0:HG_V, head % 2, :], ACT.Copy).then_inc(out_copied, 1)

        @block.vector
        def _(dve):
            chain = Chain(dve, dve_link)
            dve.wait_ge(loaded, 32)
            for head in range(HG):
                hf = fm[:, HF + head, 0:S]
                dve.wait_ge(hf_done, head + 1)
                dve.scalar_tensor_tensor(log_part[:, head % 2, :], hf, 0.0, log_part[:, head % 2, :], ALU.min, ALU.subtract).then_inc(sums_done, 1)
                dve.wait_ge(sums_done, 2 * head + 1)
                dve.tensor_tensor_scan(sums[:, head, :], resets[:, :], log_part[:, head % 2, :], 0.0, ALU.mult, ALU.subtract).then_inc(sums_done, 1)
            dve.wait_ge(sums_done, 2 * HG)
            dve.wait_ge(key_done, HG)
            for head in range(HG):
                q = qm[:, HQ + head, 0:S]
                keys, b = key(head), sums[:, head, :]
                dve.wait_ge(pairs_ready, head * (NL + 1) + 1)
                if head >= 2:
                    dve.wait_ge(out_ready, head - 1)
                dve.tensor_tensor(pairs[:, head % 2], pair_acc[:, (head * (NL + 1)) % 2], masks[:, 0:1, :].to_broadcast([P, TILES3, P]),
                                  ALU.mult).then_inc(pairs_taken, 1)
                dve.wait_ge(pairs_taken, head * (NL + 1) + 1)

                def split(l):
                    i = head * NL + l
                    m = LEVELS[l]
                    if i >= 2:
                        dve.wait_ge(decay_done, i - 1)
                    to, of = halves(apart[:, i % 2, :], m), halves(b, m)
                    meet = of[:, :, 0, m - 1:m].to_broadcast([P, S // (2 * m), m])
                    dve.tensor_tensor(to[:, :, 0, :], of[:, :, 0, :], meet, ALU.subtract).then_inc(apart_done, 1)
                    dve.tensor_tensor(to[:, :, 1, :], meet, of[:, :, 1, :], ALU.subtract).then_inc(apart_done, 1)

                def factors(l):
                    i = head * NL + l
                    dve.wait_ge(decay_done, i + 1)
                    if i >= 2:
                        dve.wait_ge(pairs_ready, (i - 2) // NL * (NL + 1) + (i - 2) % NL + 2)
                    dve.tensor_tensor(k_part[:, i % 2, :], keys, decay[:, i % 2, :], ALU.mult).then_inc(factors_done, 1)
                    dve.tensor_tensor(q_part[:, i % 2, :], q, decay[:, i % 2, :], ALU.mult).then_inc(factors_done, 1)

                def take(l):
                    n = head * (NL + 1) + 1 + l
                    dve.wait_ge(pairs_ready, n + 1)
                    dve.copy_predicated(pairs[:, head % 2], masks[:, l + 1:l + 2, :].to_broadcast([P, TILES3, P]),
                                        pair_acc[:, n % 2]).then_inc(pairs_taken, 1)
                    dve.wait_ge(pairs_taken, n + 1)

                split(0)
                for l in range(NL):
                    if l + 1 < NL:
                        split(l + 1)
                    factors(l)
                    if l >= 1:
                        take(l - 1)
                take(NL - 1)

                if head >= 1:
                    dve.wait_ge(out_ready, head)
                dve.tensor_copy(q_in[:, :], b).then_inc(apart_done, 1)
                ends = b.rearrange("p (c t) -> p c t", t=CH)[:, :, CH - 1:CH].to_broadcast([P, CHUNKS, CH])
                dve.tensor_tensor(kd[:, :].rearrange("p (c t) -> p c t", t=CH), b.rearrange("p (c t) -> p c t", t=CH), ends,
                                  ALU.subtract).then_inc(apart_done, 1)
                dve.wait_ge(last_done, 3 * (head + 1))
                dve.tensor_tensor(q_in[:, :], q_in[:, :], q, ALU.mult).then_inc(kd_done, 1)
                dve.tensor_tensor(kd[:, :], kd[:, :], keys, ALU.mult).then_inc(kd_done, 1)
                dve.wait_ge(update_ready, head + 1)
                for c in range(CHUNKS - 1):
                    if c == 0:
                        ins = dve.tensor_copy(states[:, 0, :], update_at(0))
                    else:
                        ins = dve.scalar_tensor_tensor(states[:, c, :], states[:, c - 1, :], last[:, c:c + 1], update_at(c), ALU.mult, ALU.add)
                    ins.then_inc(state_done, 1)
                    dve.wait_ge(state_done, head * (CHUNKS - 1) + c + 1)

        @block.tensor
        def _(pe):
            pe.wait_ge(key_done, HG)
            for head in range(HG):
                q, keys = qm[:, HQ + head, 0:S], key(head)
                values = lambda t: v_tok[:, t, HV + head * HG_V:HV + (head + 1) * HG_V]
                for l in range(NL + 1):
                    n = head * (NL + 1) + l
                    if n >= 2:
                        pe.wait_ge(pairs_taken, n - 1)
                    if l >= 1:
                        i = head * NL + l - 1
                        pe.wait_ge(factors_done, 2 * (i + 1))
                        left, right = k_part[:, i % 2, :], q_part[:, i % 2, :]
                    else:
                        left, right = keys, q
                    for t in range(TILES3):
                        mm = pe.matmul(pair_acc[:, n % 2, t, :], left[:, t * P:(t + 1) * P], right[:, t * P:(t + 1) * P], start=True, stop=True)
                    mm.then_inc(pairs_ready, 1)
                pe.wait_ge(kd_done, 2 * (head + 1))
                if head >= 1:
                    pe.wait_ge(turned_copied, head)
                for t in range(TILES3):
                    mm = pe.transpose(turn_acc[:, t, :], kd[:, t * P:(t + 1) * P], k.ident)
                mm.then_inc(turned, 1)
                pe.wait_ge(turned_copied, head + 1)
                if head >= 1:
                    pe.wait_ge(state_done, head * (CHUNKS - 1))
                for c in range(CHUNKS - 1):
                    rows = slice((c % 2) * CH, (c % 2 + 1) * CH)
                    mm = pe.matmul(update_at(c), kd_tok[rows, c // 2, :], v_tok[rows, c // 2, HV + head * HG_V:HV + (head + 1) * HG_V],
                                   start=True, stop=True)
                mm.then_inc(update_ready, 1)
                if head >= 2:
                    pe.wait_ge(out_copied, head - 1)
                pe.wait_ge(pairs_taken, (head + 1) * (NL + 1))
                pe.wait_ge(state_done, (head + 1) * (CHUNKS - 1))
                for t in range(TILES3):
                    pe.matmul(out[0:HG_V, head % 2, t * P:(t + 1) * P], values(t), pairs[:, head % 2, t, :], start=True, stop=False)
                    for c in range(max(1, 2 * t), 2 * t + 2):
                        mm = pe.matmul(out[0:HG_V, head % 2, c * CH:(c + 1) * CH], states[:, c - 1, :], q_in[:, c * CH:(c + 1) * CH],
                                       start=False, stop=c == 2 * t + 1)
                mm.then_inc(out_ready, 1)


def conv_branch(nc, k, qm, fm):
    tiles, back = 2, CONV_W - 1
    with stage(nc, "gate_done", "link", "conv_done", "summed", "centred", "squared", "var_ready", "root_done", "scaled", "done") as (sems, sbuf, psum, begin):
        gate_done, dve_link, conv_done, summed, centred, squared, var_ready, root_done, scaled, done = sems
        pad = sbuf("pad", [P, tiles, back + S])
        gate = sbuf("gate", [P, tiles, S])
        conv = sbuf("conv", [P, tiles, S])
        scale = sbuf("scale", [P, 2, S])
        acc = psum("acc", [P, 2, S])
        block = begin()

        @block.scalar
        def _(act):
            for t in range(tiles):
                act.activation(gate[:, t, :], fm[:, CB + t, 0:S], ACT.Sigmoid).then_inc(gate_done, 1)
            for t in range(tiles):
                act.wait_ge(centred, t + 1)
                act.activation(gate[:, t, :], conv[:, t, :], ACT.Square).then_inc(squared, 1)
            act.wait_ge(var_ready, 1)
            act.activation(scale[:, 1, :], scale[:, 0, :], ACT.Sqrt).then_inc(root_done, 1)
            for t in range(tiles):
                act.wait_ge(scaled, t + 1)
                act.activation(qm[:, CA + t, 0:S], conv[:, t, :], ACT.Silu, bias=k.one("dw_ln_b", t)).then_inc(done, 1)

        @block.vector
        def _(dve):
            chain = Chain(dve, dve_link)
            chain.link(dve.memset(pad[:, :, 0:back], 0.0))
            for t in range(tiles):
                dve.wait_ge(gate_done, t + 1)
                chain.link(dve.tensor_tensor(pad[:, t, back:back + S], qm[:, CA + t, 0:S], gate[:, t, :], ALU.mult))
            for i in range(CONV_W):
                for t in range(tiles):
                    tap = k.one("dw_w", i * tiles + t)
                    if i >= 1:
                        dve.wait_ge(conv_done, (i - 1) * tiles + t + 1)
                        ins = dve.scalar_tensor_tensor(conv[:, t, :], pad[:, t, i:i + S], tap, conv[:, t, :], ALU.mult, ALU.add)
                    else:
                        ins = dve.tensor_scalar(conv[:, t, :], pad[:, t, 0:S], tap, k.one("dw_b", t), ALU.mult, ALU.add)
                    ins.then_inc(conv_done, 1)
            dve.wait_ge(summed, 1)
            dve.wait_ge(conv_done, CONV_W * tiles)
            for t in range(tiles):
                dve.scalar_tensor_tensor(conv[:, t, :], acc[:, 0, :], -1.0 / (tiles * P), conv[:, t, :], ALU.mult, ALU.add).then_inc(centred, 1)
            dve.wait_ge(summed, 2)
            dve.tensor_scalar(scale[:, 0, :], acc[:, 1, :], 1.0 / (tiles * P), EPS, ALU.mult, ALU.add).then_inc(var_ready, 1)
            dve.wait_ge(root_done, 1)
            chain.link(dve.reciprocal(scale[:, 0, :], scale[:, 1, :]))
            dve.wait_ge(centred, tiles)
            for t in range(tiles):
                dve.scalar_tensor_tensor(conv[:, t, :], conv[:, t, :], k.one("dw_ln_g", t), scale[:, 0, :], ALU.mult, ALU.mult).then_inc(scaled, 1)

        @block.tensor
        def _(pe):
            for t in range(tiles):
                pe.wait_ge(conv_done, (CONV_W - 1) * tiles + t + 1)
                last = pe.matmul(acc[:, 0, :], k.ones, conv[:, t, :], start=t == 0, stop=t == tiles - 1)
            last.then_inc(summed, 1)
            for t in range(tiles):
                pe.wait_ge(squared, t + 1)
                last = pe.matmul(acc[:, 1, :], k.ones, gate[:, t, :], start=t == 0, stop=t == tiles - 1)
            last.then_inc(summed, 1)


def gate_heads(nc, qm, fm):
    with stage(nc, "silu_done", "gated") as ((silu_done, gated), sbuf, _, begin):
        silu = sbuf("silu", [P, HG, S])
        block = begin()

        @block.scalar
        def _(act):
            for head in range(HG):
                act.activation(silu[0:HG_V, head, :], fm[0:HG_V, HG_G + head, 0:S], ACT.Silu).then_inc(silu_done, 1)

        @block.vector
        def _(dve):
            for head in range(HG):
                dve.wait_ge(silu_done, head + 1)
                dve.tensor_tensor(qm[0:HG_V, HQ + head, :], qm[0:HG_V, HQ + head, :], silu[0:HG_V, head, :], ALU.mult).then_inc(gated, 1)


def third_block(nc, k, A, ws, b):
    n, w = 1, S
    x = tiles_of(b.x, n, w, META)
    norm, gate = k.at("norm_mix_3"), k.at("gate_b_3")
    with ExitStack() as ctx:
        halves = halves_of(nc, ctx, "h", KT, S)
        h = lambda t: halves.tile(t, S)
        rms_norm(nc, k, x, S, n, w, lambda t: k.vec[:, norm + t:norm + t + 1], halves=halves)
        qm = ctx.enter_context(nc.sbuf_tensor(f"qm_{nc.next_id()}", [P, QM3, S], F32))
        with ExitStack() as inner:
            third_branches(nc, k, A, ws, inner, h, qm)
        cuts = halves_of(nc, ctx, "y", QM3, S)
        rows_of = lambda t: HG_V if HQ <= t < CA else P
        cut_tiles(nc, [(qm[0:rows_of(t), t, :], *cuts.tile(t, S, rows_of(t))) for t in range(QM3)])
        merged = qm
        out = halves_of(nc, ctx, "merged", KT, S)
        for i, (at, ks, rows) in enumerate([(FQ, 3, P), (HQ, HG, HG_V), (CA, 2, P)]):
            merge(nc, k, ws, h, lambda t, at=at, rows=rows: cuts.tile(at + t, S, rows), ks, rows, gate + i * KT, i == 0, merged, n, w,
                  out if i == 2 else None)
        project(nc, ws, KT, [(lambda t: out.tile(t, S), KT, P)], n, w, None,
                lambda dve, chain, i, acc, tmp: dve.tensor_tensor(tile_at(b.x, i, n, w, META), tile_at(b.x, i, n, w, META), acc(0), ALU.add),
                unroll=4)
    ffn = k.at("norm_ffn_3")
    with ExitStack() as ctx:
        halves = halves_of(nc, ctx, "h", KT, S)
        rms_norm(nc, k, x, S, n, w, lambda t: k.vec[:, ffn + t:ffn + t + 1], halves=halves)
        feed_forward(nc, k, ws, k.at("ffn_dw_w"), k.at("ffn_dw_b"), lambda t: halves.tile(t, S), b.x, META, n, w)


def third_branches(nc, k, A, ws, ctx, h, qm):
    n, w = 1, S

    def sbuf(name, shape):
        return ctx.enter_context(nc.sbuf_tensor(f"{name}_{nc.next_id()}", shape, F32))

    fm = sbuf("fm", [P, FM3, S])
    v_tok = sbuf("v_tok", [P, TILES3, TM3])
    small = sbuf("small", [P, 1])
    forgotten = sbuf("forgotten", [FOX, S])
    project(nc, ws, QM3, [(h, KT, P)], n, w, copies(qm, n, w), unroll=4)
    project(nc, ws, FM3, [(h, KT, P)], n, w, copies(fm, n, w), unroll=4)
    project_tokens(nc, ws, TM3 // (2 * P), h, S,
                   lambda act, t, rows, p, acc: act.activation(v_tok[0:rows, t, p * 2 * P:(p + 1) * 2 * P], acc, ACT.Copy))
    scale_columns(nc, small[:, 0:1], k.col("fox_q_norm"), Q_SCALE)
    queries, tiles = tiles_of(qm, n, w), tiles_of(fm, n, w)
    head_norms(nc, [(queries(FQ + i), small[:, 0:1]) for i in range(3)] + [(tiles(FK + i), k.col("fox_k_norm")) for i in range(3)],
               k.half_ones, HD, n, w)
    forget_sums(nc, k, fm[0:FOX, FF, 0:S], forgotten[:, :])
    with nc.sbuf_tensor(f"fox_rows_{nc.next_id()}", [FOX, FOX * P], F32) as fox_rows:
        with stage(nc, "loaded") as ((loaded,), _, _, begin):
            block = begin()

            @block.sync
            def _(sp):
                sp.dma_start(fox_rows[:, :], A["fox_rows"]).then_inc(loaded, 16)
                sp.wait_ge(loaded, 16)
        groups = []
        for head in range(FOX):
            rows = slice((head % 2) * HD, (head % 2) * HD + HD)
            for t in range(TILES3):
                cols, nk = slice(t * P, (t + 1) * P), (t + 1) * P
                groups.append(([Part(qm[rows, FQ + head // 2, cols], fm[rows, FK + head // 2, 0:nk], k.causal[:, OFF - t * P:TAB],
                                     [v_tok[:, j, FV + head * HD:FV + (head + 1) * HD] for j in range(t + 1)],
                                     extra=(fox_rows[:, head * P:(head + 1) * P], forgotten[:, 0:nk]))],
                               qm[rows, FQ + head // 2, cols]))
        attend(nc, k, groups, wide=False, longest=S)
    hgrn(nc, k, A, qm, fm, v_tok)
    head_norms(nc, [(qm[0:HG_V, HQ + head, :], k.col("hgrn_norm")[0:HG_V]) for head in range(HG)], k.ones, HG_V, n, w, rows=HG_V)
    gate_heads(nc, qm, fm)
    conv_branch(nc, k, qm, fm)


def lay_out_third(v, A):
    w = v["w_in_3"][0]
    widths = [FOX * HD] * 3 + [FOX, 512, 512, HG * HG_V, HG * HG_V, 256, 256, 3 * D]
    at = np.concatenate([[0], np.cumsum(widths)])
    part = lambda i: w[:, at[i]:at[i + 1]]
    A["level_masks"] = level_masks()
    wb, gates = v["w_branch_3"][0], part(10)
    fox, hg = FOX * HD, HG * HG_V
    rows_of_head = np.zeros((HG, P, D), np.float32)
    rows_of_head[:, 0:HG_V] = wb[fox:fox + hg].reshape(HG, HG_V, D)
    branch = [wb[0:fox], rows_of_head.reshape(HG * P, D), wb[fox + hg:]]
    tiles = [tiled(part(0)), tiled(part(4)), tiled(part(8))]
    tiles += [tiled(part(1)), tiled(part(5)), tiled(part(7), HG_V), tiled(part(9)), tiled(part(3), FOX)]
    tiles += padded_tiles(np.concatenate([part(2), part(6)], axis=1), 2 * P)
    for i in range(3):
        tiles += in_turn(tiled(gates[:, i * D:(i + 1) * D]), tiled(branch[i]))
    tiles += [tiled(v["w_out_3"][0])]
    return tiles + ff_tiles(v["w_up_3"][0], v["w_down_3"][0])



class Consts:

    def __init__(self, vec, places):
        self.vec, self.places = vec, places

    def at(self, name):
        return self.places[name][0]

    def col(self, name):
        a, n = self.places[name]
        return self.vec[:, a:a + n]

    def one(self, name, i=0):
        a = self.places[name][0] + i
        return self.vec[:, a:a + 1]


class Buffers:
    def __init__(self, x):
        self.x = x


def build(nc, A, out, vec_places, const_places, scratch):
    with ExitStack() as ctx:
        def sbuf(name, shape):
            return ctx.enter_context(nc.sbuf_tensor(name, shape, F32))

        vec = sbuf("vec", [P, A["vec"].shape[1]])
        const = sbuf("const", [P, A["const"].shape[1]])
        k = Consts(vec, vec_places)

        def c(name):
            a, n = const_places[name]
            return const[:, a:a + n]
        k.ones, k.ident, k.mirror, k.half_ones, k.later = c("ones"), c("ident"), c("mirror"), c("half_ones"), c("later")
        k.sees_cmp, k.causal = c("sees_cmp"), c("causal")
        k.ada = sbuf("ada", [P, 3 * KT])
        b = Buffers(sbuf("x", [P, KT, T2]))
        ws = WeightStream(nc, ctx, A["stream"])
        with stage(nc, "loaded") as ((loaded,), _, _, begin):
            block = begin()

            @block.sync
            def _(sp):
                sp.dma_start(vec[:, :], A["vec"]).then_inc(loaded, 16)
                sp.dma_start(const[:, :], A["const"]).then_inc(loaded, 16)
                sp.dma_start(b.x[:, :, 0:META], A["meta"]).then_inc(loaded, 16)
                sp.dma_start(b.x[:, :, META:T2], A["x"]).then_inc(loaded, 16)
                sp.wait_ge(loaded, 64)
        ws.begin(nc)
        first_block(nc, k, A, ws, b)
        second_block(nc, k, A, ws, b, scratch)
        third_block(nc, k, A, ws, b)
        assert ws.next == ws.total, (ws.next, ws.total)
        stored = nc.alloc_semaphore("stored")
        block = ctx.enter_context(nc.Block())

        @block.sync
        def _(sp):
            sp.dma_start(out, b.x[:, :, META:T2]).then_inc(stored, 16)
            sp.wait_ge(stored, 16)



def columns(v):
    return np.asarray(v).reshape(-1, P).T


def padded(v):
    out = np.zeros((P, 1), np.float32)
    out[:np.size(v), 0] = np.asarray(v).reshape(-1)
    return out


def tiled(w, cols=P):
    w = np.asarray(w)
    kt, nt = w.shape[0] // P, w.shape[1] // cols
    out = w.reshape(kt, P, nt, cols).transpose(2, 1, 0, 3)
    if cols < P:
        out = np.concatenate([out, np.zeros(out.shape[:3] + (P - cols,), np.float32)], axis=3)
    return out


def doubled(w, cols, times):
    t = tiled(w, cols)[..., :cols]
    return np.concatenate([t] * times, axis=3)


def padded_tiles(w, multiple):
    n = -(-w.shape[1] // multiple) * multiple
    return [tiled(np.concatenate([w, np.zeros((w.shape[0], n - w.shape[1]), np.float32)], axis=1))]


def in_turn(*tiles):
    return [t[i:i + 1] for i in range(len(tiles[0])) for t in tiles]


def ff_tiles(up, down):
    gate, value = tiled(up[:, :D_FF]), tiled(up[:, D_FF:])
    out = []
    for f0, f1 in FF_PARTS:
        out += in_turn(gate[f0:f1], value[f0:f1])
        share = tiled(down[f0 * P:f1 * P])
        out += in_turn(*(share[:, :, k:k + KT] for k in range(0, f1 - f0, KT)))
    return out


def stream_of(tiles):
    n = sum(len(t) for t in tiles)
    out = np.zeros((n, P, KT, P), np.float32)
    at = 0
    for t in tiles:
        out[at:at + len(t), :, :t.shape[2]] = t
        at += len(t)
    return out.reshape(n, P, KT * P)


def tokens_last(x):
    return np.asarray(x).T.reshape(KT, P, -1).transpose(1, 0, 2)


def shape_constants():
    p = np.arange(P)[:, None]
    rel = p - np.arange(TAB)[None, :] + OFF
    same_half = (np.arange(P)[:, None] // HD) == (np.arange(P)[None, :] // HD)
    return {
        "ones": np.ones((P, P)), "ident": np.eye(P), "mirror": np.eye(P)[::-1], "half_ones": same_half,
        "later": np.arange(P)[:, None] >= np.arange(P)[None, :],
        "sees_cmp": p >= 31, "causal": np.where(rel >= 0, 0.0, BIG),
    }


def stage_constants(A):
    p = np.arange(P)[:, None]
    rel = p - np.arange(TAB)[None, :] + OFF
    A["distance"] = np.where(rel >= 0, rel, FAR).astype(np.float32)
    t = p + P * np.arange(S // P)[None, :]
    d = t[:, :, None] - (16 * np.arange(N_CMP) + 31)[None, None, :]
    A["distance_cmp"] = np.where(d >= 0, d, FAR).reshape(P, -1).astype(np.float32)
    c = np.arange(2 * T2 - 272) - 256
    A["before"] = (np.arange(P)[:, None] < c[None, :]).astype(np.float32)
    A["resets"] = np.broadcast_to((np.arange(S) % CH != 0).astype(np.float32)[None, :], (P, S))
    A["fox_rows"] = np.repeat(-np.eye(FOX, dtype=np.float32), P, axis=1)


def buckets():
    rel = OFF + P - 1 - np.arange(TAB + P - 1)
    n = np.maximum(rel, 0)
    nf = np.maximum(n, 1).astype(np.float32)
    large = 16 + (np.log(nf / np.float32(16)) / np.float32(math.log(8)) * np.float32(16)).astype(np.int32)
    bucket = np.where(n < 16, n, np.minimum(large, 31))
    out = np.zeros((33, rel.size), np.float32)
    out[bucket, np.arange(rel.size)] = -1.0
    out[:, rel < 0] = 0.0
    out[32, rel < 0] = BIG
    return out


def level_masks():
    s, t = np.arange(P)[:, None], np.arange(P)[None, :]
    out = [s == t]
    for m in (1, 2, 4, 8, 16, 32):
        out.append((s // (2 * m) == t // (2 * m)) & (s % (2 * m) < m) & (t % (2 * m) >= m))
    return np.stack(out, axis=1).astype(np.uint32)


def pack(named):
    places, parts, at = {}, [], 0
    for name, a in named.items():
        a = np.asarray(a, np.float32).reshape(P, -1)
        places[name] = (at, a.shape[1])
        parts.append(a)
        at += a.shape[1]
    return np.ascontiguousarray(np.concatenate(parts, axis=1)), places


def lay_out(v):
    A = {}
    v = {name: np.asarray(a) for name, a in v.items()}
    A["x"], A["meta"] = tokens_last(v["x"][0]), tokens_last(v["meta_tokens_2"])
    twice = lambda a: np.concatenate([a.reshape(-1), a.reshape(-1)])
    A["vec"], vec_places = pack({
        "c": columns(v["c"]), "b_ada": columns(v["b_ada"]), "g_pre": columns(v["g_pre"]), "g_post": columns(v["g_post"]),
        "conv_w": columns(v["conv_w"]), "conv_b": columns(v["conv_b"]),
        "attn_norm": columns(v["attn_norm_2"]), "b_gate": columns(v["b_gate_2"]), "ffn_norm": columns(v["ffn_norm_2"]),
        "conv_w_2": columns(v["conv_w_2"]), "conv_b_2": columns(v["conv_b_2"]),
        "q_norm_sp": padded(twice(v["q_norm_sp_2"])), "k_norm_sp": padded(twice(v["k_norm_sp_2"])),
        "q_norm_df": padded(twice(v["q_norm_df_2"])), "k_norm_df": padded(twice(v["k_norm_df_2"])),
        "lam": np.concatenate([padded(v[n]) for n in ("lam_q1_2", "lam_q2_2", "lam_k1_2", "lam_k2_2")], axis=1),
        "subln_df": padded(v["subln_df_2"]),
        "norm_mix_3": columns(v["norm_mix_g_3"]), "gate_b_3": columns(v["gate_b_3"]), "norm_ffn_3": columns(v["norm_ffn_g_3"]),
        "fox_forget_b": padded(v["fox_forget_b_3"]), "fox_q_norm": padded(twice(v["fox_q_norm_g_3"])),
        "fox_k_norm": padded(twice(v["fox_k_norm_g_3"])), "hgrn_norm": padded(v["hgrn_out_norm_g_3"]),
        "dw_w": np.concatenate([columns(v["conv_dw_w_3"][0][i]) for i in range(CONV_W)], axis=1), "dw_b": columns(v["conv_dw_b_3"]),
        "dw_ln_g": columns(v["conv_norm_g_3"]), "dw_ln_b": columns(v["conv_norm_b_3"]),
        "ffn_dw_w": columns(v["ffn_dw_w_3"]), "ffn_dw_b": columns(v["ffn_dw_b_3"]),
    })
    A["const"], const_places = pack(shape_constants())

    w = v["w_in"][0]
    cols = lambda a, n: w[:, a:a + n]
    A["w_ada"] = tiled(v["w_ada"][0])
    stage_constants(A)
    B = 4 * MIX
    kv = lambda i: cols(B + MIX + i * 256, 256)
    z_at = B + MIX + 6 * 256
    C = z_at + MIX + 3 * NH
    G = C + 3 * MIX
    merge_tiles = lambda i: in_turn(tiled(cols(G + i * D, D)), tiled(v["w_br"][0, i]))
    tiles = [tiled(cols(B, MIX)), doubled(kv(0), HD, 2), doubled(kv(1), HD, 2), doubled(kv(2), HD, 2), doubled(kv(4), HD, 2)]
    tiles += padded_tiles(np.concatenate([kv(3), kv(5), cols(z_at + MIX, 3 * NH)], axis=1), 2 * P)
    tiles += [tiled(cols(z_at, MIX))] + merge_tiles(1)
    tiles += in_turn(*[tiled(cols(i * MIX, MIX)) for i in range(4)]) + merge_tiles(0)
    tiles += [tiled(cols(C + MIX, MIX))] + in_turn(tiled(cols(C, MIX)), tiled(cols(C + 2 * MIX, MIX))) + merge_tiles(2)
    tiles += [tiled(v["w_out"][0])]
    A["w_cmp1"] = np.stack([v[n][0].reshape(32, HD, P).transpose(1, 0, 2) for n in ("w_ck1", "w_cv1")], axis=1)
    A["pos_cmp"] = np.stack([v[n][0].T for n in ("pos_ck", "pos_cv")], axis=1)
    A["w_cmp2"] = np.stack([np.concatenate([v[n][0]] * 2, axis=1) for n in ("w_ck2", "w_cv2")], axis=1)
    A["w_s_t"], A["b_s"] = v["w_s"][0].transpose(2, 0, 1), v["b_s"]
    A["ln_g"], A["ln_b"] = v["ln_g"], v["ln_b"]
    A["stream"] = stream_of(tiles + lay_out_second(v, A) + lay_out_third(v, A))
    return {name: np.ascontiguousarray(a) for name, a in A.items()}, vec_places, const_places


def kernel(**inputs):
    import concourse.bacc as bacc
    from concourse.bass_utils import run_bass_kernel_spmd

    arrays, vec_places, const_places = lay_out(inputs)
    nc = bacc.Bacc("TRN2", target_bir_lowering=False, num_devices=1)
    A = {name: nc.dram_tensor(f"in_{name}", a.shape, mybir.dt.from_np(a.dtype), kind="ExternalInput").ap() for name, a in arrays.items()}
    out = nc.dram_tensor("out", (P, KT, S), F32, kind="ExternalOutput").ap()
    scratch = nc.dram_tensor("bias_rows", (8, TAB + P - 1), F32, kind="Internal").ap()
    build(nc, A, out, vec_places, const_places, scratch)
    r = run_bass_kernel_spmd(nc, [{f"in_{name}": a for name, a in arrays.items()}], core_ids=[0])
    return r.results[0]["out"].transpose(1, 0, 2).reshape(D, S).T.reshape(1, S, D)
```

```python
import math
from contextlib import ExitStack, contextmanager

import numpy as np

import concourse.bass as bass
from concourse import mybir

F32 = mybir.dt.float32
F32R = mybir.dt.float32r
ALU = mybir.AluOpType
ACT = mybir.ActivationFunctionType
AX_X = mybir.AxisListType.X

P = 128
D = 1024
KT = D // P
S = 512
META = 16
T2 = META + S
HD = 64
EPS = 1e-6
BIG = 1e30
FAR = 1e33
Q_SCALE = -(HD ** -0.5)

MIX = 1024
NH, NKV = 16, 4
N_CMP = (S - 32) // 16 + 1
TOP_K = min(256, T2 // 4)
D_FF = 2816
FFT = D_FF // P
LAM_INIT = 0.8 - 0.6 * math.exp(-0.3 * 0)
FOX = 6
HG = 4
HG_V = 96
CH = 64
CONV_W = 31

OFF = 512
TAB = OFF + P


class Chain:

    def __init__(self, eng, done, base=0):
        self.eng, self.done, self.base, self.n = eng, done, base, 0

    def link(self, ins):
        self.n += 1
        ins.then_inc(self.done, 1)
        self.eng.wait_ge(self.done, self.base + self.n)


    def after(self):
        if self.n:
            self.eng.wait_ge(self.done, self.base + self.n)

    def add(self, ins):
        self.n += 1
        ins.then_inc(self.done, 1)


@contextmanager
def stage(nc, *names):
    sems = [nc.alloc_semaphore(f"{n}_{nc.next_id()}") for n in names]
    with ExitStack() as ctx:
        def sbuf(name, shape, dtype=F32):
            return ctx.enter_context(nc.sbuf_tensor(f"{name}_{nc.next_id()}", shape, dtype))

        def psum(name, shape):
            return ctx.enter_context(nc.psum_tensor(f"{name}_{nc.next_id()}", shape, F32))

        with ExitStack() as inner:
            def begin():
                return inner.enter_context(nc.Block())
            yield sems, sbuf, psum, begin
    if sems:
        nc.clear_and_free_semaphores(sems)
        nc.all_engine_barrier()


RAW, CUT = 2, 4
AHEAD = CUT - 1


class Halves:

    def __init__(self, hi, lo):
        self.hi, self.lo = hi, lo

    def tile(self, t, T, rows=P):
        return self.hi[0:rows, t, 0:T], self.lo[0:rows, t, 0:T]


class WeightStream:

    def __init__(self, nc, ctx, stream):
        self.stream, self.total = stream, stream.shape[0]
        self.raw = ctx.enter_context(nc.sbuf_tensor("weights_raw", [P, RAW, KT * P], F32))
        self.hi = ctx.enter_context(nc.sbuf_tensor("weights_hi", [P, CUT, KT * P], F32R))
        self.lo = ctx.enter_context(nc.sbuf_tensor("weights_lo", [P, CUT, KT * P], F32R))
        self.raw_in = [nc.alloc_semaphore(f"weights_raw_in{i}") for i in range(RAW)]
        self.hi_done = nc.alloc_semaphore("weights_hi_done")
        self.lo_done = nc.alloc_semaphore("weights_lo_done")
        self.used = nc.alloc_semaphore("weights_used")
        self.next = 0

    def take(self, n):
        first, self.next = self.next, self.next + n
        return first

    def load(self, sp, first, c, r=0, per=0):
        at = first + c
        if not per and at >= self.total:
            return
        if at >= RAW or per:
            sp.wait_ge(self.lo_done, at + r * per - RAW + 1)
        sp.dma_start(self.raw[:, at % RAW, :], self.stream[bass.ds(at + r * per, 1)].rearrange("a p m -> p (a m)")
                     ).then_inc(self.raw_in[at % RAW], 16)

    def round(self, act, first, c, r=0, per=0):
        at = first + c
        if not per and at >= self.total:
            return
        act.wait_ge(self.raw_in[at % RAW], 16 * (at // RAW + 1) + r * (per // RAW) * 16)
        if at >= CUT or per:
            act.wait_ge(self.used, at + r * per - CUT + 1)
        act.activation(self.hi[:, at % CUT, :], self.raw[:, at % RAW, :], ACT.Copy).then_inc(self.hi_done, 1)

    def rest(self, pool, first, c, r=0, per=0):
        at = first + c
        if not per and at >= self.total:
            return
        pool.wait_ge(self.hi_done, at + r * per + 1)
        pool.tensor_tensor(self.lo[:, at % CUT, :], self.raw[:, at % RAW, :], self.hi[:, at % CUT, :].bitcast(F32),
                           ALU.subtract).then_inc(self.lo_done, 1)

    def ready(self, pe, first, c, r=0, per=0):
        pe.wait_ge(self.lo_done, first + c + r * per + 1)
        return (first + c) % CUT


def rounds(eng, steps, unroll, body):
    full = steps // unroll
    if full:
        body(0, unroll, True)
    if full > 2:
        with eng.Fori(1, full) as r:
            body(r, unroll, False)
    elif full == 2:
        body(1, unroll, False)
    if steps % unroll:
        body(full, steps % unroll, full == 0)


class Round:

    def __init__(self, first, r, per):
        if isinstance(r, int):
            self.args = lambda c: (first + r * per, c)
        else:
            self.args = lambda c: (first, c, r, per)


def products(pe, accs, w, passes_of, n):
    for half in range(n):
        cols = slice(half * w, (half + 1) * w)
        for start, stop, w_hi, w_lo, x_hi, x_lo in passes_of:
            pe.matmul(accs[half], w_hi, x_hi[:, cols], start=start, stop=False)
            pe.matmul(accs[half], w_hi, x_lo[:, cols], start=False, stop=False)
            last = pe.matmul(accs[half], w_lo, x_hi[:, cols], start=False, stop=stop)
    return last


class Phase:

    def __init__(self, steps, tiles, act_step=None, dve_step=None, act_links=0, dve_links=0, parts=None):
        self.steps, self.tiles, self.act_step, self.dve_step, self.parts = steps, tiles, act_step, dve_step, parts
        self.act_links, self.dve_links, self.cuts = act_links, dve_links, 0 if parts is None else 1
        self.per_step = sum((ks + KT - 1) // KT for _, ks, _ in tiles)


def project(nc, ws, steps, tiles, n, w, act_step=None, dve_step=None, unroll=2, act_links=0, dve_links=0, scratch=(),
            parts=None):
    project_phases(nc, ws, [Phase(steps, tiles, act_step, dve_step, act_links, dve_links, parts)], n, w, unroll, scratch)


def project_phases(nc, ws, phases, n, w, unroll, scratch=()):
    for number, ph in enumerate(phases):
        ph.first = ws.take(ph.per_step * ph.steps)
        ph.per = ph.per_step * unroll
        ph.base = sum(e.steps for e in phases[:number])
        ph.act_base = sum(e.steps * e.act_links for e in phases[:number])
        ph.dve_base = sum(e.steps * (e.dve_links + e.cuts) for e in phases[:number])
        assert ph.per % CUT == 0 or ph.steps <= 2 * unroll
        assert number == 0 or phases[number - 1].steps % unroll == 0
        assert ph.parts is None or number == len(phases) - 1
    with stage(nc, "act_done", "step_done", "act_link", "dve_link", "rest_done") as (sems, sbuf, psum, begin):
        act_done, step_done, act_link, dve_link, rest_done = sems
        tmp = {name: sbuf(name, [P, unroll] + shape) for name, shape in scratch}
        acc = psum("acc", [P, unroll, len(phases[0].tiles) * n, 512])
        block = begin()

        def out_of(u, j):
            return acc[:, u, j * n:(j + 1) * n, 0:w]

        @block.sync
        def _(sp):
            for ph in phases:
                def ahead(r, count, _):
                    at = Round(ph.first, r, ph.per)
                    for c in range(count * ph.per_step):
                        ws.load(sp, *at.args(c + AHEAD + RAW))
                rounds(sp, ph.steps, unroll, ahead)

        @block.gpsimd
        def _(pool):
            for ph in phases:
                def ahead(r, count, _):
                    at = Round(ph.first, r, ph.per)
                    for u in range(count):
                        for c in range(u * ph.per_step, (u + 1) * ph.per_step):
                            ws.rest(pool, *at.args(c + AHEAD))
                        if ph.parts is not None:
                            i = r * unroll + u
                            pool.wait_ge(step_done, ph.base + i + 1)
                            full, hi, lo = ph.parts
                            pool.tensor_tensor(lo(i), full(i, tmp, u), hi(i).bitcast(F32), ALU.subtract).then_inc(rest_done, 1)
                rounds(pool, ph.steps, unroll, ahead)

        @block.tensor
        def _(pe):
            for ph in phases:
                def multiply(r, count, start):
                    at = Round(ph.first, r, ph.per)
                    for u in range(count):
                        if not start or ph.base:
                            pe.wait_ge(step_done, ph.base + (r - 1) * unroll + u + 1)
                        c = u * ph.per_step
                        for j, (source, ks, rows) in enumerate(ph.tiles):
                            accs = [acc[:, u, j * n + half, 0:w] for half in range(n)]
                            for k0 in range(0, ks, KT):
                                slot = ws.ready(pe, *at.args(c))
                                passes = []
                                for k in range(k0, min(ks, k0 + KT)):
                                    block_of = slice((k - k0) * P, (k - k0 + 1) * P)
                                    passes.append((k == 0, k == ks - 1, ws.hi[0:rows, slot, block_of], ws.lo[0:rows, slot, block_of], *source(k)))
                                products(pe, accs, w, passes, n).then_inc(ws.used, 1)
                                c += 1
                rounds(pe, ph.steps, unroll, multiply)

        @block.scalar
        def _(act):
            for ph in phases:
                def finish(r, count, start):
                    at = Round(ph.first, r, ph.per)
                    for u in range(count):
                        i = r * unroll + u
                        for c in range(u * ph.per_step, (u + 1) * ph.per_step):
                            ws.round(act, *at.args(c + AHEAD))
                        if ph.act_step is not None:
                            act.wait_ge(ws.used, ph.first + (i + 1) * ph.per_step)
                            chain = Chain(act, act_link, ph.act_base + i * ph.act_links)
                            last = ph.act_step(act, chain, i, lambda j: out_of(u, j), {k: v[:, u] for k, v in tmp.items()})
                            last.then_inc(step_done if ph.dve_step is None else act_done, 1)
                            assert chain.n == ph.act_links
                rounds(act, ph.steps, unroll, finish)

        if any(ph.dve_step is not None for ph in phases):
            @block.vector
            def _(dve):
                for ph in phases:
                    def finish(r, count, start):
                        for u in range(count):
                            i = r * unroll + u
                            if ph.act_step is not None:
                                dve.wait_ge(act_done, ph.base + i + 1)
                            else:
                                dve.wait_ge(ws.used, ph.first + (i + 1) * ph.per_step)
                            if ph.parts is not None and not start:
                                dve.wait_ge(rest_done, (r - 1) * unroll + u + 1)
                            chain = Chain(dve, dve_link, ph.dve_base + i * (ph.dve_links + ph.cuts))
                            last = ph.dve_step(dve, chain, i, lambda j: out_of(u, j), {k: v[:, u] for k, v in tmp.items()})
                            if ph.parts is not None:
                                chain.link(last)
                                last = dve.tensor_copy(ph.parts[1](i), ph.parts[0](i, tmp, u))
                            last.then_inc(step_done, 1)
                            assert chain.n == ph.dve_links + ph.cuts, (chain.n, ph.dve_links)
                    rounds(dve, ph.steps, unroll, finish)


def project_tokens(nc, ws, pairs, source, tok, epilogue):
    nt = (tok + P - 1) // P
    first = ws.take(2 * pairs)
    assert first % 2 == 0
    with stage(nc, "products_done", "taken") as (sems, sbuf, psum, begin):
        products_done, taken = sems
        acc = psum("acc", [P, 8, 512])
        block = begin()

        @block.sync
        def _(sp):
            for c in range(2 * pairs):
                ws.load(sp, first, c + AHEAD + RAW)

        @block.gpsimd
        def _(pool):
            for c in range(2 * pairs):
                ws.rest(pool, first, c + AHEAD)

        @block.tensor
        def _(pe):
            for p in range(pairs):
                slot = ws.ready(pe, first, 2 * p)
                ws.ready(pe, first, 2 * p + 1)
                for t in range(nt):
                    rows = min(P, tok - t * P)
                    i = p * nt + t
                    if i >= 8:
                        pe.wait_ge(taken, i - 7)
                    out = acc[0:rows, i % 8, 0:2 * P]
                    for k in range(KT):
                        x_hi, x_lo = (a[:, t * P:t * P + rows] for a in source(k))
                        w_hi, w_lo = (a[:, slot:slot + 2, k * P:(k + 1) * P] for a in (ws.hi, ws.lo))
                        pe.matmul(out, x_hi, w_hi, start=k == 0, stop=False)
                        pe.matmul(out, x_lo, w_hi, start=False, stop=False)
                        last = pe.matmul(out, x_hi, w_lo, start=False, stop=k == KT - 1)
                    if t < nt - 1:
                        last.then_inc(products_done, 1)
                last.then_inc(ws.used, 2)

        @block.scalar
        def _(act):
            for p in range(pairs):
                ws.round(act, first, 2 * p + AHEAD)
                for t in range(nt):
                    rows = min(P, tok - t * P)
                    i = p * nt + t
                    if t < nt - 1:
                        act.wait_ge(products_done, p * (nt - 1) + t + 1)
                    else:
                        act.wait_ge(ws.used, first + 2 * p + 2)
                    epilogue(act, t, rows, p, acc[0:rows, i % 8, 0:2 * P]).then_inc(taken, 1)
                ws.round(act, first, 2 * p + 1 + AHEAD)


def rms_norm(nc, k, A, source, T, n, w, gain, shift=None, halves=None, dest=None):
    with stage(nc, "squared", "summed", "mean_done", "root_done", "scale_done", "spread", "loaded", "scaled", "full_done", "hi_done", "lo_done", "added") as (sems, sbuf, psum, begin):
        squared, summed, mean_done, root_done, scale_done, spread, loaded, scaled, full_done, hi_done, lo_done, added = sems
        sq = sbuf("sq", [P, 4, T])
        full = sbuf("full", [P, 4, T])
        quarter = T // 4
        scale = sbuf("scale", [4, 2, quarter])
        to_rows = sbuf("to_rows", [4, 4 * P])
        acc = psum("acc", [4, 512])
        wide = psum("wide", [P, n, 512])
        block = begin()

        def halved(a):
            return a.rearrange("p (n w) -> p n w", n=n)

        @block.sync
        def _(sp):
            sp.dma_start(to_rows[:, :], A["rows_of_tiles"][0:4, 0:4 * P]).then_inc(loaded, 16)

        @block.scalar
        def _(act):
            for t in range(0, KT, 2):
                if t >= 4:
                    act.wait_ge(summed, t - 3)
                act.activation(sq[:, t % 4, :], source(t), ACT.Square).then_inc(squared, 1)
            act.wait_ge(mean_done, 1)
            act.activation(scale[:, 1], scale[:, 0], ACT.Sqrt).then_inc(root_done, 1)
            if halves is not None:
                for t in range(KT):
                    act.wait_ge(scaled, t + 1)
                    if shift is not None:
                        act.activation(full[:, t % 4, :], full[:, t % 4, :], ACT.Identity, bias=shift(t)).then_inc(full_done, 1)
                        act.wait_ge(full_done, t + 1)
                    act.activation(halves.hi[:, t, 0:T], full[:, t % 4, :], ACT.Copy).then_inc(hi_done, 1)

        @block.gpsimd
        def _(pool):
            if halves is not None:
                for t in range(0, KT, 2):
                    pool.wait_ge(hi_done, t + 1)
                    pool.tensor_tensor(halves.lo[:, t, 0:T], full[:, t % 4, :], halves.hi[:, t, 0:T].bitcast(F32),
                                       ALU.subtract).then_inc(lo_done, 1)

        @block.tensor
        def _(pe):
            for t in range(KT):
                if t % 2 == 0:
                    pe.wait_ge(squared, t // 2 + 1)
                else:
                    pe.wait_ge(added, t // 2 + 1)
                G = k.select.shape[1] // 2
                for j in range(4):
                    last = pe.matmul(acc[:, 0:quarter], k.select[:, G - j:G - j + 4], sq[:, t % 4, j * quarter:(j + 1) * quarter],
                                     start=t == 0 and j == 0, stop=t == KT - 1 and j == 3)
                last.then_inc(summed, 1)
            pe.wait_ge(loaded, 16)
            pe.wait_ge(scale_done, 1)
            for j in range(4):
                at = j * quarter % w
                last = pe.matmul(wide[:, j * quarter // w, at:at + quarter], to_rows[:, j * P:(j + 1) * P], scale[:, 0], start=True, stop=True)
            last.then_inc(spread, 1)

        @block.vector
        def _(dve):
            for t in range(1, KT, 2):
                if t >= 4:
                    dve.wait_ge(summed, t - 3)
                dve.tensor_tensor(sq[:, t % 4, :], source(t), source(t), ALU.mult).then_inc(added, 1)
            dve.wait_ge(summed, KT)
            dve.tensor_scalar(scale[:, 0], acc[:, 0:quarter], 1.0 / D, EPS, ALU.mult, ALU.add).then_inc(mean_done, 1)
            dve.wait_ge(root_done, 1)
            dve.reciprocal(scale[:, 0], scale[:, 1]).then_inc(scale_done, 1)
            dve.wait_ge(spread, 1)

            def rest(t):
                dve.wait_ge(hi_done, t + 1)
                dve.tensor_tensor(halves.lo[:, t, 0:T], full[:, t % 4, :], halves.hi[:, t, 0:T].bitcast(F32), ALU.subtract).then_inc(added, 1)

            for t in range(KT):
                if halves is not None and t >= 4:
                    if t % 2 == 0:
                        dve.wait_ge(lo_done, t // 2 - 1)
                    else:
                        dve.wait_ge(added, KT // 2 + (t - 3) // 2)
                ins = dve.scalar_tensor_tensor(halved(full[:, t % 4, :]), halved(source(t)), gain(t), wide[:, :, 0:w], ALU.mult, ALU.mult)
                ins.then_inc(scaled, 1)
                if dest is not None:
                    dve.wait_ge(scaled, t + 1)
                    dve.tensor_tensor(dest(t), dest(t), full[:, t % 4, :], ALU.add).then_inc(added, 1)
                    if t >= 3:
                        dve.wait_ge(added, KT // 2 + t - 2)
                elif t >= 2 and t % 2 == 0:
                    rest(t - 1)
            if dest is None:
                rest(KT - 1)


def cut_tiles(nc, tiles):
    with stage(nc, "hi_done", "lo_done") as ((hi_done, lo_done), _, _, begin):
        block = begin()

        @block.scalar
        def _(act):
            for full, hi, lo in tiles:
                act.activation(hi, full, ACT.Copy).then_inc(hi_done, 1)

        @block.vector
        def _(dve):
            for i, (full, hi, lo) in enumerate(tiles):
                if i % 3 < 2:
                    dve.wait_ge(hi_done, i + 1)
                    dve.tensor_tensor(lo, full, hi.bitcast(F32), ALU.subtract).then_inc(lo_done, 1)

        @block.gpsimd
        def _(pool):
            for i, (full, hi, lo) in enumerate(tiles):
                if i % 3 == 2:
                    pool.wait_ge(hi_done, i + 1)
                    pool.tensor_tensor(lo, full, hi.bitcast(F32), ALU.subtract).then_inc(lo_done, 1)


def head_norms(nc, k, A, heads, dim, n, w, rows=P):
    per = max(1, P // dim)
    select, G = (k.half_select, k.half_select.shape[1] // 2) if per == 2 else (k.select, k.select.shape[1] // 2)
    groups = per * len(heads)
    with stage(nc, "squared", "summed", "mean_done", "root_done", "inverted", "spread", "done", "loaded") as (sems, sbuf, psum, begin):
        squared, summed, mean_done, root_done, inverted, spread, done, loaded = sems
        to_rows = sbuf("to_rows", [groups, len(heads) * P])
        sq = sbuf("sq", [P, 4, n * w])
        scale = sbuf("scale", [P, 2, n * w])
        acc = psum("acc", [P, n, 512])
        wide = psum("wide", [P, 2, n, 512])
        block = begin()

        def flat(a):
            return a.rearrange("p (a b) -> p a b", a=n)

        @block.sync
        def _(sp):
            sp.dma_start(to_rows[:, :], A["rows_of_halves" if per == 2 else "rows_of_tiles"][0:groups, 0:len(heads) * P]).then_inc(loaded, 16)

        @block.scalar
        def _(act):
            for i, (tile, _) in enumerate(heads):
                if i >= 4:
                    act.wait_ge(summed, i - 3)
                act.activation(sq[0:rows, i % 4], tile, ACT.Square).then_inc(squared, 1)
            act.wait_ge(mean_done, 1)
            act.activation(scale[0:groups, 1], scale[0:groups, 0], ACT.Sqrt).then_inc(root_done, 1)

        @block.tensor
        def _(pe):
            for i in range(len(heads)):
                pe.wait_ge(squared, i + 1)
                for half in range(n):
                    last = pe.matmul(acc[0:groups, half, 0:w], select[0:rows, G - per * i:G - per * i + groups],
                                     sq[0:rows, i % 4, half * w:(half + 1) * w], start=i == 0, stop=i == len(heads) - 1)
                last.then_inc(summed, 1)
            pe.wait_ge(loaded, 16)
            pe.wait_ge(inverted, 1)
            for i in range(len(heads)):
                if i >= 2:
                    pe.wait_ge(done, i - 1)
                for half in range(n):
                    last = pe.matmul(wide[0:rows, i % 2, half, 0:w], to_rows[:, i * P:i * P + rows], scale[0:groups, 0, half * w:(half + 1) * w], start=True, stop=True)
                last.then_inc(spread, 1)

        @block.vector
        def _(dve):
            dve.wait_ge(summed, len(heads))
            dve.tensor_scalar(flat(scale[0:groups, 0]), acc[0:groups, :, 0:w], 1.0 / dim, EPS, ALU.mult, ALU.add).then_inc(mean_done, 1)
            dve.wait_ge(root_done, 1)
            dve.reciprocal(scale[0:groups, 0], scale[0:groups, 1]).then_inc(inverted, 1)
            for i, (tile, gain) in enumerate(heads):
                dve.wait_ge(spread, i + 1)
                dve.scalar_tensor_tensor(flat(tile), flat(tile), gain, wide[0:rows, i % 2, :, 0:w], ALU.mult, ALU.mult).then_inc(done, 1)


class Part:

    def __init__(self, q, keys, table, values, gate=None, extra=None, penalty=None):
        self.q, self.keys, self.table, self.values = q, keys, table, values
        self.gate, self.extra, self.penalty = gate, extra, penalty
        self.nq, self.nk = q.shape[1], keys.shape[1]
        self.blocks = [(c, min(P, self.nk - c)) for c in range(0, self.nk, P)]


def attend(nc, k, groups, wide, longest=T2, build_tables=None, build_every=0):
    lag = 3
    weigh_lag = 2
    ns = lag + 1
    parts, of = [], []
    for g, (members, out) in enumerate(groups):
        for m, part in enumerate(members):
            parts.append(part)
            of.append((g, m == 0, m == len(members) - 1))
    N = len(parts)
    last_of = [max(i for i in range(N) if of[i][0] == g) for g in range(len(groups))]
    with stage(nc, "scores_ready", "max_ready", "exp_done", "row_inverted", "weights_ready", "turned", "turned_read",
               "weighted", "out_read", "biased", "built") as (sems, sbuf, psum, begin):
        scores_ready, max_ready, exp_done, row_inverted, weights_ready, turned, turned_read, weighted, out_read, biased, built = sems
        width = 1024 if wide else 512
        probs = sbuf("probs", [P, ns, longest])
        penalties = any(part.penalty is not None for part in parts)
        bias_sum = sbuf("bias_sum", [P, longest]) if penalties else None
        probs_t = sbuf("probs_t", [P, 2, 512])
        low = sbuf("low", [P, ns, 1])
        row_sum = sbuf("row_sum", [P, ns, 1])
        row_inv = sbuf("row_inv", [P, ns, 1])
        scores = psum("scores", [P, 2, width])
        turn = psum("turn", [P, 2, 512])
        out_acc = psum("out_acc", [P, 2, 512])
        block = begin()

        def turn_block(i, b, kb):
            nq = parts[i].nq
            return turn[0:kb, i % 2, b * nq:(b + 1) * nq]

        def out_at(g, part, out):
            base = out.start_partition()
            return out_acc[base:base + out.shape[0], g % 2, 0:part.nq]

        if build_tables is not None:
            @block.gpsimd
            def _(pool):
                for i in range(0, len(groups), build_every):
                    if i >= 2 * build_every:
                        pool.wait_ge(max_ready, last_of[i - build_every - 1] + 1)
                    build_tables(pool, i // build_every).then_inc(built, 1)

        @block.tensor
        def _(pe):
            for i in range(N + lag + 1):
                if i < N:
                    part = parts[i]
                    if i >= 2:
                        pe.wait_ge(max_ready, i - 1)
                    for c in range(0, part.nk, 512):
                        e = min(part.nk, c + 512)
                        last = pe.matmul(scores[0:part.nq, i % 2, c:e], part.q, part.keys[:, c:e],
                                         start=True, stop=part.extra is None)
                        if part.extra is not None:
                            last = pe.matmul(scores[0:part.nq, i % 2, c:e], part.extra[0][:, 0:part.nq], part.extra[1][:, c:e],
                                             start=False, stop=True)
                    last.then_inc(scores_ready, 1)
                if lag <= i < N + lag:
                    j = i - lag
                    part = parts[j]
                    pe.wait_ge(weights_ready, j + 1)
                    if j >= 2:
                        pe.wait_ge(turned_read, j - 1)
                    for b, (c, kb) in enumerate(part.blocks):
                        last = pe.transpose(turn_block(j, b, kb), probs[0:part.nq, j % ns, c:c + kb], k.ident[0:part.nq, 0:part.nq])
                    last.then_inc(turned, 1)
                if i >= lag + 1:
                    j = i - lag - 1
                    part = parts[j]
                    g, opens, closes = of[j]
                    pe.wait_ge(turned_read, j + 1)
                    if opens and g >= 2:
                        pe.wait_ge(out_read, g - 1)
                    for b, (c, kb) in enumerate(part.blocks):
                        last = pe.matmul(out_at(g, part, groups[g][1]), part.values[b], probs_t[0:kb, j % 2, b * part.nq:(b + 1) * part.nq],
                                         start=opens and b == 0, stop=closes and b == len(part.blocks) - 1)
                    last.then_inc(weighted, 1)

        @block.vector
        def _(dve):
            n_biased = 0
            def invert(j):
                nq = parts[j].nq
                dve.wait_ge(exp_done, j + 1)
                dve.reciprocal(row_inv[0:nq, j % ns, :], row_sum[0:nq, j % ns, :]).then_inc(row_inverted, 1)

            for i in range(N + weigh_lag):
                j = i - weigh_lag
                if j >= 0:
                    invert(j)
                if i < N:
                    part = parts[i]
                    table = part.table
                    if build_tables is not None and of[i][1] and of[i][0] % build_every == 0:
                        dve.wait_ge(built, of[i][0] // build_every + 1)
                    if part.penalty is not None:
                        if i >= 1:
                            dve.wait_ge(max_ready, i)
                        n_biased += 1
                        dve.tensor_tensor(bias_sum[0:part.nq, 0:part.nk], part.table, part.penalty, ALU.add).then_inc(biased, 1)
                        dve.wait_ge(biased, n_biased)
                        table = bias_sum[0:part.nq, 0:part.nk]
                    dve.wait_ge(scores_ready, i + 1)
                    if i >= ns:
                        dve.wait_ge(turned, i - ns + 1)
                    dve.tensor_tensor_reduce(probs[0:part.nq, i % ns, 0:part.nk], scores[0:part.nq, i % 2, 0:part.nk], table,
                                             1.0, 3e38, ALU.add, ALU.min, low[0:part.nq, i % ns, :]).then_inc(max_ready, 1)
                if j >= 0:
                    part = parts[j]
                    dve.wait_ge(row_inverted, j + 1)
                    rows = probs[0:part.nq, j % ns, 0:part.nk]
                    gated = () if part.gate is None else (ALU.mult,)
                    dve.tensor_scalar(rows, rows, row_inv[0:part.nq, j % ns, :], part.gate, ALU.mult, *gated).then_inc(weights_ready, 1)

        @block.scalar
        def _(act):
            def copy_out(g):
                part, out = parts[last_of[g]], groups[g][1]
                act.wait_ge(weighted, last_of[g] + 1)
                act.activation(out, out_at(g, part, out), ACT.Copy).then_inc(out_read, 1)

            g_next = 0
            for i in range(N + lag + 1):
                if lag <= i < N + lag:
                    j = i - lag
                    part = parts[j]
                    act.wait_ge(turned, j + 1)
                    if j >= 2:
                        act.wait_ge(weighted, j - 1)
                    rows = part.blocks[0][1]
                    full = [b for b in part.blocks if b[1] == rows]
                    rest = part.blocks[len(full):]
                    last = act.activation(probs_t[0:rows, j % 2, 0:len(full) * part.nq], turn[0:rows, j % 2, 0:len(full) * part.nq], ACT.Copy)
                    for b, (c, kb) in enumerate(rest, len(full)):
                        last = act.activation(probs_t[0:kb, j % 2, b * part.nq:(b + 1) * part.nq], turn_block(j, b, kb), ACT.Copy)
                    last.then_inc(turned_read, 1)
                if i < N:
                    part = parts[i]
                    act.wait_ge(max_ready, i + 1)
                    act.activation(probs[0:part.nq, i % ns, 0:part.nk], probs[0:part.nq, i % ns, 0:part.nk], ACT.Exp,
                                   bias=low[0:part.nq, i % ns, :], scale=-1.0,
                                   accum_out=row_sum[0:part.nq, i % ns, :]).then_inc(exp_done, 1)
                while g_next < len(groups) and last_of[g_next] <= i - lag - 2:
                    copy_out(g_next)
                    g_next += 1
            while g_next < len(groups):
                copy_out(g_next)
                g_next += 1


def tiles_of(buffer, n, w, offset=0):
    return lambda t: buffer[:, t, offset:offset + n * w]


def tile_at(buffer, i, n, w, offset=0):
    return buffer[:, bass.ds(i, 1), offset:offset + n * w].rearrange("p a (n w) -> p (a n) w", n=n)


def merge(nc, k, ws, h, branches, merged, n, w, opens=True, out=None):
    def phase(number, y, ks, rows, bias_at):
        first, last = opens and number == 0, number == len(branches) - 1

        def gate(act, chain, i, acc, tmp):
            bias = 0.0 if bias_at is None else k.vec[:, bass.ds(bias_at + i, 1)]
            return act.activation(tmp["gate"], acc(0), ACT.Sigmoid, bias=bias)

        def combine(dve, chain, i, acc, tmp):
            if first:
                return dve.tensor_tensor(tile_at(merged, i, n, w), tmp["gate"], acc(1), ALU.mult)
            chain.link(dve.tensor_tensor(tmp["gate"], tmp["gate"], acc(1), ALU.mult))
            return dve.tensor_tensor(tile_at(merged, i, n, w), tile_at(merged, i, n, w), tmp["gate"], ALU.add)

        parts = None
        if out is not None and last:
            parts = (lambda i, tmp, u: tile_at(merged, i, n, w), lambda i: tile_at(out.hi, i, n, w), lambda i: tile_at(out.lo, i, n, w))
        return Phase(KT, [(h, KT, P), (y, ks, rows)], gate, combine, dve_links=0 if first else 1, parts=parts)

    phases = [phase(number, *branch) for number, branch in enumerate(branches)]
    project_phases(nc, ws, phases, n, w, 4 if n == 1 else 2, scratch=[("gate", [n, w])])


def feed_forward(nc, k, ws, conv_w, conv_b, h, x, off, n, w):
    T, U = n * w, 2
    with ExitStack() as ctx:
        hidden = halves_of(nc, ctx, "hidden", FFT, T)
        steps, per = FFT, 2 * U
        first = ws.take(2 * steps)
        with stage(nc, "gate_copied", "conv_done", "silu_done", "step_done", "dve_link", "rest_done") as (sems, sbuf, psum, begin):
            gate_copied, conv_done, silu_done, step_done, dve_link, rest_done = sems
            gate_pad = sbuf("gate_pad", [P, U, 2 + T])
            conv = sbuf("conv", [P, U, T])
            full = sbuf("full", [P, U, n, w])
            acc = psum("acc", [P, U, 2, n, 512])
            block = begin()

            @block.sync
            def _(sp):
                def ahead(r, count, _):
                    at = Round(first, r, per)
                    for c in range(count * 2):
                        ws.load(sp, *at.args(c + AHEAD + RAW))
                rounds(sp, steps, U, ahead)

            @block.gpsimd
            def _(pool):
                def ahead(r, count, _):
                    at = Round(first, r, per)
                    for u in range(count):
                        for c in range(2 * u, 2 * u + 2):
                            ws.rest(pool, *at.args(c + AHEAD))
                        i = r * U + u
                        pool.wait_ge(step_done, i + 1)
                        pool.tensor_tensor(tile_at(hidden.lo, i, n, w), full[:, u], tile_at(hidden.hi, i, n, w).bitcast(F32),
                                           ALU.subtract).then_inc(rest_done, 1)
                rounds(pool, steps, U, ahead)

            @block.tensor
            def _(pe):
                def multiply(r, count, start):
                    at = Round(first, r, per)
                    for u in range(count):
                        if not start:
                            pe.wait_ge(step_done, (r - 1) * U + u + 1)
                        for j in range(2):
                            slot = ws.ready(pe, *at.args(2 * u + j))
                            passes = [(t == 0, t == KT - 1, ws.hi[:, slot, t * P:(t + 1) * P], ws.lo[:, slot, t * P:(t + 1) * P], *h(t))
                                      for t in range(KT)]
                            products(pe, [acc[:, u, j, half, 0:w] for half in range(n)], w, passes, n).then_inc(ws.used, 1)
                rounds(pe, steps, U, multiply)

            @block.scalar
            def _(act):
                def finish(r, count, start):
                    at = Round(first, r, per)
                    for u in range(count):
                        i = r * U + u
                        for c in range(2 * u, 2 * u + 2):
                            ws.round(act, *at.args(c + AHEAD))
                        act.wait_ge(ws.used, first + 2 * (i + 1))
                        act.activation(gate_pad[:, u, 2:2 + T].rearrange("p (n w) -> p n w", n=n), acc[:, u, 0, :, 0:w],
                                       ACT.Copy).then_inc(gate_copied, 1)
                        act.wait_ge(conv_done, i + 1)
                        act.activation(conv[:, u, :], conv[:, u, :], ACT.Silu).then_inc(silu_done, 1)
                rounds(act, steps, U, finish)

            @block.vector
            def _(dve):
                pads = Chain(dve, dve_link)
                pads.link(dve.memset(gate_pad[:, :, 0:2], 0.0))

                def finish(r, count, start):
                    for u in range(count):
                        i = r * U + u
                        chain = Chain(dve, dve_link, 1 + i * 3)
                        taps = [k.vec[:, bass.ds(conv_w + FFT * tap + i, 1)] for tap in range(3)]
                        dve.wait_ge(gate_copied, i + 1)
                        chain.link(dve.tensor_scalar(conv[:, u, :], gate_pad[:, u, 0:T], taps[0],
                                                     k.vec[:, bass.ds(conv_b + i, 1)], ALU.mult, ALU.add))
                        chain.link(dve.scalar_tensor_tensor(conv[:, u, :], gate_pad[:, u, 1:1 + T], taps[1], conv[:, u, :], ALU.mult, ALU.add))
                        dve.scalar_tensor_tensor(conv[:, u, :], gate_pad[:, u, 2:2 + T], taps[2], conv[:, u, :],
                                                 ALU.mult, ALU.add).then_inc(conv_done, 1)
                        dve.wait_ge(silu_done, i + 1)
                        if not start:
                            dve.wait_ge(rest_done, (r - 1) * U + u + 1)
                        chain.link(dve.tensor_tensor(full[:, u], conv[:, u, :].rearrange("p (n w) -> p n w", n=n), acc[:, u, 1, :, 0:w], ALU.mult))
                        dve.tensor_copy(tile_at(hidden.hi, i, n, w), full[:, u]).then_inc(step_done, 1)
                rounds(dve, steps, U, finish)

        project(nc, ws, KT, [(lambda t: hidden.tile(t, T), FFT, P)], n, w, None,
                lambda dve, chain, i, acc, tmp: dve.tensor_tensor(tile_at(x, i, n, w, off), tile_at(x, i, n, w, off), acc(0), ALU.add),
                unroll=4)


def halves_of(nc, ctx, name, tiles, T):
    return Halves(*(ctx.enter_context(nc.sbuf_tensor(f"{name}_{part}_{nc.next_id()}", [P, tiles, T], F32R)) for part in ("hi", "lo")))


def parts_of(halves, name, n, w):
    return (lambda i, tmp, u: tmp[name][:, u], lambda i: tile_at(halves.hi, i, n, w), lambda i: tile_at(halves.lo, i, n, w))


def copies(dest, n, w, scale=1.0, at=0):
    return lambda act, chain, i, acc, tmp: act.activation(tile_at(dest, i + at, n, w), acc(0), ACT.Copy, scale=scale)



def modulation(nc, k, A, ws, b, const):
    tiles, ring_size = 3 * KT, 8
    with stage(nc, "c_loaded", "c_ready", "summed", "ada_link", "vec_loaded", "loaded", *[f"weights_in{u}" for u in range(ring_size)]) as (sems, sbuf, psum, begin):
        c_loaded, c_ready, summed, ada_link, vec_loaded, loaded = sems[:6]
        weights_in = sems[6:]
        ring = sbuf("weight_ring", [P, ring_size, D])
        c_row = sbuf("c_row", [P, D])
        product = sbuf("product", [P, 2, D])
        block = begin()

        @block.sync
        def _(sp):
            sp.dma_start(c_row[:, :], A["c_row"].partition_broadcast(P)).then_inc(c_loaded, 16)
            for i in range(tiles):
                if i >= ring_size:
                    sp.wait_ge(summed, i - ring_size + 1)
                sp.dma_start(ring[:, i % ring_size, :], A["w_ada"][i]).then_inc(weights_in[i % ring_size], 16)
            for c in range(RAW + AHEAD):
                ws.load(sp, 0, c)
            sp.wait_ge(loaded, 48)

        @block.scalar
        def _(act):
            act.dma_start(k.vec[:, :], A["vec"]).then_inc(vec_loaded, 16)
            act.dma_start(b.x[:, :, META:T2], A["x"]).then_inc(loaded, 16)
            act.dma_start(b.x[:, :, 0:META], A["meta"]).then_inc(loaded, 16)
            act.dma_start(const[:, :], A["const"]).then_inc(loaded, 16)
            act.wait_ge(c_loaded, 16)
            act.activation(c_row[:, :], c_row[:, :], ACT.Silu).then_inc(c_ready, 1)
            for c in range(AHEAD):
                ws.round(act, 0, c)

        @block.gpsimd
        def _(pool):
            for c in range(AHEAD):
                ws.rest(pool, 0, c)

        @block.vector
        def _(dve):
            dve.wait_ge(c_ready, 1)
            for i in range(tiles):
                dve.wait_ge(weights_in[i % ring_size], 16 * (i // ring_size + 1))
                if i >= 2:
                    dve.wait_ge(summed, i - 1)
                dve.tensor_tensor_reduce(product[:, i % 2, :], ring[:, i % ring_size, :], c_row[:, :], 1.0, 0.0, ALU.mult, ALU.add,
                                         k.ada[:, i:i + 1]).then_inc(summed, 1)
            chain = Chain(dve, ada_link)
            dve.wait_ge(summed, tiles)
            dve.wait_ge(vec_loaded, 16)
            chain.link(dve.tensor_tensor(k.ada[:, :], k.ada[:, :], k.col("b_ada"), ALU.add))
            chain.link(dve.scalar_tensor_tensor(k.ada[:, KT:2 * KT], k.ada[:, KT:2 * KT], 1.0, k.col("g_pre"), ALU.add, ALU.mult))
            chain.link(dve.tensor_tensor(k.ada[:, 2 * KT:], k.ada[:, 2 * KT:], k.col("g_post"), ALU.mult))


def conv_mixer(nc, k, ws, h, y):
    cw, cb = k.at("conv_w"), k.at("conv_b")

    def ahead(act, chain, i, acc, tmp):
        act.activation(tmp["xin"], acc(2), ACT.Copy)
        return act.activation(tmp["z"], acc(3), ACT.Silu)

    def mix(dve, chain, i, acc, tmp):
        pad, conv = tmp["pad"], tmp["conv"]
        chain.link(dve.memset(pad[:, 0:2], 0.0))
        chain.link(dve.tensor_tensor(pad[:, 2:2 + S].unsqueeze(1), acc(1), tmp["xin"], ALU.mult))
        taps = [k.vec[:, bass.ds(cw + KT * tap + i, 1)] for tap in range(3)]
        chain.link(dve.tensor_scalar(conv, pad[:, 0:S], taps[0], k.vec[:, bass.ds(cb + i, 1)], ALU.mult, ALU.add))
        chain.link(dve.scalar_tensor_tensor(conv, pad[:, 1:1 + S], taps[1], conv, ALU.mult, ALU.add))
        chain.link(dve.scalar_tensor_tensor(conv, pad[:, 2:2 + S], taps[2], conv, ALU.mult, ALU.add))
        chain.link(dve.tensor_tensor(conv.unsqueeze(1), conv.unsqueeze(1), acc(0), ALU.mult))
        return dve.tensor_tensor(tmp["z"], conv.unsqueeze(1), tmp["z"], ALU.mult)

    project(nc, ws, KT, [(h, KT, P)] * 4, 1, S, ahead, mix, dve_links=6,
            scratch=[("xin", [1, S]), ("z", [1, S]), ("pad", [2 + S]), ("conv", [S])], parts=parts_of(y, "z", 1, S))


def compress(nc, k, A, kv, k_cmp, v_cmp):
    with stage(nc, "loaded", "hidden_ready", "pos_copied", "hidden_done", "out_ready", "copied") as (sems, sbuf, psum, begin):
        loaded, hidden_ready, pos_copied, hidden_done, out_ready, copied = sems
        w1 = sbuf("w1", [P, 2, 16, P])
        pos = sbuf("pos", [P, 2, 16])
        w2 = sbuf("w2", [P, 2, P])
        pos_term = sbuf("pos_term", [P, 2])
        hidden = sbuf("hidden", [P, 2, NKV * N_CMP])
        acc = psum("acc", [P, 2, 512])
        pos_acc = psum("pos_acc", [P, 2, 512])
        out = psum("out", [P, 2, 512])
        block = begin()

        @block.sync
        def _(sp):
            sp.dma_start(w1[:, :, :, :], A["w_cmp1"]).then_inc(loaded, 16)
            sp.dma_start(pos[:, :, :], A["pos_cmp"]).then_inc(loaded, 16)
            sp.dma_start(w2[:, :, :], A["w_cmp2"]).then_inc(loaded, 16)

        @block.tensor
        def _(pe):
            pe.wait_ge(loaded, 48)
            for a in range(2):
                for s in range(16):
                    pe.matmul(acc[:, a, 0:NKV * N_CMP].rearrange("p (g n) -> p g n", g=NKV), w1[:, a, s, :],
                              kv[:, a * NKV:(a + 1) * NKV, 2 * s:2 * s + 16 * (N_CMP - 1) + 1:16], start=s == 0, stop=s == 15)
                for s in range(16):
                    last = pe.matmul(pos_acc[:, a, 0:1], w1[:, a, s, :], pos[:, a, s:s + 1], start=s == 0, stop=s == 15)
                last.then_inc(hidden_ready, 1)
            pe.wait_ge(hidden_done, 1)
            pe.matmul(out[:, 0, 0:NKV * N_CMP], w2[:, 0, :], hidden[:, 0, :], start=True, stop=True).then_inc(out_ready, 1)
            pe.wait_ge(hidden_done, 2)
            for g in range(NKV):
                last = pe.matmul(out[0:N_CMP, 1, g * HD:(g + 1) * HD], hidden[:, 1, g * N_CMP:(g + 1) * N_CMP], w2[:, 1, 0:HD],
                                 start=True, stop=True)
            last.then_inc(out_ready, 1)

        @block.vector
        def _(dve):
            for a in range(2):
                dve.wait_ge(hidden_ready, a + 1)
                dve.tensor_copy(pos_term[:, a:a + 1], pos_acc[:, a, 0:1]).then_inc(pos_copied, 1)
            dve.wait_ge(out_ready, 1)
            for odd in range(2):
                rows = slice(odd * HD, (odd + 1) * HD)
                dve.tensor_copy(k_cmp[rows, odd, :], out[rows, 0, 0:NKV * N_CMP]).then_inc(copied, 1)
            dve.wait_ge(out_ready, 2)
            dve.tensor_copy(v_cmp[0:N_CMP, :], out[0:N_CMP, 1, 0:NKV * HD]).then_inc(copied, 1)

        @block.scalar
        def _(act):
            for a in range(2):
                act.wait_ge(pos_copied, a + 1)
                act.activation(hidden[:, a, :], acc[:, a, 0:NKV * N_CMP], ACT.Silu, bias=pos_term[:, a:a + 1]).then_inc(hidden_done, 1)


def sparse_mixer(nc, k, A, ws, h, branch):
    q = branch.enter_context(nc.sbuf_tensor(f"q_{nc.next_id()}", [P, KT, S], F32))
    y = q
    with ExitStack() as ctx:
        def sbuf(name, shape):
            return ctx.enter_context(nc.sbuf_tensor(f"{name}_{nc.next_id()}", shape, F32))

        k_cmp = sbuf("k_cmp", [P, 2, NKV * N_CMP])
        v_cmp = sbuf("v_cmp", [N_CMP, NKV * HD])
        project(nc, ws, KT, [(h, KT, P)], 1, S, copies(q, 1, S, Q_SCALE), unroll=4)
        with nc.sbuf_tensor(f"kv_cmp_{nc.next_id()}", [P, 2 * NKV, S], F32) as kv:

            def spread(copy, i, half, acc):
                rows = acc(0)[half * HD:(half + 1) * HD]
                copy(kv[0:HD, 2 * i + half, :], rows[:, 0, :])
                return copy(kv[HD:P, 2 * i + half, 0:S - 1], rows[:, 0, 1:S])

            project(nc, ws, NKV, [(h, KT, P)], 1, S,
                    lambda act, chain, i, acc, tmp: spread(lambda out, a: act.activation(out, a, ACT.Copy), i, 0, acc),
                    lambda dve, chain, i, acc, tmp: spread(dve.tensor_copy, i, 1, acc), unroll=4)
            compress(nc, k, A, kv, k_cmp, v_cmp)
        keys = sbuf("keys_t", [P, 2, 2 * NKV, S])
        v_tok = sbuf("v_tok", [P, S // P, 2 * NKV * HD])
        gates = sbuf("gates", [P, S // P, 3 * NH])

        def split(copy, i, half, acc):
            rows = acc(0)[half * HD:(half + 1) * HD, 0, :]
            copy(keys[0:HD, 0, 2 * i + half, :], rows)
            return copy(keys[HD:P, 1, 2 * i + half, :], rows)

        project(nc, ws, NKV, [(h, KT, P)], 1, S,
                lambda act, chain, i, acc, tmp: split(lambda out, a: act.activation(out, a, ACT.Copy), i, 0, acc),
                lambda dve, chain, i, acc, tmp: split(dve.tensor_copy, i, 1, acc), unroll=4)

        def take(act, t, rows, p, acc):
            if p < 2:
                return act.activation(v_tok[0:rows, t, p * 2 * P:(p + 1) * 2 * P], acc, ACT.Copy)
            return act.activation(gates[0:rows, t, :], acc[:, 0:3 * NH], ACT.Sigmoid)

        project_tokens(nc, ws, 3, h, S, take)
        distance = sbuf("distance", [P, TAB])
        distance_cmp = sbuf("distance_cmp", [P, 4 * N_CMP])
        with stage(nc, "hidden", "loaded", "emptied") as ((hidden, loaded, emptied), _, _, begin):
            block = begin()

            @block.sync
            def _(sp):
                sp.dma_start(distance[:, :], A["distance"]).then_inc(loaded, 16)
                sp.dma_start(distance_cmp[:, :], A["distance_cmp"]).then_inc(loaded, 16)
                sp.wait_ge(loaded, 32)

            @block.vector
            def _(dve):
                first = gates[:, 0, 0:3 * NH:3]
                dve.tensor_scalar(first, first, k.sees_cmp, None, ALU.mult).then_inc(hidden, 1)
                dve.memset(keys[HD:P, 0], 0.0).then_inc(emptied, 1)

            @block.gpsimd
            def _(pool):
                pool.memset(keys[0:HD, 1], 0.0).then_inc(emptied, 1)
                pool.memset(k_cmp[HD:P, 0], 0.0).then_inc(emptied, 1)
                pool.memset(k_cmp[0:HD, 1], 0.0).then_inc(emptied, 1)

        table = sbuf("alibi", [P, 2, TAB])
        table_cmp = sbuf("alibi_cmp", [P, 2, 4 * N_CMP])
        slopes = [float(np.float32(2.0) ** np.float32(-8.0 * i / NH)) for i in range(1, NH + 1)]

        def build_tables(pool, head):
            pool.tensor_scalar(table_cmp[:, head % 2, :], distance_cmp[:, :], slopes[head], None, ALU.mult)
            return pool.tensor_scalar(table[:, head % 2, :], distance[:, :], slopes[head], None, ALU.mult)

        groups = []
        for head in range(NH):
            base, g = (head % 2) * HD, head // (NH // NKV)
            rows = slice(base, base + HD)
            for t in range(S // P):
                cols = slice(t * P, (t + 1) * P)
                qb = q[:, head // 2, cols]
                members = [Part(qb, k_cmp[:, head % 2, g * N_CMP:(g + 1) * N_CMP], table_cmp[:, head % 2, t * N_CMP:(t + 1) * N_CMP],
                                [v_cmp[0:N_CMP, g * HD:(g + 1) * HD]], gate=gates[:, t, 3 * head:3 * head + 1])]
                for kind in range(2):
                    c = (kind * NKV + g) * HD
                    members.append(Part(qb, keys[:, head % 2, kind * NKV + g, 0:(t + 1) * P], table[:, head % 2, OFF - t * P:TAB],
                                        [v_tok[:, b, c:c + HD] for b in range(t + 1)],
                                        gate=gates[:, t, 3 * head + 1 + kind:3 * head + 2 + kind]))
                groups.append((members, y[rows, head // 2, cols]))
        attend(nc, k, groups, wide=False, longest=S, build_tables=build_tables, build_every=S // P)

    out = halves_of(nc, branch, "y", KT, S)
    project(nc, ws, KT, [(h, KT, P)], 1, S,
            lambda act, chain, i, acc, tmp: act.activation(tmp["z"], acc(0), ACT.Silu),
            lambda dve, chain, i, acc, tmp: dve.tensor_tensor(tile_at(y, i, 1, S), tile_at(y, i, 1, S), tmp["z"], ALU.mult),
            unroll=4, scratch=[("z", [1, S])],
            parts=(lambda i, tmp, u: tile_at(y, i, 1, S), lambda i: tile_at(out.hi, i, 1, S), lambda i: tile_at(out.lo, i, 1, S)))
    return out


def gmlp_mixer(nc, k, A, ws, h, y):
    chunks = S // P
    with ExitStack() as ctx:
        mixed = ctx.enter_context(nc.sbuf_tensor(f"mixed_{nc.next_id()}", [P, KT, S], F32))
        inner = ctx.enter_context(ExitStack())
        v_tok = inner.enter_context(nc.sbuf_tensor(f"v_tok_{nc.next_id()}", [P, chunks, MIX], F32))
        project_tokens(nc, ws, MIX // (2 * P), h, S,
                       lambda act, t, rows, p, acc: act.activation(v_tok[0:rows, t, p * 2 * P:(p + 1) * 2 * P], acc, ACT.Gelu_apprx_tanh))
        with stage(nc, "loaded", "mask_done", "var_ready", "root_done", "normed", "mixed_ready", "taken", "dve_link") as (sems, sbuf, psum, begin):
            loaded, mask_done, var_ready, root_done, normed, mixed_ready, taken, dve_link = sems
            w_s = sbuf("w_s", [P, KT, P])
            b_s = sbuf("b_s", [P, KT, P])
            ln = sbuf("ln", [P, 2, MIX])
            stats = sbuf("stats", [P, 2, 6])
            moments = sbuf("moments", [P, chunks, 2])
            root = sbuf("root", [P, chunks, 2])
            acc = psum("acc", [P, 2, chunks, P])
            block = begin()

            @block.sync
            def _(sp):
                sp.dma_start(w_s[:, :, :], A["w_s_t"]).then_inc(loaded, 16)
                sp.dma_start(b_s[:, :, :], A["b_s"].partition_broadcast(P)).then_inc(loaded, 16)
                sp.dma_start(ln[:, 0, :], A["ln_g"].partition_broadcast(P)).then_inc(loaded, 16)
                sp.dma_start(ln[:, 1, :], A["ln_b"].partition_broadcast(P)).then_inc(loaded, 16)

            @block.gpsimd
            def _(pool):
                pool.wait_ge(loaded, 64)
                pool.affine_select(w_s[:, :, :], w_s[:, :, :], pattern=[[0, KT], [1, P]], compare_op=ALU.is_ge, fill=0.0, base=0,
                                   channel_multiplier=-1).then_inc(mask_done, 1)

            @block.vector
            def _(dve):
                chain = Chain(dve, dve_link)
                for t in range(chunks):
                    chain.link(dve.bn_stats(stats[:, 0, :], v_tok[:, t, 0:512]))
                    chain.link(dve.bn_stats(stats[:, 1, :], v_tok[:, t, 512:1024]))
                    chain.link(dve.bn_aggr(moments[:, t, :], stats[:, :, :]))
                    dve.tensor_scalar(root[:, t, 0:1], moments[:, t, 1:2], EPS, None, ALU.add).then_inc(var_ready, 1)
                dve.wait_ge(loaded, 64)
                for t in range(chunks):
                    dve.wait_ge(root_done, t + 1)
                    chain.link(dve.reciprocal(root[:, t, 0:1], root[:, t, 1:2]))
                    chain.link(dve.tensor_scalar(v_tok[:, t, :], v_tok[:, t, :], moments[:, t, 0:1], root[:, t, 0:1], ALU.subtract, ALU.mult))
                    chain.link(dve.tensor_tensor(v_tok[:, t, :], v_tok[:, t, :], ln[:, 0, :], ALU.mult))
                    dve.tensor_tensor(v_tok[:, t, :], v_tok[:, t, :], ln[:, 1, :], ALU.add).then_inc(normed, 1)
                for g in range(KT):
                    dve.wait_ge(mixed_ready, g + 1)
                    dve.tensor_tensor(mixed[:, g, :].rearrange("p (n i) -> p n i", i=P), acc[:, g % 2],
                                      b_s[:, g:g + 1, :].to_broadcast([P, chunks, P]), ALU.add).then_inc(taken, 1)

            @block.scalar
            def _(act):
                for t in range(chunks):
                    act.wait_ge(var_ready, t + 1)
                    act.activation(root[:, t, 1:2], root[:, t, 0:1], ACT.Sqrt).then_inc(root_done, 1)

            @block.tensor
            def _(pe):
                pe.wait_ge(mask_done, 1)
                pe.wait_ge(normed, chunks)
                for g in range(KT):
                    if g >= 2:
                        pe.wait_ge(taken, g - 1)
                    for t in range(chunks):
                        last = pe.matmul(acc[:, g % 2, t, :], v_tok[:, t, g * P:(g + 1) * P], w_s[:, g, :], start=True, stop=True)
                    last.then_inc(mixed_ready, 1)

        inner.close()

        def ahead(act, chain, i, acc, tmp):
            act.activation(tmp["u"], acc(0), ACT.Gelu_apprx_tanh)
            return act.activation(tmp["z"], acc(1), ACT.Silu)

        def mix(dve, chain, i, acc, tmp):
            chain.link(dve.tensor_tensor(tmp["u"], tmp["u"], tile_at(mixed, i, 1, S), ALU.mult))
            return dve.tensor_tensor(tmp["u"], tmp["u"], tmp["z"], ALU.mult)

        project(nc, ws, KT, [(h, KT, P)] * 2, 1, S, ahead, mix, dve_links=1, scratch=[("u", [1, S]), ("z", [1, S])],
                parts=parts_of(y, "u", 1, S))


def first_block(nc, k, A, ws, b, const):
    n, w = 1, S
    x = tiles_of(b.x, n, w, META)
    modulation(nc, k, A, ws, b, const)
    with ExitStack() as ctx:
        halves = halves_of(nc, ctx, "h", KT, S)
        h = lambda t: halves.tile(t, S)
        rms_norm(nc, k, A, x, S, n, w, lambda t: k.ada[:, KT + t:KT + t + 1], lambda t: k.ada[:, t:t + 1], halves=halves)
        merged = ctx.enter_context(nc.sbuf_tensor(f"merged_{nc.next_id()}", [P, KT, S], F32))
        with ExitStack() as branch:
            y = sparse_mixer(nc, k, A, ws, h, branch)
            merge(nc, k, ws, h, [(lambda t: y.tile(t, S), KT, P, None)], merged, n, w)
        with ExitStack() as branch:
            y = halves_of(nc, branch, "y", KT, S)
            conv_mixer(nc, k, ws, h, y)
            merge(nc, k, ws, h, [(lambda t: y.tile(t, S), KT, P, None)], merged, n, w, opens=False)
            gmlp_mixer(nc, k, A, ws, h, y)
            out = halves_of(nc, branch, "merged", KT, S)
            merge(nc, k, ws, h, [(lambda t: y.tile(t, S), KT, P, None)], merged, n, w, opens=False, out=out)
            project(nc, ws, KT, [(lambda t: out.tile(t, S), KT, P)], n, w, copies(merged, n, w), unroll=4)
        rms_norm(nc, k, A, tiles_of(merged, n, w), S, n, w, lambda t: k.ada[:, 2 * KT + t:2 * KT + t + 1], dest=x)



SB_Q, SP_Q, DF_Q, QM2 = 0, 2, 4, 8
SB_K, SP_K, IX_Q, IX_K, DF_K, FM2 = 0, 2, 4, 6, 7, 11
SB_V, SP_V, DF_V, IX_W, TM2 = 0, 256, 512, 1024, 1032
N2, W2 = 2, T2 // 2
QT2 = (T2 + P - 1) // P
ROWS2 = [min(P, T2 - t * P) for t in range(QT2)]
REPLACED = -3e38
PAD = -2e30


def stick_breaking(nc, k, A, qm, fm, v_tok):
    scale = HD ** -0.5
    units = [(head, half) for head in range(4) for half in range(N2)]
    kbs = {half: [kb for kb in reversed(range(QT2)) if kb * P < (half + 1) * W2] for half in range(N2)}
    steps = [(u, head, half, kb) for u, (head, half) in enumerate(units) for kb in kbs[half]]
    N, U, RING = len(steps), len(units), 4
    of_unit = [[i for i in range(N) if steps[i][0] == u] for u in range(U)] + [[]]
    names = ["scores_ready", "masked_done", "abs_done", "exp_done", "log_done", "relu_done", "soft_done", "sums_ready", "exponent_ready",
             "weights_done", "weighed", "out_copied", "hidden", "loaded"]
    with stage(nc, *names) as (sems, sbuf, psum, begin):
        (scores_ready, masked_done, abs_done, exp_done, log_done, relu_done, soft_done, sums_ready, exponent_ready, weights_done, weighed,
         out_copied, hidden, loaded) = sems
        before = sbuf("before", list(A["before"].shape))
        hide = sbuf("hide", list(A["before"].shape))
        masked = sbuf("masked", [P, 2, QT2, W2])
        log_part = sbuf("log_part", [P, 2, QT2, W2])
        soft = sbuf("soft", [P, 2, QT2, W2])
        scores = psum("scores", [P, RING, 512])
        sums = psum("sums", [P, 2, 512])
        out = psum("out", [P, 2, 512])
        block = begin()

        def window(half, kb):
            c = half * W2 - kb * P + 256
            return slice(c, c + W2)

        def spans(u):
            out = [(P, slice(0, min(len(of_unit[u]), QT2 - 1)))]
            if len(of_unit[u]) == QT2:
                out.append((ROWS2[QT2 - 1], slice(QT2 - 1, QT2)))
            return out

        spans_to = [sum(len(spans(v)) for v in range(u)) for u in range(U + 1)]
        steps_to = [sum(len(of_unit[v]) for v in range(u)) for u in range(U + 1)]

        def in_turn_steps(*units_of):
            longest = max(len(of_unit[u]) for u in units_of)
            return [(which, of_unit[u][n]) for n in range(longest) for which, u in enumerate(units_of) if n < len(of_unit[u])]

        @block.sync
        def _(sp):
            sp.dma_start(before[:, :], A["before"]).then_inc(loaded, 16)

        @block.tensor
        def _(pe):
            def score(i):
                u, head, half, kb = steps[i]
                rows = slice((head % 2) * HD, (head % 2) * HD + HD)
                if i >= RING:
                    pe.wait_ge(masked_done, i - RING + 1)
                pe.matmul(scores[0:ROWS2[kb], i % RING, 0:W2], fm[rows, SB_K + head // 2, kb * P:kb * P + ROWS2[kb]],
                          qm[rows, SB_Q + head // 2, half * W2:(half + 1) * W2], start=True, stop=True).then_inc(scores_ready, 1)

            def add_up(i):
                u, head, half, kb = steps[i]
                pe.wait_ge(soft_done, i + 1)
                if i >= 2:
                    pe.wait_ge(exponent_ready, i - 1)
                after = [b for b in kbs[half] if b > kb]
                for b in after:
                    pe.matmul(sums[0:ROWS2[kb], i % 2, 0:W2], k.ones[0:ROWS2[b], 0:ROWS2[kb]], soft[0:ROWS2[b], u % 2, b, :],
                              start=b == after[0], stop=False)
                pe.matmul(sums[0:ROWS2[kb], i % 2, 0:W2], k.later[0:ROWS2[kb], 0:ROWS2[kb]], soft[0:ROWS2[kb], u % 2, kb, :],
                          start=not after, stop=True).then_inc(sums_ready, 1)

            def weigh(u):
                head, half = units[u]
                base = (head % 2) * HD
                pe.wait_ge(weights_done, spans_to[u + 1])
                if u >= 2:
                    pe.wait_ge(out_copied, u - 1)
                for i in of_unit[u]:
                    kb = steps[i][3]
                    last = pe.matmul(out[base:base + HD, u % 2, 0:W2], v_tok[0:ROWS2[kb], kb, SB_V + head * HD:SB_V + (head + 1) * HD],
                                     masked[0:ROWS2[kb], u % 2, kb, :], start=i == of_unit[u][0], stop=i == of_unit[u][-1])
                last.then_inc(weighed, 1)

            for i in of_unit[0]:
                score(i)
            for u in range(U + 1):
                if u >= 1:
                    weigh(u - 1)
                if u < U:
                    for which, i in in_turn_steps(u + 1, u):
                        if which == 0:
                            score(i)
                        else:
                            add_up(i)

        @block.scalar
        def _(act):
            for u in range(U + 1):
                if u < U:
                    for i in of_unit[u]:
                        r, kb = ROWS2[steps[i][3]], steps[i][3]
                        act.wait_ge(scores_ready, i + 1)
                        if u >= 2:
                            act.wait_ge(relu_done, spans_to[u - 1])
                        act.activation(log_part[0:r, u % 2, kb, :], scores[0:r, i % RING, 0:W2], ACT.Abs, scale=scale).then_inc(abs_done, 1)
                    act.wait_ge(abs_done, steps_to[u + 1])
                    for r, span in spans(u):
                        part = log_part[0:r, u % 2, span, :]
                        act.activation(part, part, ACT.Exp, scale=-1.0).then_inc(exp_done, 1)
                if u >= 1:
                    act.wait_ge(exponent_ready, steps_to[u])
                    for r, span in spans(u - 1):
                        part = masked[0:r, (u - 1) % 2, span, :]
                        act.activation(part, part, ACT.Exp).then_inc(weights_done, 1)
                if u < U:
                    act.wait_ge(exp_done, spans_to[u + 1])
                    for r, span in spans(u):
                        part = log_part[0:r, u % 2, span, :]
                        act.activation(part, part, ACT.Ln, bias=1.0).then_inc(log_done, 1)
                if u >= 1:
                    head, half = units[u - 1]
                    rows = slice((head % 2) * HD, (head % 2) * HD + HD)
                    act.wait_ge(weighed, u)
                    act.activation(qm[rows, SB_Q + head // 2, half * W2:(half + 1) * W2], out[rows, (u - 1) % 2, 0:W2],
                                   ACT.Copy).then_inc(out_copied, 1)

        @block.vector
        def _(dve):
            dve.wait_ge(loaded, 16)
            dve.tensor_scalar(hide[:, :], before[:, :], 1.0, BIG, ALU.subtract, ALU.mult).then_inc(hidden, 1)
            dve.wait_ge(hidden, 1)

            def mask(i):
                u, head, half, kb = steps[i]
                r = ROWS2[kb]
                dve.wait_ge(abs_done, i + 1)
                if u >= 2:
                    dve.wait_ge(weighed, u - 1)
                dve.scalar_tensor_tensor(masked[0:r, u % 2, kb, :], scores[0:r, i % RING, 0:W2], scale, hide[0:r, window(half, kb)],
                                         ALU.mult, ALU.add).then_inc(masked_done, 1)

            def exponent(i):
                u, head, half, kb = steps[i]
                r = ROWS2[kb]
                dve.wait_ge(sums_ready, i + 1)
                dve.tensor_tensor(masked[0:r, u % 2, kb, :], masked[0:r, u % 2, kb, :], sums[0:r, i % 2, 0:W2],
                                  ALU.subtract).then_inc(exponent_ready, 1)

            for i in of_unit[0]:
                mask(i)
            for u in range(U):
                dve.wait_ge(masked_done, steps_to[u + 1])
                for n, (r, span) in enumerate(spans(u)):
                    dve.wait_ge(log_done, spans_to[u] + n + 1)
                    if u >= 2:
                        dve.wait_ge(sums_ready, steps_to[u - 1])
                    dve.scalar_tensor_tensor(soft[0:r, u % 2, span, :], masked[0:r, u % 2, span, :], 0.0, log_part[0:r, u % 2, span, :],
                                             ALU.max, ALU.add).then_inc(relu_done, 1)
                dve.wait_ge(relu_done, spans_to[u + 1])
                for i in of_unit[u]:
                    _, head, half, kb = steps[i]
                    r = ROWS2[kb]
                    dve.tensor_tensor(soft[0:r, u % 2, kb, :], soft[0:r, u % 2, kb, :], before[0:r, window(half, kb)], ALU.mult).then_inc(soft_done, 1)
                for which, i in in_turn_steps(u + 1, u):
                    if which == 0:
                        mask(i)
                    else:
                        exponent(i)


def keys_and_tables(nc, k, A, fm, v_tok, penalty, scratch, table):
    heads = 8
    full_rounds, rest = divmod(TOP_K, 8)
    jobs = [(t, j) for t in range(1, QT2) for j in range(heads)]
    RING, width = 3, TAB + P - 1
    half = (width + 1) // 2
    row_parts = [(0, half), (half, width)]
    names = ["dots_ready", "relu_done", "added", "loaded", "rows_ready", "rows_copied", "rows_stored", "table_in", "turned", "turned_copied"]
    with stage(nc, *names, "link0", "link1") as (sems, sbuf, psum, begin):
        dots_ready, relu_done, added, loaded, rows_ready, rows_copied, rows_stored, table_in, turned, turned_copied = sems[:len(names)]
        by_bucket = sbuf("by_bucket", [33, 8])
        bucket = sbuf("bucket", [33, width])
        bias_rows = sbuf("bias_rows", [8, width])
        flipped = sbuf("flipped", [P, TAB])
        rows_acc = psum("rows_acc", [8, 2, 512])
        turn = psum("turn", [P, 2, 512])
        relu = sbuf("relu", [P, RING, T2])
        scores = sbuf("scores", [P, 2, T2 + 8])
        tops = sbuf("tops", [P, 2, 8])
        dots = psum("dots", [P, 2, 1024])
        block = begin()

        def keys_of(t):
            return min((t + 1) * P, T2)

        @block.sync
        def _(sp):
            sp.dma_start(by_bucket[:, :], A["rel_bias"]).then_inc(loaded, 16)
            sp.dma_start(bucket[:, :], A["bucket"]).then_inc(loaded, 16)
            sp.wait_ge(rows_copied, 2)
            sp.dma_start(scratch, bias_rows[:, :]).then_inc(rows_stored, 16)
            sp.wait_ge(rows_stored, 16)
            for head in range(8):
                if head >= 1:
                    sp.wait_ge(turned, head)
                src = bass.AP(tensor=scratch.tensor, offset=head * width, ap=[[1, P], [1, TAB]])
                sp.dma_start(flipped[:, :], src).then_inc(table_in, 16)

        @block.tensor
        def _(pe):
            pe.wait_ge(loaded, 32)
            for i, (a, e) in enumerate(row_parts):
                pe.matmul(rows_acc[:, i, 0:e - a], by_bucket[:, :], bucket[:, a:e], start=True, stop=True).then_inc(rows_ready, 1)

            def turn_tables():
                for head in range(8):
                    pe.wait_ge(table_in, 16 * (head + 1))
                    if head >= 1:
                        pe.wait_ge(turned_copied, head)
                    for i in range(2):
                        last = pe.matmul(turn[:, i, 0:TAB // 2], k.mirror, flipped[:, i * TAB // 2:(i + 1) * TAB // 2], start=True, stop=True)
                    last.then_inc(turned, 1)

            for i, (t, j) in enumerate(jobs):
                if i == 2 * heads:
                    turn_tables()
                rows = slice((j % 4) * 32, (j % 4) * 32 + 32)
                if i >= 2:
                    pe.wait_ge(relu_done, i - 1)
                for c in range(0, keys_of(t), 512):
                    e = min(c + 512, keys_of(t))
                    last = pe.matmul(dots[0:ROWS2[t], i % 2, c:e], fm[rows, IX_Q + j // 4, t * P:t * P + ROWS2[t]], fm[rows, IX_K, c:e],
                                     start=True, stop=True, tile_position=((j % 4) * 32, 0))
                last.then_inc(dots_ready, 1)

        @block.scalar
        def _(act):
            for i, (a, e) in enumerate(row_parts):
                act.wait_ge(rows_ready, i + 1)
                act.activation(bias_rows[:, a:e], rows_acc[:, i, 0:e - a], ACT.Copy).then_inc(rows_copied, 1)

            def copy_tables():
                for head in range(8):
                    act.wait_ge(turned, head + 1)
                    act.activation(table[:, head, :].rearrange("p (a b) -> p a b", a=2), turn[:, :, 0:TAB // 2], ACT.Copy).then_inc(turned_copied, 1)

            for i, (t, j) in enumerate(jobs):
                if i == 2 * heads:
                    copy_tables()
                act.wait_ge(dots_ready, i + 1)
                if i >= RING:
                    act.wait_ge(added, i - RING + 1)
                act.activation(relu[0:ROWS2[t], i % RING, 0:keys_of(t)], dots[0:ROWS2[t], i % 2, 0:keys_of(t)], ACT.Relu).then_inc(relu_done, 1)

        @block.vector
        def _(dve):
            chains = [Chain(dve, link) for link in sems[len(names):]]
            for t0 in range(1, QT2, 2):
                blocks = [t for t in (t0, t0 + 1) if t < QT2]
                for i, (t, j) in enumerate(jobs):
                    if t not in blocks:
                        continue
                    chain, r, nk = chains[t - t0], ROWS2[t], keys_of(t)
                    s = scores[0:r, t - t0, 0:nk]
                    weight = v_tok[0:r, t, IX_W + j:IX_W + j + 1]
                    chain.after()
                    dve.wait_ge(relu_done, i + 1)
                    if j == 0:
                        ins = dve.tensor_scalar(s, relu[0:r, i % RING, 0:nk], weight, None, ALU.mult)
                    else:
                        dve.wait_ge(added, i)
                        ins = dve.scalar_tensor_tensor(s, relu[0:r, i % RING, 0:nk], weight, s, ALU.mult, ALU.add)
                    ins.then_inc(added, 1)
                dve.wait_ge(added, (blocks[-1]) * heads)
                for t in blocks:
                    chain, r, nk = chains[t - t0], ROWS2[t], keys_of(t)
                    s = scores[0:r, t - t0, 0:nk]
                    chain.add(dve.tensor_tensor(s, s, k.causal[0:r, OFF - t * P:OFF - t * P + nk], ALU.subtract))
                    chain.add(dve.memset(scores[0:r, t - t0, nk:nk + 8], PAD))
                for n in range(full_rounds + (rest > 0)):
                    for t in blocks:
                        chain, r, nk = chains[t - t0], ROWS2[t], keys_of(t)
                        chain.after()
                        chain.add(dve.max(tops[0:r, t - t0, :], scores[0:r, t - t0, 0:nk + 8]))
                    if n == full_rounds:
                        for t in blocks:
                            chains[t - t0].after()
                            chains[t - t0].add(dve.memset(tops[0:ROWS2[t], t - t0, rest:8], PAD))
                    for t in blocks:
                        chain, r, nk = chains[t - t0], ROWS2[t], keys_of(t)
                        s = scores[0:r, t - t0, 0:nk + 8]
                        chain.after()
                        chain.add(dve.match_replace(s, tops[0:r, t - t0, :], s, REPLACED))
                for t in blocks:
                    chain, r, nk = chains[t - t0], ROWS2[t], keys_of(t)
                    chain.after()
                    chain.add(dve.tensor_scalar(penalty[0:r, t, 0:nk], scores[0:r, t - t0, 0:nk], REPLACED, BIG, ALU.not_equal, ALU.mult))


def mixing_scalars(nc, k, neg_lam, q_sp, q_df):
    with stage(nc, "products_ready", "sums_ready", "exp_done", "link") as (sems, sbuf, psum, begin):
        products_ready, sums_ready, exp_done, dve_link = sems
        prod = sbuf("prod", [P, 2])
        e = sbuf("e", [P, 2])
        acc = psum("acc", [P, 2])
        block = begin()

        @block.vector
        def _(dve):
            chain = Chain(dve, dve_link)
            lam = k.col("lam")
            dve.tensor_tensor(prod[:, :], lam[:, 0:2], lam[:, 2:4], ALU.mult).then_inc(products_ready, 1)
            chain.link(dve.tensor_scalar(q_sp, k.col("q_norm_sp"), Q_SCALE, None, ALU.mult))
            chain.link(dve.tensor_scalar(q_df, k.col("q_norm_df"), Q_SCALE, None, ALU.mult))
            dve.wait_ge(exp_done, 1)
            chain.link(dve.tensor_tensor(neg_lam, e[:, 1:2], e[:, 0:1], ALU.subtract))
            chain.link(dve.tensor_scalar(neg_lam, neg_lam, LAM_INIT, None, ALU.subtract))

        @block.tensor
        def _(pe):
            pe.wait_ge(products_ready, 1)
            pe.matmul(acc[:, :], k.ones, prod[:, :], start=True, stop=True).then_inc(sums_ready, 1)

        @block.scalar
        def _(act):
            act.wait_ge(sums_ready, 1)
            act.activation(e[:, :], acc[:, :], ACT.Exp).then_inc(exp_done, 1)


def scale_columns(nc, out, col, factor):
    with stage(nc, "scaled") as ((scaled,), _, _, begin):
        block = begin()

        @block.vector
        def _(dve):
            dve.tensor_scalar(out, col, factor, None, ALU.mult).then_inc(scaled, 1)


def second_attention(nc, k, A, ws, h, qm, scratch):
    n, w = N2, W2
    with ExitStack() as ctx:
        def sbuf(name, shape):
            return ctx.enter_context(nc.sbuf_tensor(f"{name}_{nc.next_id()}", shape, F32))

        fm = sbuf("fm", [P, FM2, T2])
        v_tok = sbuf("v_tok", [P, QT2, TM2])
        small = sbuf("small", [P, 4])
        def take(act, t, rows, p, acc):
            width = min(2 * P, TM2 - p * 2 * P)
            return act.activation(v_tok[0:rows, t, p * 2 * P:p * 2 * P + width], acc[:, 0:width], ACT.Copy)

        project_tokens(nc, ws, (TM2 + 2 * P - 1) // (2 * P), h, T2, take)
        project_phases(nc, ws, [Phase(QM2, [(h, KT, P)], copies(qm, n, w)), Phase(FM2, [(h, KT, P)], copies(fm, n, w))], n, w, unroll=4)
        mixing_scalars(nc, k, small[:, 0:1], small[:, 1:2], small[:, 2:3])
        scale_columns(nc, small[:, 3:4], k.col("subln_df"), 1.0 - LAM_INIT)
        queries, tiles = tiles_of(qm, n, w), tiles_of(fm, n, w)
        head_norms(nc, k, A, [(queries(SP_Q + i), small[:, 1:2]) for i in range(2)] + [(tiles(SP_K + i), k.col("k_norm_sp")) for i in range(2)]
                   + [(queries(DF_Q + i), small[:, 2:3]) for i in range(4)] + [(tiles(DF_K + i), k.col("k_norm_df")) for i in range(4)],
                   HD, n, w)
        stick_breaking(nc, k, A, qm, fm, v_tok)
        table = sbuf("table", [P, 8, TAB])
        penalty = sbuf("penalty", [P, QT2, T2])
        keys_and_tables(nc, k, A, fm, v_tok, penalty, scratch, table)
        groups = []
        for t in range(QT2):
            nq, nk = ROWS2[t], min((t + 1) * P, T2)
            cols = slice(t * P, t * P + nq)
            for head in range(4):
                rows = slice((head % 2) * HD, (head % 2) * HD + HD)
                groups.append(([Part(qm[rows, SP_Q + head // 2, cols], fm[rows, SP_K + head // 2, 0:nk],
                                     table[0:nq, head, OFF - t * P:OFF - t * P + nk],
                                     [v_tok[0:ROWS2[b], b, SP_V + head * HD:SP_V + (head + 1) * HD] for b in range(t + 1)],
                                     penalty=penalty[0:nq, t, 0:nk] if t >= 1 else None)], qm[rows, SP_Q + head // 2, cols]))
            for head in range(4):
                members = []
                for m in range(2):
                    rows = slice(m * HD, (m + 1) * HD)
                    members.append(Part(qm[rows, DF_Q + head, cols], fm[rows, DF_K + head, 0:nk],
                                        table[0:nq, 4 + head, OFF - t * P:OFF - t * P + nk],
                                        [v_tok[0:ROWS2[b], b, DF_V + head * P:DF_V + (head + 1) * P] for b in range(t + 1)],
                                        gate=small[0:nq, 0:1] if m == 1 else None))
                groups.append((members, qm[:, DF_Q + head, cols]))
        attend(nc, k, groups, wide=True)
        head_norms(nc, k, A, [(queries(DF_Q + head), small[:, 3:4]) for head in range(4)], P, n, w)


def second_block(nc, k, A, ws, b, scratch):
    n, w = N2, W2
    x = tiles_of(b.x, n, w)
    norm, gate = k.at("attn_norm"), k.at("b_gate")
    with ExitStack() as ctx:
        halves = halves_of(nc, ctx, "h", KT, T2)
        h = lambda t: halves.tile(t, T2)
        rms_norm(nc, k, A, x, T2, n, w, lambda t: k.vec[:, norm + t:norm + t + 1], halves=halves)
        qm = ctx.enter_context(nc.sbuf_tensor(f"qm_{nc.next_id()}", [P, QM2, T2], F32))
        second_attention(nc, k, A, ws, h, qm, scratch)
        cut = halves_of(nc, ctx, "y", KT, T2)
        cut_tiles(nc, [(qm[:, t, :], *cut.tile(t, T2)) for t in range(KT)])
        out = halves_of(nc, ctx, "merged", KT, T2)
        merged = qm
        branches = [(lambda t, at=at: cut.tile(at + t, T2), ks, P, gate + i * KT) for i, (at, ks) in enumerate([(SB_Q, 2), (SP_Q, 2), (DF_Q, 4)])]
        merge(nc, k, ws, h, branches, merged, n, w, out=out)
        project(nc, ws, KT, [(lambda t: out.tile(t, T2), KT, P)], n, w, None,
                lambda dve, chain, i, acc, tmp: dve.tensor_tensor(tile_at(b.x, i, n, w), tile_at(b.x, i, n, w), acc(0), ALU.add), unroll=4)
    ffn = k.at("ffn_norm")
    with ExitStack() as ctx:
        halves = halves_of(nc, ctx, "h", KT, T2)
        rms_norm(nc, k, A, x, T2, n, w, lambda t: k.vec[:, ffn + t:ffn + t + 1], halves=halves)
        feed_forward(nc, k, ws, k.at("conv_w_2"), k.at("conv_b_2"), lambda t: halves.tile(t, T2), b.x, 0, n, w)


def lay_out_second(v, A):
    w = v["w_in_2"][0]
    widths = [256] * 6 + [256, 32, 8, 512, 512, 512, D, D, D]
    at = np.concatenate([[0], np.cumsum(widths)])
    part = lambda i: w[:, at[i]:at[i + 1]]
    A["rel_bias"] = np.concatenate([v["rel_bias_2"], np.ones((1, 8), np.float32)])
    A["bucket"] = buckets()
    tiles = padded_tiles(np.concatenate([part(2), part(5), part(11), part(8)], axis=1), 2 * P)
    tiles += [tiled(part(0)), tiled(part(3)), tiled(part(9))]
    tiles += [tiled(part(1)), tiled(part(4)), tiled(part(6)), doubled(part(7), 32, 4), tiled(part(10))]
    for i, name in enumerate(("w_br_sb_2", "w_br_sp_2", "w_br_df_2")):
        tiles += in_turn(tiled(part(12 + i)), tiled(v[name][0]))
    tiles += [tiled(v["w_out_2"][0])]
    return tiles + ff_tiles(v["w_up_2"][0], v["w_down_2"][0])



FQ, HQ, CA, QM3 = 0, 3, 7, 9
FK, HF, HG_G, CB, FF, FM3 = 0, 3, 7, 11, 13, 14
FV, HV, TM3 = 0, FOX * HD, 2 * FOX * HD
LEVELS = [1, 2, 4, 8, 16, 32]
TILES3 = S // P
CHUNKS = S // CH
CONV_TILES = 2


def forget_sums(nc, k, A, fm, ff, sums, fox_rows, keys):
    with stage(nc, "link", "ones_done", "log_done", "loaded", "emptied", "copied") as (sems, sbuf, psum, begin):
        dve_link, ones_done, log_done, loaded, emptied, copied = sems
        a = sbuf("a", [FOX, 3, S])
        ones = sbuf("ones", [FOX, S])
        block = begin()

        @block.vector
        def _(dve):
            chain = Chain(dve, dve_link)
            dve.memset(ones[:, :], 1.0).then_inc(ones_done, 1)
            dve.tensor_copy(keys[HD:P, 1], fm[HD:P, FK:FK + FOX // 2, 0:S]).then_inc(copied, 1)
            dve.wait_ge(ones_done, 1)
            chain.link(dve.tensor_scalar(a[:, 0, :], ff, k.one("fox_forget_b")[0:FOX], -1.0, ALU.add, ALU.mult))
            dve.wait_ge(log_done, 3)
            chain.link(dve.scalar_tensor_tensor(a[:, 2, :], a[:, 0, :], 0.0, a[:, 1, :], ALU.max, ALU.add))
            chain.link(dve.tensor_tensor_scan(sums, ones[:, :], a[:, 2, :], 0.0, ALU.mult, ALU.add))

        @block.sync
        def _(sp):
            sp.dma_start(fox_rows[:, :], A["fox_rows"]).then_inc(loaded, 16)
            sp.wait_ge(loaded, 16)

        @block.gpsimd
        def _(pool):
            pool.memset(keys[HD:P, 0], 0.0).then_inc(emptied, 1)
            pool.memset(keys[0:HD, 1], 0.0).then_inc(emptied, 1)

        @block.scalar
        def _(act):
            act.activation(keys[0:HD, 0], fm[0:HD, FK:FK + FOX // 2, 0:S], ACT.Copy).then_inc(copied, 1)
            act.wait_ge(dve_link, 1)
            chain = Chain(act, log_done)
            chain.link(act.activation(a[:, 1, :], a[:, 0, :], ACT.Abs))
            chain.link(act.activation(a[:, 1, :], a[:, 1, :], ACT.Exp, scale=-1.0))
            chain.link(act.activation(a[:, 1, :], a[:, 1, :], ACT.Ln, bias=1.0))


def hgrn(nc, k, A, qm, fm, v_tok):
    names = ["hf_done", "gate_link", "key_done", "sums_done", "apart_done", "decay_done", "k_done", "q_done", "pairs_ready", "pairs_taken",
             "ends_apart", "last_done", "kd_done", "turned", "turned_copied", "update_ready", "state_done", "out_ready", "out_copied", "loaded", "gate_done", "padded", "conv_done"]
    with stage(nc, *names) as (sems, sbuf, psum, begin):
        (hf_done, gate_link, key_done, sums_done, apart_done, decay_done, k_done, q_done, pairs_ready, pairs_taken,
         ends_apart, last_done, kd_done, turned, turned_copied, update_ready, state_done, out_ready, out_copied, loaded, gate_done, padded, conv_done) = sems
        masks = sbuf("masks", [P, 1 + len(LEVELS), P], mybir.dt.uint32)
        resets = sbuf("resets", [P, S])
        sums = sbuf("sums", [P, HG, S])
        apart = sbuf("apart", [P, 2, S])
        decay = sbuf("decay", [P, 2, S])
        k_part = sbuf("k_part", [P, 2, S])
        q_part = sbuf("q_part", [P, 2, S])
        pairs = sbuf("pairs", [P, 2, TILES3, P])
        q_in = sbuf("q_in", [P, 2, S])
        kd = sbuf("kd", [P, S])
        kd_tok = sbuf("kd_tok", [P, TILES3, P])
        last = sbuf("last", [P, 2, CHUNKS])
        states = sbuf("states", [P, 2, CHUNKS - 1, HG_V])
        back = CONV_W - 1
        pad = sbuf("pad", [P, CONV_TILES, back + S])
        pair_acc = psum("pair_acc", [P, 2, TILES3, P])
        turn_acc = psum("turn_acc", [P, TILES3, P])
        update = psum("update", [P, 2, 512])
        out = psum("out", [P, 2, 512])
        block = begin()
        NL = len(LEVELS)

        def halves(a, m):
            return a.rearrange("p (n a m) -> p n a m", a=2, m=m)

        def key(head):
            return fm[:, HF + head, 0:S]

        def update_at(c):
            return update[:, c % 2, (c // 2) * HG_V:(c // 2 + 1) * HG_V]

        @block.sync
        def _(sp):
            sp.dma_start(masks[:, :, :], A["level_masks"]).then_inc(loaded, 16)
            sp.dma_start(resets[:, :], A["resets"]).then_inc(loaded, 16)

        @block.scalar
        def _(act):
            links = Chain(act, gate_link)
            hf = fm[:, HF:HF + HG, 0:S]
            links.link(act.activation(sums[:, :, :], hf, ACT.Abs))
            links.link(act.activation(sums[:, :, :], sums[:, :, :], ACT.Exp, scale=-1.0))
            act.activation(sums[:, :, :], sums[:, :, :], ACT.Ln, bias=1.0).then_inc(hf_done, 1)
            act.wait_ge(sums_done, 1)
            act.activation(hf, hf, ACT.Sigmoid, scale=-1.0).then_inc(key_done, 1)
            for t in range(CONV_TILES):
                act.activation(fm[:, CB + t, 0:S], fm[:, CB + t, 0:S], ACT.Sigmoid).then_inc(gate_done, 1)

            def copy_out(head):
                act.wait_ge(out_ready, head + 1)
                act.activation(qm[0:HG_V, HQ + head, :], out[0:HG_V, head % 2, :], ACT.Copy).then_inc(out_copied, 1)

            for head in range(HG):
                act.wait_ge(ends_apart, head + 1)
                if head >= 2:
                    act.wait_ge(out_ready, head - 1)
                act.activation(q_in[:, head % 2, :], sums[:, head, :], ACT.Exp, scale=-1.0).then_inc(last_done, 1)
                act.activation(last[:, head % 2, :], sums[:, head, CH - 1:S:CH], ACT.Exp, scale=-1.0).then_inc(last_done, 1)
                act.activation(kd[:, :], kd[:, :], ACT.Exp).then_inc(last_done, 1)
                for l in range(NL):
                    i = head * NL + l
                    act.wait_ge(apart_done, 2 * (i + 1))
                    if i >= 2:
                        act.wait_ge(k_done, i - 1)
                        act.wait_ge(q_done, i - 1)
                    act.activation(decay[:, i % 2, :], apart[:, i % 2, :], ACT.Exp).then_inc(decay_done, 1)
                    if l == 1 and head >= 1:
                        copy_out(head - 1)
                    if l == 3:
                        act.wait_ge(turned, head + 1)
                        if head >= 1:
                            act.wait_ge(update_ready, head)
                        act.activation(kd_tok[:, :, :], turn_acc[:, :, :], ACT.Copy).then_inc(turned_copied, 1)
            copy_out(HG - 1)

        @block.gpsimd
        def _(pool):
            for i in range(HG * NL):
                pool.wait_ge(decay_done, i + 1)
                if i >= 2:
                    pool.wait_ge(pairs_ready, (i - 2) // NL * (NL + 1) + (i - 2) % NL + 2)
                pool.tensor_tensor(k_part[:, i % 2, :], key(i // NL), decay[:, i % 2, :], ALU.mult).then_inc(k_done, 1)

        @block.vector
        def _(dve):
            PIECES = 4 * NL - 8
            assert HG * PIECES >= CONV_W * CONV_TILES

            def convolve(head, a, e):
                for piece in range(head * PIECES + a, min(head * PIECES + e, CONV_W * CONV_TILES)):
                    i, t = divmod(piece, CONV_TILES)
                    conv, tap = fm[:, CB + t, 0:S], k.one("dw_w", piece)
                    if i >= 1:
                        dve.wait_ge(conv_done, piece - CONV_TILES + 1)
                        ins = dve.scalar_tensor_tensor(conv, pad[:, t, i:i + S], tap, conv, ALU.mult, ALU.add)
                    else:
                        ins = dve.tensor_scalar(conv, pad[:, t, 0:S], tap, k.one("dw_b", t), ALU.mult, ALU.add)
                    ins.then_inc(conv_done, 1)

            dve.memset(pad[:, :, 0:back], 0.0).then_inc(padded, 1)
            dve.wait_ge(loaded, 32)
            dve.wait_ge(hf_done, 1)
            dve.scalar_tensor_tensor(sums[:, :, :], fm[:, HF:HF + HG, 0:S], 0.0, sums[:, :, :], ALU.min, ALU.subtract).then_inc(sums_done, 1)
            dve.wait_ge(sums_done, 1)
            for head in range(HG):
                dve.tensor_tensor_scan(sums[:, head, :], resets[:, :], sums[:, head, :], 0.0, ALU.mult, ALU.subtract).then_inc(sums_done, 1)
            dve.wait_ge(sums_done, 1 + HG)
            dve.wait_ge(key_done, 1)
            for t in range(CONV_TILES):
                dve.wait_ge(gate_done, t + 1)
                dve.tensor_tensor(pad[:, t, back:back + S], qm[:, CA + t, 0:S], fm[:, CB + t, 0:S], ALU.mult).then_inc(padded, 1)
            dve.wait_ge(padded, 1 + CONV_TILES)
            for head in range(HG):
                q = qm[:, HQ + head, 0:S]
                keys, b = key(head), sums[:, head, :]
                if head >= 1:
                    dve.wait_ge(turned, head)
                ends = b.rearrange("p (c t) -> p c t", t=CH)[:, :, CH - 1:CH].to_broadcast([P, CHUNKS, CH])
                dve.tensor_tensor(kd[:, :].rearrange("p (c t) -> p c t", t=CH), b.rearrange("p (c t) -> p c t", t=CH), ends,
                                  ALU.subtract).then_inc(ends_apart, 1)
                dve.wait_ge(pairs_ready, head * (NL + 1) + 1)
                if head >= 2:
                    dve.wait_ge(out_ready, head - 1)
                dve.tensor_tensor(pairs[:, head % 2], pair_acc[:, (head * (NL + 1)) % 2], masks[:, 0:1, :].to_broadcast([P, TILES3, P]),
                                  ALU.mult).then_inc(pairs_taken, 1)
                dve.wait_ge(pairs_taken, head * (NL + 1) + 1)

                def split(l):
                    i = head * NL + l
                    m = LEVELS[l]
                    if i >= 2:
                        dve.wait_ge(decay_done, i - 1)
                    to, of = halves(apart[:, i % 2, :], m), halves(b, m)
                    meet = of[:, :, 0, m - 1:m].to_broadcast([P, S // (2 * m), m])
                    dve.tensor_tensor(to[:, :, 0, :], of[:, :, 0, :], meet, ALU.subtract).then_inc(apart_done, 1)
                    dve.tensor_tensor(to[:, :, 1, :], meet, of[:, :, 1, :], ALU.subtract).then_inc(apart_done, 1)

                def weigh_queries(l):
                    i = head * NL + l
                    dve.wait_ge(decay_done, i + 1)
                    if i >= 2:
                        dve.wait_ge(pairs_ready, (i - 2) // NL * (NL + 1) + (i - 2) % NL + 2)
                    dve.tensor_tensor(q_part[:, i % 2, :], q, decay[:, i % 2, :], ALU.mult).then_inc(q_done, 1)

                def take(l):
                    n = head * (NL + 1) + 1 + l
                    dve.wait_ge(pairs_ready, n + 1)
                    dve.copy_predicated(pairs[:, head % 2], masks[:, l + 1:l + 2, :].to_broadcast([P, TILES3, P]),
                                        pair_acc[:, n % 2]).then_inc(pairs_taken, 1)
                    dve.wait_ge(pairs_taken, n + 1)

                def weigh_ends():
                    dve.wait_ge(last_done, 3 * (head + 1))
                    dve.tensor_tensor(q_in[:, head % 2, :], q_in[:, head % 2, :], q, ALU.mult).then_inc(kd_done, 1)
                    dve.tensor_tensor(kd[:, :], kd[:, :], keys, ALU.mult).then_inc(kd_done, 1)

                def carry():
                    dve.wait_ge(update_ready, head + 1)
                    if head >= 2:
                        dve.wait_ge(out_ready, head - 1)
                    for c in range(CHUNKS - 1):
                        if c == 0:
                            ins = dve.tensor_copy(states[:, head % 2, 0, :], update_at(0))
                        else:
                            ins = dve.scalar_tensor_tensor(states[:, head % 2, c, :], states[:, head % 2, c - 1, :], last[:, head % 2, c:c + 1],
                                                           update_at(c), ALU.mult, ALU.add)
                        ins.then_inc(state_done, 1)
                        dve.wait_ge(state_done, head * (CHUNKS - 1) + c + 1)

                split(0)
                for l in range(NL):
                    if l + 1 < NL:
                        split(l + 1)
                    convolve(head, 2 * l, 2 * l + 1)
                    weigh_queries(l)
                    convolve(head, 2 * l + 1, 2 * l + 2)
                    if l >= 1:
                        take(l - 1)
                    if l == 1:
                        weigh_ends()
                convolve(head, 2 * NL, PIECES)
                carry()
                take(NL - 1)

        @block.tensor
        def _(pe):
            pe.wait_ge(key_done, 1)

            def multiply(head):
                if head >= 2:
                    pe.wait_ge(out_copied, head - 1)
                pe.wait_ge(pairs_taken, (head + 1) * (NL + 1))
                pe.wait_ge(state_done, (head + 1) * (CHUNKS - 1))
                for t in range(TILES3):
                    pe.matmul(out[0:HG_V, head % 2, t * P:(t + 1) * P], v_tok[:, t, HV + head * HG_V:HV + (head + 1) * HG_V],
                              pairs[:, head % 2, t, :], start=True, stop=False)
                    for c in range(max(1, 2 * t), 2 * t + 2):
                        mm = pe.matmul(out[0:HG_V, head % 2, c * CH:(c + 1) * CH], states[:, head % 2, c - 1, :],
                                       q_in[:, head % 2, c * CH:(c + 1) * CH], start=False, stop=c == 2 * t + 1)
                mm.then_inc(out_ready, 1)

            for head in range(HG):
                q, keys = qm[:, HQ + head, 0:S], key(head)
                def turn():
                    pe.wait_ge(kd_done, 2 * (head + 1))
                    if head >= 1:
                        pe.wait_ge(turned_copied, head)
                    for t in range(TILES3):
                        mm = pe.transpose(turn_acc[:, t, :], kd[:, t * P:(t + 1) * P], k.ident)
                    mm.then_inc(turned, 1)

                def add_up():
                    pe.wait_ge(turned_copied, head + 1)
                    if head >= 1:
                        pe.wait_ge(state_done, head * (CHUNKS - 1))
                    for c in range(CHUNKS - 1):
                        rows = slice((c % 2) * CH, (c % 2 + 1) * CH)
                        mm = pe.matmul(update_at(c), kd_tok[rows, c // 2, :], v_tok[rows, c // 2, HV + head * HG_V:HV + (head + 1) * HG_V],
                                       start=True, stop=True)
                    mm.then_inc(update_ready, 1)

                for l in range(NL + 1):
                    n = head * (NL + 1) + l
                    if n >= 2:
                        pe.wait_ge(pairs_taken, n - 1)
                    if l >= 1:
                        i = head * NL + l - 1
                        pe.wait_ge(k_done, i + 1)
                        pe.wait_ge(q_done, i + 1)
                        left, right = k_part[:, i % 2, :], q_part[:, i % 2, :]
                    else:
                        left, right = keys, q
                    for t in range(TILES3):
                        mm = pe.matmul(pair_acc[:, n % 2, t, :], left[:, t * P:(t + 1) * P], right[:, t * P:(t + 1) * P], start=True, stop=True)
                    mm.then_inc(pairs_ready, 1)
                    if l == 0 and head >= 1:
                        multiply(head - 1)
                    elif l == 3:
                        turn()
                    elif l == 5:
                        add_up()
            multiply(HG - 1)


def conv_norm(nc, k, qm, fm):
    tiles = CONV_TILES
    with stage(nc, "link", "summed", "centred", "squared", "var_ready", "root_done", "scaled", "done") as (sems, sbuf, psum, begin):
        dve_link, summed, centred, squared, var_ready, root_done, scaled, done = sems
        square = sbuf("square", [P, tiles, S])
        scale = sbuf("scale", [P, 2, S])
        acc = psum("acc", [P, 2, S])
        block = begin()
        conv = [fm[:, CB + t, 0:S] for t in range(tiles)]

        @block.scalar
        def _(act):
            for t in range(tiles):
                act.wait_ge(centred, t + 1)
                act.activation(square[:, t, :], conv[t], ACT.Square).then_inc(squared, 1)
            act.wait_ge(var_ready, 1)
            act.activation(scale[:, 1, :], scale[:, 0, :], ACT.Sqrt).then_inc(root_done, 1)
            for t in range(tiles):
                act.wait_ge(scaled, t + 1)
                act.activation(qm[:, CA + t, 0:S], conv[t], ACT.Silu, bias=k.one("dw_ln_b", t)).then_inc(done, 1)

        @block.vector
        def _(dve):
            chain = Chain(dve, dve_link)
            dve.wait_ge(summed, 1)
            for t in range(tiles):
                dve.scalar_tensor_tensor(conv[t], acc[:, 0, :], -1.0 / (tiles * P), conv[t], ALU.mult, ALU.add).then_inc(centred, 1)
            dve.wait_ge(summed, 2)
            dve.tensor_scalar(scale[:, 0, :], acc[:, 1, :], 1.0 / (tiles * P), EPS, ALU.mult, ALU.add).then_inc(var_ready, 1)
            dve.wait_ge(root_done, 1)
            chain.link(dve.reciprocal(scale[:, 0, :], scale[:, 1, :]))
            dve.wait_ge(centred, tiles)
            for t in range(tiles):
                dve.scalar_tensor_tensor(conv[t], conv[t], k.one("dw_ln_g", t), scale[:, 0, :], ALU.mult, ALU.mult).then_inc(scaled, 1)

        @block.tensor
        def _(pe):
            for t in range(tiles):
                last = pe.matmul(acc[:, 0, :], k.ones, conv[t], start=t == 0, stop=t == tiles - 1)
            last.then_inc(summed, 1)
            for t in range(tiles):
                pe.wait_ge(squared, t + 1)
                last = pe.matmul(acc[:, 1, :], k.ones, square[:, t, :], start=t == 0, stop=t == tiles - 1)
            last.then_inc(summed, 1)


def gate_heads(nc, qm, fm):
    with stage(nc, "silu_done", "gated") as ((silu_done, gated), sbuf, _, begin):
        silu = sbuf("silu", [P, HG, S])
        block = begin()

        @block.scalar
        def _(act):
            for head in range(HG):
                act.activation(silu[0:HG_V, head, :], fm[0:HG_V, HG_G + head, 0:S], ACT.Silu).then_inc(silu_done, 1)

        @block.vector
        def _(dve):
            for head in range(HG):
                dve.wait_ge(silu_done, head + 1)
                dve.tensor_tensor(qm[0:HG_V, HQ + head, :], qm[0:HG_V, HQ + head, :], silu[0:HG_V, head, :], ALU.mult).then_inc(gated, 1)


def third_block(nc, k, A, ws, b):
    n, w = 1, S
    x = tiles_of(b.x, n, w, META)
    norm, gate = k.at("norm_mix_3"), k.at("gate_b_3")
    with ExitStack() as ctx:
        halves = halves_of(nc, ctx, "h", KT, S)
        h = lambda t: halves.tile(t, S)
        rms_norm(nc, k, A, x, S, n, w, lambda t: k.vec[:, norm + t:norm + t + 1], halves=halves)
        qm = ctx.enter_context(nc.sbuf_tensor(f"qm_{nc.next_id()}", [P, QM3, S], F32))
        with ExitStack() as inner:
            third_branches(nc, k, A, ws, inner, h, qm)
        cuts = halves_of(nc, ctx, "y", QM3, S)
        rows_of = lambda t: HG_V if HQ <= t < CA else P
        cut_tiles(nc, [(qm[0:rows_of(t), t, :], *cuts.tile(t, S, rows_of(t))) for t in range(QM3)])
        merged = qm
        out = halves_of(nc, ctx, "merged", KT, S)
        branches = [(lambda t, at=at, rows=rows: cuts.tile(at + t, S, rows), ks, rows, gate + i * KT)
                    for i, (at, ks, rows) in enumerate([(FQ, 3, P), (HQ, HG, HG_V), (CA, 2, P)])]
        merge(nc, k, ws, h, branches, merged, n, w, out=out)
        project(nc, ws, KT, [(lambda t: out.tile(t, S), KT, P)], n, w, None,
                lambda dve, chain, i, acc, tmp: dve.tensor_tensor(tile_at(b.x, i, n, w, META), tile_at(b.x, i, n, w, META), acc(0), ALU.add),
                unroll=4)
    ffn = k.at("norm_ffn_3")
    with ExitStack() as ctx:
        halves = halves_of(nc, ctx, "h", KT, S)
        rms_norm(nc, k, A, x, S, n, w, lambda t: k.vec[:, ffn + t:ffn + t + 1], halves=halves)
        feed_forward(nc, k, ws, k.at("ffn_dw_w"), k.at("ffn_dw_b"), lambda t: halves.tile(t, S), b.x, META, n, w)


def third_branches(nc, k, A, ws, ctx, h, qm):
    n, w = 1, S

    def sbuf(name, shape):
        return ctx.enter_context(nc.sbuf_tensor(f"{name}_{nc.next_id()}", shape, F32))

    fm = sbuf("fm", [P, FM3, S])
    v_tok = sbuf("v_tok", [P, TILES3, TM3])
    small = sbuf("small", [P, 1])
    forgotten = sbuf("forgotten", [FOX, S])
    project(nc, ws, QM3, [(h, KT, P)], n, w, copies(qm, n, w), unroll=4)
    project(nc, ws, FM3, [(h, KT, P)], n, w, copies(fm, n, w), unroll=4)
    project_tokens(nc, ws, TM3 // (2 * P), h, S,
                   lambda act, t, rows, p, acc: act.activation(v_tok[0:rows, t, p * 2 * P:(p + 1) * 2 * P], acc, ACT.Copy))
    scale_columns(nc, small[:, 0:1], k.col("fox_q_norm"), Q_SCALE)
    queries, tiles = tiles_of(qm, n, w), tiles_of(fm, n, w)
    head_norms(nc, k, A, [(queries(FQ + i), small[:, 0:1]) for i in range(3)] + [(tiles(FK + i), k.col("fox_k_norm")) for i in range(3)],
               HD, n, w)
    with ExitStack() as inner:
        fox_rows = inner.enter_context(nc.sbuf_tensor(f"fox_rows_{nc.next_id()}", [FOX, FOX * P], F32))
        keys = inner.enter_context(nc.sbuf_tensor(f"fox_keys_{nc.next_id()}", [P, 2, FOX // 2, S], F32))
        forget_sums(nc, k, A, fm, fm[0:FOX, FF, 0:S], forgotten[:, :], fox_rows, keys)
        groups = []
        for head in range(FOX):
            rows = slice((head % 2) * HD, (head % 2) * HD + HD)
            for t in range(TILES3):
                cols, nk = slice(t * P, (t + 1) * P), (t + 1) * P
                groups.append(([Part(qm[:, FQ + head // 2, cols], keys[:, head % 2, head // 2, 0:nk], k.causal[:, OFF - t * P:TAB],
                                     [v_tok[:, j, FV + head * HD:FV + (head + 1) * HD] for j in range(t + 1)],
                                     extra=(fox_rows[:, head * P:(head + 1) * P], forgotten[:, 0:nk]))],
                               qm[rows, FQ + head // 2, cols]))
        attend(nc, k, groups, wide=False, longest=S)
    hgrn(nc, k, A, qm, fm, v_tok)
    head_norms(nc, k, A, [(qm[0:HG_V, HQ + head, :], k.col("hgrn_norm")[0:HG_V]) for head in range(HG)], HG_V, n, w, rows=HG_V)
    gate_heads(nc, qm, fm)
    conv_norm(nc, k, qm, fm)


def lay_out_third(v, A):
    w = v["w_in_3"][0]
    widths = [FOX * HD] * 3 + [FOX, 512, 512, HG * HG_V, HG * HG_V, 256, 256, 3 * D]
    at = np.concatenate([[0], np.cumsum(widths)])
    part = lambda i: w[:, at[i]:at[i + 1]]
    A["level_masks"] = level_masks()
    wb, gates = v["w_branch_3"][0], part(10)
    fox, hg = FOX * HD, HG * HG_V
    rows_of_head = np.zeros((HG, P, D), np.float32)
    rows_of_head[:, 0:HG_V] = wb[fox:fox + hg].reshape(HG, HG_V, D)
    branch = [wb[0:fox], rows_of_head.reshape(HG * P, D), wb[fox + hg:]]
    tiles = [tiled(part(0)), tiled(part(4)), tiled(part(8))]
    tiles += [tiled(part(1)), tiled(part(5)), tiled(part(7), HG_V), tiled(part(9)), tiled(part(3), FOX)]
    tiles += padded_tiles(np.concatenate([part(2), part(6)], axis=1), 2 * P)
    for i in range(3):
        tiles += in_turn(tiled(gates[:, i * D:(i + 1) * D]), tiled(branch[i]))
    tiles += [tiled(v["w_out_3"][0])]
    return tiles + ff_tiles(v["w_up_3"][0], v["w_down_3"][0])



class Consts:

    def __init__(self, vec, places):
        self.vec, self.places = vec, places

    def at(self, name):
        return self.places[name][0]

    def col(self, name):
        a, n = self.places[name]
        return self.vec[:, a:a + n]

    def one(self, name, i=0):
        a = self.places[name][0] + i
        return self.vec[:, a:a + 1]


class Buffers:
    def __init__(self, x):
        self.x = x


def build(nc, A, out, vec_places, const_places, scratch):
    with ExitStack() as ctx:
        def sbuf(name, shape):
            return ctx.enter_context(nc.sbuf_tensor(name, shape, F32))

        vec = sbuf("vec", [P, A["vec"].shape[1]])
        const = sbuf("const", [P, A["const"].shape[1]])
        k = Consts(vec, vec_places)

        def c(name):
            a, n = const_places[name]
            return const[:, a:a + n]
        k.ones, k.ident, k.mirror, k.later = c("ones"), c("ident"), c("mirror"), c("later")
        k.half_select, k.select = c("half_select"), c("select")
        k.sees_cmp, k.causal = c("sees_cmp"), c("causal")
        k.ada = sbuf("ada", [P, 3 * KT])
        b = Buffers(sbuf("x", [P, KT, T2]))
        ws = WeightStream(nc, ctx, A["stream"])
        first_block(nc, k, A, ws, b, const)
        second_block(nc, k, A, ws, b, scratch)
        third_block(nc, k, A, ws, b)
        assert ws.next == ws.total, (ws.next, ws.total)
        stored = nc.alloc_semaphore("stored")
        block = ctx.enter_context(nc.Block())

        @block.sync
        def _(sp):
            sp.dma_start(out, b.x[:, :, META:T2]).then_inc(stored, 16)
            sp.wait_ge(stored, 16)



def columns(v):
    return np.asarray(v).reshape(-1, P).T


def padded(v):
    out = np.zeros((P, 1), np.float32)
    out[:np.size(v), 0] = np.asarray(v).reshape(-1)
    return out


def tiled(w, cols=P):
    w = np.asarray(w)
    kt, nt = w.shape[0] // P, w.shape[1] // cols
    out = w.reshape(kt, P, nt, cols).transpose(2, 1, 0, 3)
    if cols < P:
        out = np.concatenate([out, np.zeros(out.shape[:3] + (P - cols,), np.float32)], axis=3)
    return out


def doubled(w, cols, times):
    t = tiled(w, cols)[..., :cols]
    return np.concatenate([t] * times, axis=3)


def padded_tiles(w, multiple):
    n = -(-w.shape[1] // multiple) * multiple
    return [tiled(np.concatenate([w, np.zeros((w.shape[0], n - w.shape[1]), np.float32)], axis=1))]


def in_turn(*tiles):
    return [t[i:i + 1] for i in range(len(tiles[0])) for t in tiles]


def ff_tiles(up, down):
    down = tiled(down)
    return in_turn(tiled(up[:, :D_FF]), tiled(up[:, D_FF:])) + in_turn(*(down[:, :, k:k + KT] for k in range(0, FFT, KT)))


def stream_of(tiles):
    n = sum(len(t) for t in tiles)
    out = np.zeros((n, P, KT, P), np.float32)
    at = 0
    for t in tiles:
        out[at:at + len(t), :, :t.shape[2]] = t
        at += len(t)
    return out.reshape(n, P, KT * P)


def tokens_last(x):
    return np.asarray(x).T.reshape(KT, P, -1).transpose(1, 0, 2)


def shape_constants():
    p = np.arange(P)[:, None]
    rel = p - np.arange(TAB)[None, :] + OFF
    select = np.arange(48)[None, :] - 24
    return {
        "ones": np.ones((P, P)), "ident": np.eye(P), "mirror": np.eye(P)[::-1], 
        "half_select": select == p // HD, "select": (select[:, 16:32] == 0) & (p >= 0),
        "later": np.arange(P)[:, None] >= np.arange(P)[None, :],
        "sees_cmp": p >= 31, "causal": np.where(rel >= 0, 0.0, BIG),
    }


def stage_constants(A):
    p = np.arange(P)[:, None]
    rel = p - np.arange(TAB)[None, :] + OFF
    A["distance"] = np.where(rel >= 0, rel, FAR).astype(np.float32)
    t = p + P * np.arange(S // P)[None, :]
    d = t[:, :, None] - (16 * np.arange(N_CMP) + 31)[None, None, :]
    A["distance_cmp"] = np.where(d >= 0, d, FAR).reshape(P, -1).astype(np.float32)
    c = np.arange(2 * T2 - 272) - 256
    A["before"] = (np.arange(P)[:, None] < c[None, :]).astype(np.float32)
    A["rows_of_halves"] = np.repeat(np.eye(24, dtype=np.float32), HD, axis=1)
    A["rows_of_tiles"] = np.repeat(np.eye(8, dtype=np.float32), P, axis=1)
    A["resets"] = np.broadcast_to((np.arange(S) % CH != 0).astype(np.float32)[None, :], (P, S))
    A["fox_rows"] = np.repeat(-np.eye(FOX, dtype=np.float32), P, axis=1)


def buckets():
    rel = OFF + P - 1 - np.arange(TAB + P - 1)
    n = np.maximum(rel, 0)
    nf = np.maximum(n, 1).astype(np.float32)
    large = 16 + (np.log(nf / np.float32(16)) / np.float32(math.log(8)) * np.float32(16)).astype(np.int32)
    bucket = np.where(n < 16, n, np.minimum(large, 31))
    out = np.zeros((33, rel.size), np.float32)
    out[bucket, np.arange(rel.size)] = -1.0
    out[:, rel < 0] = 0.0
    out[32, rel < 0] = BIG
    return out


def level_masks():
    s, t = np.arange(P)[:, None], np.arange(P)[None, :]
    out = [s == t]
    for m in (1, 2, 4, 8, 16, 32):
        out.append((s // (2 * m) == t // (2 * m)) & (s % (2 * m) < m) & (t % (2 * m) >= m))
    return np.stack(out, axis=1).astype(np.uint32)


def pack(named):
    places, parts, at = {}, [], 0
    for name, a in named.items():
        a = np.asarray(a, np.float32).reshape(P, -1)
        places[name] = (at, a.shape[1])
        parts.append(a)
        at += a.shape[1]
    return np.ascontiguousarray(np.concatenate(parts, axis=1)), places


def lay_out(v):
    A = {}
    v = {name: np.asarray(a) for name, a in v.items()}
    A["x"], A["meta"] = tokens_last(v["x"][0]), tokens_last(v["meta_tokens_2"])
    twice = lambda a: np.concatenate([a.reshape(-1), a.reshape(-1)])
    A["vec"], vec_places = pack({
        "b_ada": columns(v["b_ada"]), "g_pre": columns(v["g_pre"]), "g_post": columns(v["g_post"]),
        "conv_w": columns(v["conv_w"]), "conv_b": columns(v["conv_b"]),
        "attn_norm": columns(v["attn_norm_2"]), "b_gate": columns(v["b_gate_2"]), "ffn_norm": columns(v["ffn_norm_2"]),
        "conv_w_2": columns(v["conv_w_2"]), "conv_b_2": columns(v["conv_b_2"]),
        "q_norm_sp": padded(twice(v["q_norm_sp_2"])), "k_norm_sp": padded(twice(v["k_norm_sp_2"])),
        "q_norm_df": padded(twice(v["q_norm_df_2"])), "k_norm_df": padded(twice(v["k_norm_df_2"])),
        "lam": np.concatenate([padded(v[n]) for n in ("lam_q1_2", "lam_q2_2", "lam_k1_2", "lam_k2_2")], axis=1),
        "subln_df": padded(v["subln_df_2"]),
        "norm_mix_3": columns(v["norm_mix_g_3"]), "gate_b_3": columns(v["gate_b_3"]), "norm_ffn_3": columns(v["norm_ffn_g_3"]),
        "fox_forget_b": padded(v["fox_forget_b_3"]), "fox_q_norm": padded(twice(v["fox_q_norm_g_3"])),
        "fox_k_norm": padded(twice(v["fox_k_norm_g_3"])), "hgrn_norm": padded(v["hgrn_out_norm_g_3"]),
        "dw_w": np.concatenate([columns(v["conv_dw_w_3"][0][i]) for i in range(CONV_W)], axis=1), "dw_b": columns(v["conv_dw_b_3"]),
        "dw_ln_g": columns(v["conv_norm_g_3"]), "dw_ln_b": columns(v["conv_norm_b_3"]),
        "ffn_dw_w": columns(v["ffn_dw_w_3"]), "ffn_dw_b": columns(v["ffn_dw_b_3"]),
    })
    A["const"], const_places = pack(shape_constants())

    w = v["w_in"][0]
    cols = lambda a, n: w[:, a:a + n]
    A["w_ada"], A["c_row"] = v["w_ada"][0].T.reshape(3 * KT, P, D), v["c"][0]
    stage_constants(A)
    B = 4 * MIX
    kv = lambda i: cols(B + MIX + i * 256, 256)
    z_at = B + MIX + 6 * 256
    C = z_at + MIX + 3 * NH
    G = C + 3 * MIX
    merge_tiles = lambda i: in_turn(tiled(cols(G + i * D, D)), tiled(v["w_br"][0, i]))
    tiles = [tiled(cols(B, MIX)), tiled(kv(0)), tiled(kv(1)), tiled(kv(2)), tiled(kv(4))]
    tiles += padded_tiles(np.concatenate([kv(3), kv(5), cols(z_at + MIX, 3 * NH)], axis=1), 2 * P)
    tiles += [tiled(cols(z_at, MIX))] + merge_tiles(1)
    tiles += in_turn(*[tiled(cols(i * MIX, MIX)) for i in range(4)]) + merge_tiles(0)
    tiles += [tiled(cols(C + MIX, MIX))] + in_turn(tiled(cols(C, MIX)), tiled(cols(C + 2 * MIX, MIX))) + merge_tiles(2)
    tiles += [tiled(v["w_out"][0])]
    A["w_cmp1"] = np.stack([v[n][0].reshape(16, P, P).transpose(1, 0, 2) for n in ("w_ck1", "w_cv1")], axis=1)
    A["pos_cmp"] = np.stack([v[n][0].reshape(16, P).T for n in ("pos_ck", "pos_cv")], axis=1)
    A["w_cmp2"] = np.stack([np.concatenate([v[n][0]] * 2, axis=1) for n in ("w_ck2", "w_cv2")], axis=1)
    A["w_s_t"], A["b_s"] = v["w_s"][0].transpose(2, 0, 1), v["b_s"]
    A["ln_g"], A["ln_b"] = v["ln_g"], v["ln_b"]
    A["stream"] = stream_of(tiles + lay_out_second(v, A) + lay_out_third(v, A))
    return {name: np.ascontiguousarray(a) for name, a in A.items()}, vec_places, const_places


def kernel(**inputs):
    import concourse.bacc as bacc
    from concourse.bass_utils import run_bass_kernel_spmd

    arrays, vec_places, const_places = lay_out(inputs)
    nc = bacc.Bacc("TRN2", target_bir_lowering=False, num_devices=1)
    A = {name: nc.dram_tensor(f"in_{name}", a.shape, mybir.dt.from_np(a.dtype), kind="ExternalInput").ap() for name, a in arrays.items()}
    out = nc.dram_tensor("out", (P, KT, S), F32, kind="ExternalOutput").ap()
    scratch = nc.dram_tensor("bias_rows", (8, TAB + P - 1), F32, kind="Internal").ap()
    build(nc, A, out, vec_places, const_places, scratch)
    r = run_bass_kernel_spmd(nc, [{f"in_{name}": a for name, a in arrays.items()}], core_ids=[0])
    return r.results[0]["out"].transpose(1, 0, 2).reshape(D, S).T.reshape(1, S, D)
```
